# Optimizing a Trainium2 kernel written in Bass

```python
import jax
import jax.numpy as jnp
from jax import lax
import numpy as np

D_MODEL = 1024
BATCH = 1
SEQ = 256
DEPTH = 2

GRID_W = 64
CTX_LEN = 256
HEAD_DIM = 64
MIX_WIDTH = D_MODEL
N_MIX_HEADS = MIX_WIDTH // HEAD_DIM
N_DIR = 2
RET_HEADS = N_MIX_HEADS // 4
RET_WIDTH = RET_HEADS * HEAD_DIM
RET_CHUNK = 128
GDN_HEADS = N_MIX_HEADS // 4
GDN_WIDTH = GDN_HEADS * HEAD_DIM
GDN_CHUNK = 64
GDN_CONV = 5
SWA_HEADS = N_MIX_HEADS - RET_HEADS - GDN_HEADS
SWA_KV_HEADS = SWA_HEADS // 4
SWA_GROUP = SWA_HEADS // SWA_KV_HEADS
SWA_WIDTH = SWA_HEADS * HEAD_DIM
SWA_KV_WIDTH = SWA_KV_HEADS * HEAD_DIM
WINDOW = 128
ATTN_BLOCK = 128
ROPE_BASE = 10000.0
RET_COLS = 4 * RET_WIDTH
GDN_COLS = 4 * GDN_WIDTH + 2 * N_DIR * GDN_HEADS
SWA_COLS = SWA_WIDTH + 2 * SWA_KV_WIDTH
IN_COLS = RET_COLS + GDN_COLS + SWA_COLS
DENSE_FF = 2816
N_EXPERTS = 8
TOP_K = 2
EXPERT_FF = 3584
MOE_BLOCK = 128
N_DENSE_LAYERS = (DEPTH + 1) // 2
N_MOE_LAYERS = DEPTH // 2
EPS = 1e-6

kernel_name = 'hybrid_retention_deltanet_swa_moe_dit'

def split_cols(p, sizes):
    idx = [int(s) for s in np.cumsum(sizes)[:-1]]
    return jnp.split(p, idx, axis=-1)

def rms_norm(x, gain):
    xf = x.astype(jnp.float32)
    y = xf * lax.rsqrt(jnp.mean(xf * xf, axis=-1, keepdims=True) + EPS)
    return (y * gain.astype(jnp.float32)).astype(x.dtype)

def modulate(h, shift, scale):
    return h * (1 + scale) + shift

def l2_normalize(t):
    return t * lax.rsqrt(jnp.sum(t * t, axis=-1, keepdims=True) + EPS)

def flip_dir(t, direction):
    return jnp.flip(t, axis=1) if direction == 1 else t

def axial_rope(n_tokens):
    rows = n_tokens // GRID_W
    row = jnp.repeat(jnp.arange(rows, dtype=jnp.float32), GRID_W)
    col = jnp.tile(jnp.arange(GRID_W, dtype=jnp.float32), rows)
    n_freq = HEAD_DIM // 4
    inv = ROPE_BASE ** (-jnp.arange(n_freq, dtype=jnp.float32) / n_freq)
    ang = jnp.concatenate([row[:, None] * inv, col[:, None] * inv], axis=-1)
    return jnp.cos(ang)[:, None, :], jnp.sin(ang)[:, None, :]

def apply_rope(t, cos, sin):
    half = t.shape[-1] // 2
    t1 = t[..., :half].astype(jnp.float32)
    t2 = t[..., half:].astype(jnp.float32)
    return jnp.concatenate([t1 * cos - t2 * sin, t2 * cos + t1 * sin], axis=-1).astype(t.dtype)

def depthwise_conv_centred(x, w):
    return lax.conv_general_dilated(x, w[:, None, :].astype(x.dtype), window_strides=(1,), padding='SAME',
                                    dimension_numbers=('NWC', 'WIO', 'NWC'), feature_group_count=x.shape[-1])

def retention_chunkwise(q, k, v, log_gamma, s0):
    b, t, h, dk = q.shape
    n = t // RET_CHUNK
    qc = q.reshape(b, n, RET_CHUNK, h, dk)
    kc = k.reshape(b, n, RET_CHUNK, h, dk)
    vc = v.reshape(b, n, RET_CHUNK, h, -1)
    pos = jnp.arange(RET_CHUNK, dtype=jnp.float32)
    diff = pos[:, None] - pos[None, :]
    intra_decay = jnp.exp(jnp.where(diff[None] >= 0, diff[None] * log_gamma[:, None, None], -jnp.inf))
    scores = jnp.einsum('bnihd,bnjhd->bnhij', qc, kc) * intra_decay
    o_intra = jnp.einsum('bnhij,bnjhe->bnihe', scores, vc)
    k_w = jnp.exp((RET_CHUNK - 1 - pos)[:, None] * log_gamma)
    chunk_kv = jnp.einsum('bnjhd,bnjhe->nbhde', kc * k_w[..., None], vc)
    chunk_decay = jnp.exp(RET_CHUNK * log_gamma)[:, None, None]

    def step(s, kv):
        return s * chunk_decay + kv, s

    s_final, s_prev = lax.scan(step, s0, chunk_kv)
    q_w = jnp.exp((pos + 1)[:, None] * log_gamma)
    o_inter = jnp.einsum('bnihd,nbhde->bnihe', qc * q_w[..., None], s_prev)
    return (o_intra + o_inter).reshape(b, t, h, -1), s_final

def gated_delta_chunkwise(q, k, v, g, beta, s0):
    b, t, h, dk = q.shape
    dv = v.shape[-1]
    n = t // GDN_CHUNK

    def blk(z):
        return z.reshape(b, n, GDN_CHUNK, h, -1).transpose(0, 1, 3, 2, 4)

    q, k, v = blk(q), blk(k), blk(v)
    g = g.reshape(b, n, GDN_CHUNK, h).transpose(0, 1, 3, 2)
    beta = beta.reshape(b, n, GDN_CHUNK, h).transpose(0, 1, 3, 2)
    gcs = jnp.cumsum(g, axis=-1)
    idx = jnp.arange(GDN_CHUNK)
    incl = idx[:, None] >= idx[None, :]
    strict = idx[:, None] > idx[None, :]
    decay = jnp.exp(jnp.where(incl, gcs[..., :, None] - gcs[..., None, :], -jnp.inf))
    kb = k * beta[..., None]
    a_mat = jnp.where(strict, jnp.einsum('bnhid,bnhjd->bnhij', kb, k) * decay, 0.0)
    rhs = jnp.concatenate([v * beta[..., None], kb * jnp.exp(gcs)[..., None]], axis=-1)
    sol = lax.linalg.triangular_solve(a_mat + jnp.eye(GDN_CHUNK, dtype=a_mat.dtype), rhs, left_side=True,
                                      lower=True, unit_diagonal=True)
    u, w = sol[..., :dv], sol[..., dv:]
    attn = jnp.einsum('bnhid,bnhjd->bnhij', q, k) * decay
    q_dec = q * jnp.exp(gcs)[..., None]
    k_dec = k * jnp.exp(gcs[..., -1:] - gcs)[..., None]
    blk_decay = jnp.exp(gcs[..., -1])
    xs = tuple(jnp.moveaxis(z, 1, 0) for z in (u, w, q_dec, k_dec, attn, blk_decay))

    def step(s, inp):
        u_n, w_n, qd_n, kd_n, at_n, dec_n = inp
        v_new = u_n - jnp.einsum('bhcd,bhde->bhce', w_n, s)
        o = jnp.einsum('bhcd,bhde->bhce', qd_n, s) + jnp.einsum('bhij,bhje->bhie', at_n, v_new)
        s = s * dec_n[..., None, None] + jnp.einsum('bhcd,bhce->bhde', kd_n, v_new)
        return s, o

    s_final, o = lax.scan(step, s0, xs)
    o = jnp.moveaxis(o, 0, 1).transpose(0, 1, 3, 2, 4).reshape(b, t, h, dv)
    return o, s_final

def retention_mixer(p_ctx, p_lat, log_neg_decay, gn_gain, cos, sin):
    def heads(p):
        b, t = p.shape[:2]
        q, k, v, g = split_cols(p.astype(jnp.float32), [RET_WIDTH] * 4)
        hd = lambda z: z.reshape(b, t, RET_HEADS, HEAD_DIM)
        return hd(q), hd(k) * HEAD_DIM ** -0.5, hd(v), g

    qc, kc, vc, gc = heads(p_ctx)
    ql, kl, vl, gl = heads(p_lat)
    ql, kl = apply_rope(ql, cos, sin), apply_rope(kl, cos, sin)
    log_gamma = -jnp.exp(log_neg_decay.astype(jnp.float32))
    b = p_lat.shape[0]
    s0 = jnp.zeros((b, RET_HEADS, HEAD_DIM, HEAD_DIM), jnp.float32)
    o_c = jnp.zeros_like(vc)
    o_l = jnp.zeros_like(vl)
    for d in range(N_DIR):
        oc, s_ctx = retention_chunkwise(flip_dir(qc, d), flip_dir(kc, d), flip_dir(vc, d), log_gamma[d], s0)
        ol, _ = retention_chunkwise(flip_dir(ql, d), flip_dir(kl, d), flip_dir(vl, d), log_gamma[d], s_ctx)
        o_c = o_c + flip_dir(oc, d)
        o_l = o_l + flip_dir(ol, d)

    def finish(o, g):
        mu = jnp.mean(o, axis=-1, keepdims=True)
        var = jnp.mean(jnp.square(o - mu), axis=-1, keepdims=True)
        y = ((o - mu) * lax.rsqrt(var + EPS)).reshape(o.shape[0], o.shape[1], RET_WIDTH)
        return y * gn_gain.astype(jnp.float32) * jax.nn.silu(g)

    return finish(o_c, gc), finish(o_l, gl)

def gated_deltanet_mixer(p_ctx, p_lat, conv_w, a_log, dt_bias, norm_gain):
    def prep(p):
        b, t = p.shape[:2]
        qkv, z, a, bt = split_cols(p.astype(jnp.float32),
                                   [3 * GDN_WIDTH, GDN_WIDTH, N_DIR * GDN_HEADS, N_DIR * GDN_HEADS])
        qkv = jax.nn.silu(depthwise_conv_centred(qkv, conv_w.astype(jnp.float32)))
        q, k, v = split_cols(qkv, [GDN_WIDTH] * 3)
        hd = lambda y: y.reshape(b, t, GDN_HEADS, HEAD_DIM)
        q = l2_normalize(hd(q)) * HEAD_DIM ** -0.5
        k = l2_normalize(hd(k))
        a = a.reshape(b, t, N_DIR, GDN_HEADS)
        bt = bt.reshape(b, t, N_DIR, GDN_HEADS)
        g = -jnp.exp(a_log.astype(jnp.float32)) * jax.nn.softplus(a + dt_bias.astype(jnp.float32))
        return q, k, hd(v), z, g, jax.nn.sigmoid(bt)

    qc, kc, vc, zc, gc, bc = prep(p_ctx)
    ql, kl, vl, zl, gl, bl = prep(p_lat)
    b = p_lat.shape[0]
    s0 = jnp.zeros((b, GDN_HEADS, HEAD_DIM, HEAD_DIM), jnp.float32)
    o_c = jnp.zeros_like(vc)
    o_l = jnp.zeros_like(vl)
    for d in range(N_DIR):
        oc, s_ctx = gated_delta_chunkwise(flip_dir(qc, d), flip_dir(kc, d), flip_dir(vc, d),
                                          flip_dir(gc[:, :, d], d), flip_dir(bc[:, :, d], d), s0)
        ol, _ = gated_delta_chunkwise(flip_dir(ql, d), flip_dir(kl, d), flip_dir(vl, d),
                                      flip_dir(gl[:, :, d], d), flip_dir(bl[:, :, d], d), s_ctx)
        o_c = o_c + flip_dir(oc, d)
        o_l = o_l + flip_dir(ol, d)

    def finish(o, z):
        o = o * lax.rsqrt(jnp.mean(o * o, axis=-1, keepdims=True) + EPS) * norm_gain.astype(jnp.float32)
        return o.reshape(o.shape[0], o.shape[1], GDN_WIDTH) * jax.nn.silu(z)

    return finish(o_c, zc), finish(o_l, zl)

def window_attention_mixer(p_ctx, p_lat, sink, cos, sin):
    b, n_lat = p_lat.shape[:2]
    n_ctx = p_ctx.shape[1]
    scale = HEAD_DIM ** -0.5

    def heads(p):
        t = p.shape[1]
        q, k, v = split_cols(p, [SWA_WIDTH, SWA_KV_WIDTH, SWA_KV_WIDTH])
        return (q.reshape(b, t, SWA_HEADS, HEAD_DIM), k.reshape(b, t, SWA_KV_HEADS, HEAD_DIM),
                v.reshape(b, t, SWA_KV_HEADS, HEAD_DIM))

    qc, kc, vc = heads(p_ctx)
    ql, kl, vl = heads(p_lat)
    ql = apply_rope(ql, cos, sin)
    kl = apply_rope(kl, cos, sin)
    qc = qc.reshape(b, n_ctx, SWA_KV_HEADS, SWA_GROUP, HEAD_DIM)
    ql = ql.reshape(b, n_lat, SWA_KV_HEADS, SWA_GROUP, HEAD_DIM)
    sink_g = sink.astype(jnp.float32).reshape(SWA_KV_HEADS, SWA_GROUP)
    s_cc = jnp.einsum('bqgrd,bkgd->bgrqk', qc, kc).astype(jnp.float32) * scale
    sink_c = jnp.broadcast_to(sink_g[None, :, :, None, None], s_cc.shape[:-1] + (1,))
    p_c = jax.nn.softmax(jnp.concatenate([s_cc, sink_c], axis=-1), axis=-1)[..., :n_ctx].astype(vc.dtype)
    o_c = jnp.einsum('bgrqk,bkgd->bqgrd', p_c, vc).reshape(b, n_ctx, SWA_WIDTH)
    nb = n_lat // ATTN_BLOCK
    qb = ql.reshape(b, nb, ATTN_BLOCK, SWA_KV_HEADS, SWA_GROUP, HEAD_DIM)

    def band(z):
        zp = jnp.pad(z, ((0, 0), (ATTN_BLOCK, ATTN_BLOCK), (0, 0), (0, 0)))
        zp = zp.reshape(b, nb + 2, ATTN_BLOCK, SWA_KV_HEADS, HEAD_DIM)
        return jnp.concatenate([zp[:, :nb], zp[:, 1:nb + 1], zp[:, 2:]], axis=2)

    kw, vw = band(kl), band(vl)
    s_loc = jnp.einsum('bnqgrd,bnkgd->bngrqk', qb, kw).astype(jnp.float32) * scale
    s_ctx = jnp.einsum('bnqgrd,bkgd->bngrqk', qb, kc).astype(jnp.float32) * scale
    q_pos = jnp.arange(nb)[:, None, None] * ATTN_BLOCK + jnp.arange(ATTN_BLOCK)[None, :, None]
    k_pos = (jnp.arange(nb)[:, None, None] - 1) * ATTN_BLOCK + jnp.arange(3 * ATTN_BLOCK)[None, None, :]
    valid = (jnp.abs(k_pos - q_pos) <= WINDOW) & (k_pos >= 0) & (k_pos < n_lat)
    s_loc = jnp.where(valid[None, :, None, None], s_loc, -jnp.inf)
    sink_l = jnp.broadcast_to(sink_g[None, None, :, :, None, None], s_loc.shape[:-1] + (1,))
    p_l = jax.nn.softmax(jnp.concatenate([s_loc, s_ctx, sink_l], axis=-1), axis=-1).astype(vl.dtype)
    n_band = 3 * ATTN_BLOCK
    o_l = (jnp.einsum('bngrqk,bnkgd->bnqgrd', p_l[..., :n_band], vw)
           + jnp.einsum('bngrqk,bkgd->bnqgrd', p_l[..., n_band:n_band + n_ctx], vc))
    return o_c, o_l.reshape(b, n_lat, SWA_WIDTH)

def token_mixers(p_ctx, p_lat, ret_decay, ret_gn_g, gdn_conv_w, gdn_a_log, gdn_dt_bias, gdn_norm_g, swa_sink,
                 cos, sin):
    pc = split_cols(p_ctx, [RET_COLS, GDN_COLS, SWA_COLS])
    pl = split_cols(p_lat, [RET_COLS, GDN_COLS, SWA_COLS])
    rc, rl = retention_mixer(pc[0], pl[0], ret_decay, ret_gn_g, cos, sin)
    dc, dl = gated_deltanet_mixer(pc[1], pl[1], gdn_conv_w, gdn_a_log, gdn_dt_bias, gdn_norm_g)
    wc, wl = window_attention_mixer(pc[2], pl[2], swa_sink, cos, sin)
    dt = p_lat.dtype
    o_ctx = jnp.concatenate([rc.astype(dt), dc.astype(dt), wc.astype(dt)], axis=-1)
    o_lat = jnp.concatenate([rl.astype(dt), dl.astype(dt), wl.astype(dt)], axis=-1)
    return o_ctx, o_lat

def swiglu(h, w1, w3, w2):
    return (jax.nn.silu(h @ w1) * (h @ w3)) @ w2

def moe_swiglu(h, router_w, w_gate, w_up, w_down):
    n_tok, d = h.shape
    logits = (h @ router_w).astype(jnp.float32)
    top_logit, top_idx = lax.top_k(logits, TOP_K)
    gate = jax.nn.softmax(top_logit, axis=-1)
    n_assign = n_tok * TOP_K
    expert_flat = top_idx.reshape(n_assign)
    order = jnp.argsort(expert_flat)
    expert_sorted = expert_flat[order]
    token_sorted = (order // TOP_K).astype(jnp.int32)
    gate_sorted = gate.reshape(n_assign)[order]
    counts = jnp.bincount(expert_flat, length=N_EXPERTS)
    group_start = jnp.cumsum(counts) - counts
    padded = (counts + MOE_BLOCK - 1) // MOE_BLOCK * MOE_BLOCK
    padded_end = jnp.cumsum(padded)
    padded_start = padded_end - padded
    dest = padded_start[expert_sorted] + jnp.arange(n_assign) - group_start[expert_sorted]
    n_blocks = -(-n_assign // MOE_BLOCK) + N_EXPERTS
    n_rows = n_blocks * MOE_BLOCK
    row_token = jnp.zeros((n_rows,), jnp.int32).at[dest].set(token_sorted)
    row_gate = jnp.zeros((n_rows,), jnp.float32).at[dest].set(gate_sorted)
    block_start = jnp.arange(n_blocks) * MOE_BLOCK
    block_expert = jnp.minimum(jnp.searchsorted(padded_end, block_start, side='right'), N_EXPERTS - 1)

    def expert_block(args):
        tok, e = args
        xb = h[tok]
        hid = jax.nn.silu(xb @ w_gate[e]) * (xb @ w_up[e])
        return hid @ w_down[e]

    y = lax.map(expert_block, (row_token.reshape(n_blocks, MOE_BLOCK), block_expert))
    y = y.reshape(n_rows, d) * row_gate[:, None].astype(h.dtype)
    return jnp.zeros_like(h).at[row_token].add(y)

def setup_inputs(seed: int = 0) -> dict:
    key = jax.random.key(seed)
    ks = jax.random.split(key, 32)
    f32 = jnp.float32
    d = D_MODEL

    def nrm(k, shape, scale):
        return jax.random.normal(k, shape, f32) * scale

    ret_base = np.log(-np.log(1.0 - 2.0 ** (-5.0 - np.arange(RET_HEADS))))
    dt = jnp.exp(jax.random.uniform(ks[12], (DEPTH, N_DIR, GDN_HEADS), f32, np.log(1e-3), np.log(1e-1)))
    return {
        'x': nrm(ks[0], (BATCH, SEQ, d), 1.0),
        'c': nrm(ks[1], (BATCH, d), 1.0),
        'ctx': nrm(ks[2], (BATCH, CTX_LEN, d), 1.0),
        'c_ctx': nrm(ks[3], (d,), 1.0),
        'ada_w': nrm(ks[4], (DEPTH, d, 6 * d), 0.5 * d ** -0.5),
        'ada_b': nrm(ks[5], (DEPTH, 6 * d), 0.02),
        'norm1_g': 1.0 + nrm(ks[6], (DEPTH, d), 0.05),
        'w_in': nrm(ks[7], (DEPTH, d, IN_COLS), d ** -0.5),
        'ret_decay': jnp.asarray(ret_base, f32) + nrm(ks[8], (DEPTH, N_DIR, RET_HEADS), 0.05),
        'ret_gn_g': 1.0 + nrm(ks[9], (DEPTH, RET_WIDTH), 0.05),
        'gdn_conv_w': nrm(ks[10], (DEPTH, GDN_CONV, 3 * GDN_WIDTH), GDN_CONV ** -0.5),
        'gdn_a_log': jnp.log(jax.random.uniform(ks[11], (DEPTH, N_DIR, GDN_HEADS), f32, 1.0, 16.0)),
        'gdn_dt_bias': dt + jnp.log(-jnp.expm1(-dt)),
        'gdn_norm_g': 1.0 + nrm(ks[13], (DEPTH, HEAD_DIM), 0.05),
        'swa_sink': nrm(ks[14], (DEPTH, SWA_HEADS), 0.5),
        'w_out': nrm(ks[15], (DEPTH, MIX_WIDTH, d), MIX_WIDTH ** -0.5),
        'norm2_g': 1.0 + nrm(ks[16], (DEPTH, d), 0.05),
        'ffn_w1': nrm(ks[17], (N_DENSE_LAYERS, d, DENSE_FF), d ** -0.5),
        'ffn_w3': nrm(ks[18], (N_DENSE_LAYERS, d, DENSE_FF), d ** -0.5),
        'ffn_w2': nrm(ks[19], (N_DENSE_LAYERS, DENSE_FF, d), DENSE_FF ** -0.5),
        'router_w': nrm(ks[20], (N_MOE_LAYERS, d, N_EXPERTS), d ** -0.5),
        'moe_w1': nrm(ks[21], (N_MOE_LAYERS, N_EXPERTS, d, EXPERT_FF), d ** -0.5),
        'moe_w3': nrm(ks[22], (N_MOE_LAYERS, N_EXPERTS, d, EXPERT_FF), d ** -0.5),
        'moe_w2': nrm(ks[23], (N_MOE_LAYERS, N_EXPERTS, EXPERT_FF, d), EXPERT_FF ** -0.5),
        'final_g': 1.0 + nrm(ks[24], (d,), 0.05),
    }

def reference(x, c, ctx, c_ctx, ada_w, ada_b, norm1_g, w_in, ret_decay, ret_gn_g, gdn_conv_w, gdn_a_log,
              gdn_dt_bias, gdn_norm_g, swa_sink, w_out, norm2_g, ffn_w1, ffn_w3, ffn_w2, router_w, moe_w1, moe_w3,
              moe_w2, final_g):
    b, n_lat, d = x.shape
    n_ctx = ctx.shape[1]
    cos, sin = axial_rope(n_lat)
    silu_c = jax.nn.silu(c)
    silu_cc = jax.nn.silu(c_ctx)
    for layer in range(DEPTH):
        last = layer == DEPTH - 1
        mx = jnp.split((silu_c @ ada_w[layer] + ada_b[layer])[:, None, :], 6, axis=-1)
        mc = jnp.split(silu_cc @ ada_w[layer] + ada_b[layer], 6, axis=-1)
        hx = modulate(rms_norm(x, norm1_g[layer]), mx[0], mx[1])
        hc = modulate(rms_norm(ctx, norm1_g[layer]), mc[0], mc[1])
        oc, ox = token_mixers(hc @ w_in[layer], hx @ w_in[layer], ret_decay[layer], ret_gn_g[layer],
                              gdn_conv_w[layer], gdn_a_log[layer], gdn_dt_bias[layer], gdn_norm_g[layer],
                              swa_sink[layer], cos, sin)
        x = x + mx[2] * (ox @ w_out[layer])
        tokens = modulate(rms_norm(x, norm2_g[layer]), mx[3], mx[4]).reshape(-1, d)
        if not last:
            ctx = ctx + mc[2] * (oc @ w_out[layer])
            hc2 = modulate(rms_norm(ctx, norm2_g[layer]), mc[3], mc[4])
            tokens = jnp.concatenate([hc2.reshape(-1, d), tokens], axis=0)
        i = layer // 2
        if layer % 2 == 0:
            y = swiglu(tokens, ffn_w1[i], ffn_w3[i], ffn_w2[i])
        else:
            y = moe_swiglu(tokens, router_w[i], moe_w1[i], moe_w3[i], moe_w2[i])
        x = x + mx[5] * y[tokens.shape[0] - b * n_lat:].reshape(b, n_lat, d)
        if not last:
            ctx = ctx + mc[5] * y[:b * n_ctx].reshape(b, n_ctx, d)
    return rms_norm(x, final_g)


_drawn_inputs = setup_inputs


def setup_inputs(seed=0):
    import zlib

    import numpy as np

    out = dict(_drawn_inputs(seed))
    spreads = {}
    factors = {'ret_gn_g': 5.641, 'gdn_norm_g': 6.627, 'swa_sink': 21.459}
    for name, (base, spread) in spreads.items():
        noise = np.random.default_rng([zlib.crc32(name.encode()), seed]).standard_normal(out[name].shape)
        drawn = base * np.exp(spread * noise) if base else spread * noise
        out[name] = jnp.asarray(drawn.astype(out[name].dtype))
    for name, factor in factors.items():
        out[name] = (out[name] * factor).astype(out[name].dtype)
    return out
```

```python
from contextlib import ExitStack

import numpy as np

import concourse.bass as bass
from concourse import mybir

F32 = mybir.dt.float32
I32 = mybir.dt.int32
ALU = mybir.AluOpType
ACT = mybir.ActivationFunctionType
AX_X = mybir.AxisListType.X

P = 128
D = 1024
DT = D // P
CTX = 256
LAT = 256
TOK = CTX + LAT
TT = TOK // P
HD = 64
SCALE = HD ** -0.5
EPS = 1e-6
CHUNK = 64
IN_COLS = 2832
FF = 2816
EXPERTS = 8
EFF = 3584
EC = EFF // 512
ITEMS = EXPERTS + 3
NEG = -1e30
SLOT = 4096
NSLOT = 7
LEVELS = (1, 2, 4, 8, 16, 32)

CONST = {}
_at = 0
for _name, _n in (("ident", P), ("ones", P), ("head_mean", P), ("incl0", P), ("incl1", P), ("half0", P),
                  ("half1", P), ("neg0", P), ("neg1", P), ("before", P), ("iota", P), ("same", P),
                  ("level0", 6 * P), ("level1", 6 * P), ("diff", 512), ("diff_pos", 512), ("diag2", 512),
                  ("band", 512), ("cos", LAT), ("sin", LAT), ("eps", 1), ("expert", 8)):
    CONST[_name] = (_at, _n)
    _at += _n
NCONST = _at

FF_PARTS = ((0, 12), (12, 22))


def steps(d):
    return [(t, c) for t in (0, 1, 2, 3) for c in (0, 1)] if d == 0 else \
        [(t, c) for t in (1, 0, 3, 2) for c in (1, 0)]


V_ADAB, V_N1, V_N2, V_CONV, V_RETG, V_FIN, V_GDNG, V_C, V_CC, NVEC = 0, 48, 56, 64, 94, 96, 104, 105, 113, 121


def const_table():
    t = np.zeros((P, NCONST), np.float32)

    def put(name, a):
        o, n = CONST[name]
        t[:, o:o + n] = np.asarray(a, np.float32).reshape(P, n)

    r = np.arange(P)
    row, col = r[:, None], r[None, :]
    same = row // CHUNK == col // CHUNK
    put("ident", np.eye(P))
    put("ones", np.ones((P, P)))
    put("head_mean", (row // HD == col // HD) / HD)
    put("incl0", same & (row <= col))
    put("incl1", same & (row >= col))
    put("half0", np.broadcast_to(row < CHUNK, (P, P)))
    put("half1", np.broadcast_to(row >= CHUNK, (P, P)))
    put("same", same)
    put("neg0", np.where(same & (col >= row), 0.0, NEG))
    put("neg1", np.where(same & (col <= row), 0.0, NEG))
    put("before", row < col)
    put("iota", np.broadcast_to(col, (P, P)))
    lv = [(col // b == row // b + 1) & ((col // b) % 2 == 1) for b in LEVELS]
    put("level0", np.stack(lv, 1))
    put("level1", np.stack([m.T for m in lv], 1))
    j = np.arange(256).reshape(2, P).T[:, :, None]
    i = np.arange(256)[None, None, :]
    put("diff", i - j)
    put("diff_pos", np.maximum(i - j, 0))
    put("diag2", 1.0 + (i == j))
    put("band", np.where(np.abs(i - j) <= 128, 0.0, NEG))
    n = np.arange(LAT, dtype=np.float32)
    inv = np.float32(10000.0) ** (-np.arange(16, dtype=np.float32) / np.float32(16))
    f = r % 32
    ang = np.where(f[:, None] < 16, (n // 64)[None, :], (n % 64)[None, :]).astype(np.float32) * inv[f % 16][:, None]
    put("cos", np.cos(ang))
    put("sin", np.sin(ang) * np.where(r % 64 < 32, -1.0, 1.0)[:, None])
    put("eps", np.full((P, 1), EPS))
    put("expert", np.broadcast_to(np.arange(8), (P, 8)))
    return t


class Ledger:

    def __init__(self, nc, ctx, known):
        self.nc, self.ctx, self.known = nc, ctx, known
        self.sems, self.count, self.at = {}, {}, {}

    def sem(self, name):
        if name not in self.sems:
            self.sems[name] = self.ctx.enter_context(self.nc.semaphore(name))
        return self.sems[name]

    def mark(self, name, key, n=1):
        self.count[name] = self.count.get(name, 0) + n
        assert (name, key) not in self.at, (name, key)
        self.at[name, key] = self.count[name]
        return self.sem(name), n

    def when(self, name, key):
        if self.known is None:
            return self.sem(name), 1
        return self.sem(name), self.known.at[name, key]

    def note(self, name, key, value):
        assert (name, key) not in self.at, (name, key)
        self.at[name, key] = value

    def noted(self, name, key, default):
        return self.at.get((name, key), default) if self.known is None else self.known.at[name, key]


def build(nc, A, out, ctab, known):
    ctx = ExitStack()
    with ctx:
        L = Ledger(nc, ctx, known)
        mark, when = L.mark, L.when

        def sb(name, n, dt=F32):
            return ctx.enter_context(nc.sbuf_tensor(name, [P, n], dt))

        ring = sb("ring", NSLOT * SLOT)
        xT = sb("xT", DT * TOK)[:, :].rearrange("p (k n) -> p k n", k=DT)
        hbuf = sb("hT", DT * TOK)
        hT = hbuf[:, :].rearrange("p (k n) -> p k n", k=DT)
        oT = hT
        table = sb("table", NCONST)
        work = sb("work", 6192)
        gates = sb("gates", 2048)
        tmpA, tmpB = sb("tmpA", 512), sb("tmpB", 512)
        vecT = sb("vecT", 2 * P)
        mods = sb("mods", 96)
        scl = sb("scl", 32)
        csil = sb("csil", 16)
        rows = sb("rows", 64)
        small = sb("small", 720)
        ints = sb("ints", 4, I32)
        psum = [ctx.enter_context(nc.psum_tensor(f"bank{i}", [P, 512], F32)) for i in range(8)]

        def const(name, i=None):
            o, n = CONST[name]
            return table[:, o:o + n] if i is None else table[:, o + i * P:o + (i + 1) * P]

        ident = const("ident")
        eps = const("eps")

        def slot(s):
            return ring[:, s * SLOT:(s + 1) * SLOT]

        arena = ring[:, 2 * SLOT:7 * SLOT]

        def carve(base, sizes):
            got = []
            for n in sizes:
                got.append(base[:, carve.at:carve.at + n])
                carve.at += n
            return got

        carve.at = SLOT
        rqk, rv, sq, skd, sv, decay, smask, sc, pr, pT, oraw, taps = carve(
            arena, (2048, 1024, 2048, 1024, 512, 2048, 3072, 1024, 1024, 1024, 512, 1024))
        rqk = rqk.rearrange("p (c n) -> p c n", c=4)
        rv = rv.rearrange("p (t n) -> p t n", t=TT)
        sq = sq.rearrange("p (c n) -> p c n", c=4)
        skd = skd.rearrange("p (c n) -> p c n", c=2)
        sv = sv.rearrange("p (t n) -> p t n", t=TT)
        assert carve.at <= 5 * SLOT
        carve.at = 0
        gT, gTT, gAT, gP1, gNT, gAtt, gWU, gKQ, gKD, gRW, gRU, gKB = carve(
            arena, (2048,) * 8 + (1024,) * 4)
        assert carve.at == 5 * SLOT

        def grp(buf, t, n=512):
            return buf[:, t * n:(t + 1) * n]

        def kbuf(t):
            return grp(gKB, t % 2)

        def smk(h, part):
            return grp(smask, 3 * (h % 2) + part)

        def dec(h):
            return grp(decay, h % 2, 1024)

        cin = work[:, 0:3120].rearrange("p (c s n) -> p c s n", c=6, s=2)
        tok = work[:, 0:3072].rearrange("p (t n) -> p t n", t=TT)
        acc = work[:, 3120:6192].rearrange("p (c s n) -> p c s n", c=6, s=2)
        acc2 = work[:, 3120:6192].rearrange("p (c n) -> p c n", c=6)
        qkT = work[:, 3120:3120 + 2048].rearrange("p (c n) -> p c n", c=4)
        rgate = gates[:, 0:1024].rearrange("p (c n) -> p c n", c=2)
        zgate = gates[:, 1024:2048].rearrange("p (c n) -> p c n", c=2)

        vrows = gates[:, 0:2 * P]
        xin = hbuf[:, :]

        def hidT(f):
            return work[:, f * 512:(f + 1) * 512]

        hrow = work[:, 0:2048].rearrange("p (t n) -> p t n", t=2)
        osb = work[:, 0:2048]
        yrow = work[:, 2048:3072]
        yacc = work[:, 3072:5120].rearrange("p (k n) -> p k n", k=DT)
        pick, wpick, spread = (work[:, a:a + 256] for a in (5120, 5376, 5632))
        hid, mhT = gates[:, 0:1024], gates[:, 1024:2048]
        hg = hT[:, :, 0:P]

        sm_at = [0]

        def sml(n):
            sm_at[0] += n
            return small[:, sm_at[0] - n:sm_at[0]]

        ab = sml(64)
        spz, spe, spl = sml(32), sml(32), sml(32)
        gl = sml(32)
        beta = sml(32)
        gex = sml(128)
        gcs = sml(32)
        kdf = sml(32)
        bgf = sml(32)
        sdec = sml(32)
        ssq = sml(32)
        mx, nmx, rsm, es, den = (sml(4) for _ in range(5))
        lgt, lsum, l256, ln1, ealog = sml(8), sml(4), sml(8), sml(4), sml(8)
        router = sb("router", 64)[:, :].rearrange("p (k e) -> p k e", k=DT)
        rt = small[:, 0:352]
        rt_at = [0]

        def rts(n):
            rt_at[0] += n
            return rt[:, rt_at[0] - n:rt_at[0]]
        lgts = rts(16).rearrange("p (t e) -> p t e", t=2)
        sel = rts(16).rearrange("p (t e) -> p t e", t=2)
        wexp = rts(16).rearrange("p (t e) -> p t e", t=2)
        less, cmp1, cmp2 = (rts(64).rearrange("p (e f) -> p e f", e=8) for _ in range(3))
        rank, over, nm1, wsum, place, intf = rts(8), rts(8), rts(2), rts(2), rts(24), rts(4)
        itemf = small[:, 352:424]
        items = itemf[:, :].rearrange("p (i u t) -> p i u t", i=3, u=12)
        poolone = sb("poolone", 1)
        krot = oraw
        state = tmpB[:, 0:256].rearrange("p (c n) -> p c n", c=2)
        vnew = tmpA[:, 0:256]

        VEC = [vecT[:, l * P:(l + 1) * P] for l in range(2)]
        modv = mods[:, :].rearrange("p (m v) -> p m v", v=2)
        sclv = scl[:, :].rearrange("p (n m v) -> p n m v", n=2, v=2)

        loads = []
        where = {}

        def load(key, s, pieces):
            loads.append((key, s, pieces))
            where[key] = s

        def wtile(ap, c0, n):
            return ap[:, c0:c0 + n].rearrange("(k p) n -> p k n", p=P)

        def kslot(s, n=512):
            return slot(s)[:, 0:DT * n].rearrange("p (k n) -> p k n", k=DT)

        for l in range(2):
            for n in range(12):
                load(("ada", l, n), n % NSLOT, [(kslot(n % NSLOT), wtile(A["ada_w"][l], n * 512, 512))])
            W = A["w_in"][l]
            for n, (name, c0) in enumerate((("gqk", 1024), ("gvz", 1536), ("kvab", None), ("sq", 2064),
                                            ("rqk", 0), ("rvg", 512))):
                v = kslot(n % 3)
                if name == "kvab":
                    pieces = [(v[:, :, 0:256], wtile(W, 2576, 256)), (v[:, :, 256:272], wtile(W, 2048, 16))]
                else:
                    pieces = [(v, wtile(W, c0, 512))]
                load((name, l), n % 3, pieces)
            for n in range(2):
                load(("wo", l, n), n, [(kslot(n), wtile(A["w_out"][l], n * 512, 512))])
            if l == 0:
                s = 2
                for f0, f1 in FF_PARTS:
                    for f in range(f0, f1, 2):
                        v = kslot(s)
                        load(("up", f), s, [(v[:, :, 0:256], wtile(A["ffn_w1"][0], f * P, 256)),
                                            (v[:, :, 256:512], wtile(A["ffn_w3"][0], f * P, 256))])
                        s = (s + 1) % NSLOT
                    for f in range(f0, f1, 4):
                        m = min(4, f1 - f)
                        v = slot(s)[:, 0:m * D].rearrange("p (q n) -> p q n", q=m)
                        load(("down", f), s, [(v, A["ffn_w2"][0][f * P:(f + m) * P, :].rearrange(
                            "(q p) n -> p q n", p=P))])
                        s = (s + 1) % NSLOT

        phase_done = ctx.enter_context(nc.semaphore("phase_done"))
        AFTER_PHASE = {("up", 0): 2}
        moe_gate_done = ctx.enter_context(nc.semaphore("moe_gate_done"))
        moe_up_done = ctx.enter_context(nc.semaphore("moe_up_done"))
        moe_down_done = ctx.enter_context(nc.semaphore("moe_down_done"))
        moe_slot_full = [ctx.enter_context(nc.semaphore(f"moe_slot_full{s}")) for s in range(NSLOT)]
        (moe_sel_ready, moe_gathered, moe_rows_ready, moe_spread, moe_spread_ready, moe_silu_ready,
         moe_hid_ready, moe_turned, moe_hidT_ready, moe_y_ready, moe_scattered, moe_added, ints_ready,
         out_stored, moe_picks, moe_y_half) = [ctx.enter_context(nc.semaphore(n)) for n in (
             "moe_sel_ready", "moe_gathered", "moe_rows_ready", "moe_spread", "moe_spread_ready",
             "moe_silu_ready", "moe_hid_ready", "moe_turned", "moe_hidT_ready", "moe_y_ready",
             "moe_scattered", "moe_added", "ints_ready", "out_stored", "moe_picks", "moe_y_half")]
        PRODUCT_DONE = {"w1": moe_gate_done, "w3": moe_up_done, "w2": moe_down_done}
        STREAM = [("w1", 0), ("w3", 0)]
        for c in range(EC):
            STREAM += [("w1", c + 1), ("w3", c + 1)] if c + 1 < EC else []
            STREAM += [("w2", c)]
        assert len(STREAM) == 3 * NSLOT
        MOE_SLOT = {k: (n + 2) % NSLOT for n, k in enumerate(STREAM)}
        MOE_USE = {k: n // NSLOT for n, k in enumerate(STREAM)}

        block = ctx.enter_context(nc.Block())

        uses = [0] * 8
        was_read = set()

        def open_bank(pe, key, b):
            if uses[b]:
                pe.wait_ge(L.sem(f"bank_read{b}"), uses[b])
            uses[b] += 1
            L.note("bank", key, b)
            L.note("turn", key, uses[b])
            return psum[b]

        def filled(key):
            return mark(f"bank_full{L.at['bank', key]}", key)

        def bank(key):
            return psum[L.noted("bank", key, 0)]

        def full(key):
            return when(f"bank_full{L.noted('bank', key, 0)}", key)

        def read(key):
            assert key not in was_read, key
            was_read.add(key)
            return L.sem(f"bank_read{L.noted('bank', key, 0)}"), 1

        def drained(key):
            return L.sem(f"bank_read{L.noted('bank', key, 0)}"), L.noted("turn", key, 1)

        def weights(key):
            return when(f"slot_full{where[key]}", key)

        def fill_frees(key, product):
            L.note("released", key, (f"bank_full{L.at['bank', product]}", product))

        def stepper(eng, name):
            sem = L.sem(name)
            n = [0]

            def step(ins):
                n[0] += 1
                ins.then_inc(sem, 1)

            def settle():
                eng.wait_ge(sem, n[0])
            return step, settle

        @block.sync
        def _(sp):
            held = {}
            for key, s, pieces in loads:
                if s in held:
                    sp.wait_ge(*when(*L.noted("released", held[s], ("bank_full0", "-"))))
                if key in AFTER_PHASE:
                    sp.wait_ge(phase_done, 4 * AFTER_PHASE[key])
                for i, (dst, src) in enumerate(pieces):
                    sp.dma_start(dst, src).then_inc(
                        *mark(f"slot_full{s}", key if i == len(pieces) - 1 else (key, i), 16))
                held[s] = key
            sp.wait_ge(phase_done, 4 * 4)
            w1, w3, w2 = A["moe_w1"][0], A["moe_w3"][0], A["moe_w2"][0]

            def expert(item, e):
                w1e = w1[bass.ds(e, 1)].rearrange("o (k p) n -> p (o k) n", p=P)
                w3e = w3[bass.ds(e, 1)].rearrange("o (k p) n -> p (o k) n", p=P)
                w2e = w2[bass.ds(e, 1)].rearrange("o (k p) n -> p (o k) n", p=P)
                for n, (kind, c) in enumerate(STREAM):
                    s = MOE_SLOT[kind, c]
                    if n < NSLOT:
                        k0, c0 = STREAM[n + 2 * NSLOT]
                        sp.wait_ge(PRODUCT_DONE[k0], item * EC + (c0 + 1))
                    else:
                        k0, c0 = STREAM[n - NSLOT]
                        sp.wait_ge(PRODUCT_DONE[k0], item * EC + (EC + c0 + 1))
                    if kind == "w2":
                        dst = slot(s).rearrange("p (q n) -> p q n", q=4)
                        src = w2e[:, 4 * c:4 * c + 4, :]
                    else:
                        dst = kslot(s)
                        src = (w1e if kind == "w1" else w3e)[:, :, c * 512:(c + 1) * 512]
                    sp.dma_start(dst, src).then_inc(moe_slot_full[s], 16)

            with sp.Fori(0, EXPERTS) as e:
                expert(e, e)
            sp.wait_ge(ints_ready, 1)
            n_over = sp.value_load(ints[0:1, 0:1], min_val=0, max_val=3)
            with sp.Fori(0, ITEMS - EXPERTS) as o:
                with sp.If(o < n_over):
                    e = sp.value_load(ints[0:1, bass.ds(o + 1, 1)], min_val=0, max_val=EXPERTS - 1)
                    expert(o + EXPERTS, e)
            for t in range(2):
                sp.wait_ge(*when("out_row", t))
                sp.dma_start(out[0, t * P:(t + 1) * P, :], osb[:, t * D:(t + 1) * D]).then_inc(out_stored, 16)
            sp.wait_ge(out_stored, 32)

        @block.tensor
        def _(pe):
            rot = [0]

            def product(key, banks=range(8)):
                banks = list(banks)
                rot[0] += 1
                return open_bank(pe, key, banks[rot[0] % len(banks)])

            def mm(o, w, x, start=True, stop=True):
                return nc.tensor.matmul(o, w, x, start=start, stop=stop)

            def turn(o, x, n=P):
                return nc.tensor.transpose(o, x, ident[0:n, 0:n])

            pe.wait_ge(*when("table_in", 0))
            for l in range(2):
                pe.wait_ge(*when(f"vec_in{l}", l))
                o = product(("vec", l))
                turn(o[:, 0:NVEC], vrows[0:NVEC, l * P:(l + 1) * P], NVEC).then_inc(*filled(("vec", l)))
            pe.wait_ge(*when("x_in", 0))
            for k in range(DT):
                o = product(("x", k))
                for t in range(TT):
                    ins = turn(o[:, t * P:(t + 1) * P], xin[:, t * D + k * P:t * D + (k + 1) * P])
                ins.then_inc(*filled(("x", k)))

            def ada(l):
                pe.wait_ge(*when("cond", 0))
                key = ("ada", l)
                o = product(key)
                for n in range(12):
                    pe.wait_ge(*weights(("ada", l, n)))
                    w = kslot(where["ada", l, n])
                    for m in range(4):
                        at = (4 * n + m) * 2
                        for k in range(DT):
                            ins = mm(o[:, at:at + 2], w[:, k, m * P:(m + 1) * P], csil[:, k:16:8], k == 0, k == DT - 1)
                    if n < 11:
                        ins.then_inc(*mark("ada_slot_used", (l, n)))
                        L.note("released", ("ada", l, n), ("ada_slot_used", (l, n)))
                ins.then_inc(*filled(key))
                fill_frees(("ada", l, 11), key)

            def norm(n, lo=0):
                key = ("ss", n)
                o = product(key)
                for k in range(DT):
                    pe.wait_ge(*when("square", (n, k)))
                    ins = mm(o[:, lo:TOK], const("ones"), hT[:, k, lo:TOK], k == 0, k == DT - 1)
                ins.then_inc(*filled(key))

            def by_channel(key, w, c, x, lo=0):
                o = product(key)
                for k in range(DT):
                    ins = mm(o[:, lo:TOK], w[:, k, c * P:(c + 1) * P], x[:, k, lo:TOK], k == 0, k == DT - 1)
                ins.then_inc(*filled(key))

            def by_token(key, w, c0, n, t):
                o = product(key)
                for k in range(DT):
                    ins = mm(o[:, 0:n], hT[:, k, t * P:(t + 1) * P], w[:, k, c0:c0 + n], k == 0, k == DT - 1)
                ins.then_inc(*filled(key))

            def project(l):
                pe.wait_ge(*when("mod", (2 * l, DT - 1)))
                for name in ("gqk", "gvz", "kvab", "sq", "rqk", "rvg"):
                    pe.wait_ge(*weights((name, l)))
                    w = kslot(where[name, l])
                    if name == "gqk":
                        keys = [(("gc", l, c), c) for c in range(4)]
                    elif name == "gvz":
                        keys = [(("gc", l, 4), 0), (("gc", l, 5), 1), (("z", l, 0), 2), (("z", l, 1), 3)]
                    elif name == "kvab":
                        keys = [(("sk", l), 0)]
                    elif name == "rvg":
                        keys = [(("rg", l, 0), 2), (("rg", l, 1), 3)]
                    else:
                        keys = [((name, l, c), c) for c in range(4)]
                    for key, c in keys:
                        by_channel(key, w, c, hT)
                    if name == "kvab":
                        for t in range(TT):
                            key = ("vab", l, t)
                            by_token(key, w, P, 144, t)
                    if name == "rvg":
                        for t in range(TT):
                            key = ("rv", l, t)
                            by_token(key, w, 0, 256, t)
                    fill_frees((name, l), key)

            def window(l):
                q0 = 0 if l == 0 else 2
                units = [(h, t) for h in range(8) for t in range(q0, TT)]

                def score(h, t):
                    m, p = divmod(h, 2)
                    nk = CTX if t < 2 else TOK
                    if (h, t) == units[0]:
                        pe.wait_ge(*drained(("sk", l)))
                        for c in range(4):
                            pe.wait_ge(*when("sq_ready", (l, c)))
                        pe.wait_ge(*when("sk_ready", l))
                    o = product(("sc", l, h, t), range(6))
                    mm(o[:, 0:nk], sq[p * HD:p * HD + HD, m, t * P:(t + 1) * P], skd[p * HD:p * HD + HD, m // 2, 0:nk]
                       ).then_inc(*filled(("sc", l, h, t)))

                def turn_probs(h, t):
                    pe.wait_ge(*when("probs", (l, h, t)))
                    o = product(("pt", l, h, t), range(6))
                    i = units.index((h, t))
                    for k in range(2 if t < 2 else 4):
                        ins = turn(o[:, k * P:(k + 1) * P], pr[:, (i % 2) * 512 + k * P:(i % 2) * 512 + (k + 1) * P])
                    ins.then_inc(*filled(("pt", l, h, t)))

                def values(h, t):
                    m, p = divmod(h, 2)
                    i = units.index((h, t))
                    key = ("so", l, m)
                    if p == 0 and t == q0:
                        open_bank(pe, key, 6 + m % 2)
                    o = psum[6 + m % 2]
                    pe.wait_ge(*drained(("pt", l, h, t)))
                    nk = 2 if t < 2 else 4
                    for k in range(nk):
                        ins = mm(o[p * HD:p * HD + HD, t * P:(t + 1) * P], sv[:, k, (h // 4) * HD:(h // 4) * HD + HD],
                                 pT[:, (i % 2) * 512 + k * P:(i % 2) * 512 + (k + 1) * P], k == 0, k == nk - 1)
                    if (p, t) == (1, TT - 1):
                        ins.then_inc(*filled(key))

                for i in range(len(units) + 3):
                    if i < len(units):
                        score(*units[i])
                    if 0 <= i - 2 < len(units):
                        turn_probs(*units[i - 2])
                    if 0 <= i - 3 < len(units):
                        values(*units[i - 3])

            def retention(l):
                for c in range(4):
                    pe.wait_ge(*when("rqk_ready", (l, c)))
                for t in range(TT):
                    pe.wait_ge(*drained(("rv", l, t)))

                def scores(h):
                    i, p = divmod(h, 2)
                    hp = slice(p * HD, p * HD + HD)
                    for part in range(3):
                        key = ("rs", l, h, part)
                        o = product(key, range(6))
                        qs = slice(0, CTX) if part == 2 else slice(CTX, TOK)
                        for j in range(2):
                            kt = j if part != 1 else 2 + j
                            ins = mm(o[:, j * 256:(j + 1) * 256], rqk[hp, 2 + i, kt * P:(kt + 1) * P], rqk[hp, i, qs])
                        ins.then_inc(*filled(key))

                def values(h):
                    i, p = divmod(h, 2)
                    key = ("ro", l, i)
                    if p == 0:
                        open_bank(pe, key, 6 + i)
                    o = psum[6 + i]
                    for part in range(3):
                        pe.wait_ge(*drained(("rs", l, h, part)))
                    hp = slice(p * HD, p * HD + HD)
                    hv = slice(h * HD, h * HD + HD)
                    for j in range(2):
                        mm(o[hp, 0:CTX], rv[:, j, hv], smk(h, 2)[:, j * 256:(j + 1) * 256], j == 0, j == 1)
                    for j in range(4):
                        ins = mm(o[hp, CTX:TOK], rv[:, j, hv], smk(h, j // 2)[:, (j % 2) * 256:(j % 2 + 1) * 256],
                                 j == 0, j == 3)
                    if p == 1:
                        ins.then_inc(*filled(key))
                    else:
                        ins.then_inc(*mark("ret_values", (l, h)))

                for h in range(4 + 1):
                    if h < 4:
                        scores(h)
                    if h >= 1:
                        values(h - 1)
                for i in range(2):
                    pe.wait_ge(*drained(("ro", l, i)))
                    mm(product(("rmean", l, i))[:, :], const("head_mean"), oraw)\
                        .then_inc(*filled(("rmean", l, i)))
                    pe.wait_ge(*when("head_square", ("r", l, i)))
                    mm(product(("rvar", l, i))[:, :], const("head_mean"), tmpB[:, :])\
                        .then_inc(*filled(("rvar", l, i)))

            def delta_prepare(l):
                for c in range(6):
                    pe.wait_ge(*when("conv_silu", (l, c)))
                for t in range(TT):
                    for part, cs in enumerate((range(4), range(4, 6))):
                        key = ("ct", l, t, part)
                        o = product(key)
                        for j, c in enumerate(cs):
                            ins = turn(o[:, j * P:(j + 1) * P], acc2[:, c, t * P:(t + 1) * P])
                        ins.then_inc(*filled(key))
                for t in range(TT):
                    key = ("qkt", l, t)
                    pe.wait_ge(*when("qk_unit", (l, t)))
                    o = product(key)
                    for j in range(4):
                        ins = turn(o[:, j * P:(j + 1) * P], tok[:, t, j * P:(j + 1) * P])
                    ins.then_inc(*filled(key))
                pe.wait_ge(*when("log_decay", l))
                key = ("gsum", l)
                o = product(key)
                for d in range(2):
                    mm(o[:, 16 * d:16 * d + 16], const(f"incl{d}"), gl[:, 16 * d:16 * d + 16])
                for j, name in enumerate(("same", "half0", "half1")):
                    ins = mm(o[:, 32 + 32 * j:64 + 32 * j], const(name), gl)
                ins.then_inc(*filled(key))

            def delta(l, d):
                R6 = range(6)
                for t in range(TT):
                    key = ("kq", l, d, t)
                    pe.wait_ge(*when("kbqd", (l, d, t)))
                    o = product(key, R6)
                    for j in range(4):
                        ins = turn(o[:, j * P:(j + 1) * P], kbuf(t)[:, j * P:(j + 1) * P])
                    ins.then_inc(*filled(key))
                    key = ("dec", l, d, t)
                    o = product(key, R6)
                    for h in range(4):
                        at = 16 * d + 4 * t + h
                        ins = mm(o[:, h * P:(h + 1) * P], gl[:, at:at + 1].to_broadcast([P, P]), const(f"incl{d}"))
                    ins.then_inc(*filled(key))
                for t in range(TT):
                    pe.wait_ge(*drained(("kq", l, d, t)))
                    for p in range(2):
                        key = ("kkqk", l, d, t, p)
                        o = product(key, R6)
                        hp = slice(p * HD, p * HD + HD)
                        ts = slice(t * P, (t + 1) * P)
                        for i in range(2):
                            mm(o[:, i * P:(i + 1) * P], qkT[hp, 2 + i, ts], grp(gKQ, t)[hp, i * P:(i + 1) * P])
                            ins = mm(o[:, (2 + i) * P:(3 + i) * P], qkT[hp, 2 + i, ts], qkT[hp, i, ts])
                        ins.then_inc(*filled(key))
                for t in range(TT):
                    key = ("T0", l, d, t)
                    pe.wait_ge(*when("TT_first", (l, d, t)))
                    o = product(key, R6)
                    for h in range(4):
                        ins = turn(o[:, h * P:(h + 1) * P], grp(gTT, t)[:, h * P:(h + 1) * P])
                    ins.then_inc(*filled(key))

                def by_head(key, a, b, t):
                    o = product(key, R6)
                    for h in range(4):
                        hs = slice(h * P, (h + 1) * P)
                        ins = mm(o[:, hs], grp(a, t)[:, hs], grp(b, t)[:, hs])
                    ins.then_inc(*filled(key))

                for v in range(1, 6):
                    for t in range(TT):
                        pe.wait_ge(*when("NT", (l, d, v, t)))
                        if v == 1:
                            pe.wait_ge(*drained(("T0", l, d, t)))
                        else:
                            pe.wait_ge(*drained(("TP", l, d, v - 1, t)))
                        by_head(("P1", l, d, v, t), gNT, gT, t)
                    for t in range(TT):
                        pe.wait_ge(*drained(("P1", l, d, v, t)))
                        if v > 1:
                            pe.wait_ge(*drained(("TTP", l, d, v - 1, t)))
                        if v < 5:
                            by_head(("TP", l, d, v, t), gTT, gP1, t)
                        by_head(("TTP", l, d, v, t), gP1, gTT, t)
                for t in range(TT):
                    key = ("wu", l, d, t)
                    pe.wait_ge(*drained(("TTP", l, d, 5, t)))
                    o = product(key, R6)
                    for h in range(4):
                        i, p = divmod(h, 2)
                        th = grp(gTT, t)[:, h * P:(h + 1) * P]
                        hs = slice(h * HD, h * HD + HD)
                        mm(o[p * HD:p * HD + HD, i * P:(i + 1) * P], grp(gRW, t, 256)[:, hs], th)
                        ins = mm(o[:, 256 + h * HD:256 + h * HD + HD], th, grp(gRU, t, 256)[:, hs])
                    ins.then_inc(*filled(key))
                pe.wait_ge(*when("state_zero", (l, d)))
                for n, (t, c) in enumerate(steps(d)):
                    cs = slice(c * CHUNK, c * CHUNK + CHUNK)
                    key = ("vn", l, d, n)
                    pe.wait_ge(*drained(("wu", l, d, t)))
                    if n:
                        pe.wait_ge(*drained(("su", l, d, n - 1)))
                    o = product(key, R6)
                    for i in range(2):
                        ins = mm(o[cs, i * P:(i + 1) * P], grp(gWU, t)[:, i * P + c * CHUNK:i * P + (c + 1) * CHUNK],
                                 state[:, i, :])
                    ins.then_inc(*filled(key))
                    pe.wait_ge(*when("kd", (l, d, t)))
                    go = ("go", l, d, t)
                    if n % 2 == 0:
                        open_bank(pe, go, 6 + (n // 2) % 2)
                    og = psum[6 + (n // 2) % 2]
                    pe.wait_ge(*drained(("vn", l, d, n)))
                    for i in range(2):
                        cols = slice(i * P + c * CHUNK, i * P + (c + 1) * CHUNK)
                        mm(og[:, cols], state[:, i, :],
                           grp(gKQ, t)[:, (2 + i) * P + c * CHUNK:(2 + i) * P + (c + 1) * CHUNK], True, False)
                        for p in range(2):
                            h = 2 * i + p
                            ins = mm(og[p * HD:p * HD + HD, cols], vnew[:, h * HD:h * HD + HD],
                                     grp(gAtt, t)[:, h * P + c * CHUNK:h * P + (c + 1) * CHUNK], False, True)
                    if n % 2 == 1:
                        ins.then_inc(*filled(go))
                    key = ("su", l, d, n)
                    o = product(key, R6)
                    for h in range(4):
                        i, p = divmod(h, 2)
                        hs = slice(h * HD, h * HD + HD)
                        ins = mm(o[p * HD:p * HD + HD, i * HD:(i + 1) * HD], grp(gKD, t, 256)[cs, hs], vnew[cs, hs])
                    ins.then_inc(*filled(key))

            def delta_finish(l):
                for i in range(2):
                    pe.wait_ge(*when("head_square", ("g", l, i)))
                    mm(product(("gvar", l, i))[:, :], const("head_mean"), tmpB[:, :])\
                        .then_inc(*filled(("gvar", l, i)))

            def out_project(l, lo):
                pe.wait_ge(*when("mixed", l))
                for m in range(4):
                    pe.wait_ge(*drained(("so", l, m)))
                for n in range(2):
                    pe.wait_ge(*weights(("wo", l, n)))
                    for c in range(4):
                        by_channel(("wo", l, 4 * n + c), kslot(where["wo", l, n]), c, oT, lo)
                    fill_frees(("wo", l, n), ("wo", l, 4 * n + 3))

            def ffn():
                pe.wait_ge(*when("mod", (1, DT - 1)))
                for half, (f0, f1) in enumerate(FF_PARTS):
                    for f in range(f0, f1):
                        w = kslot(where["up", f - f % 2])
                        pe.wait_ge(*weights(("up", f - f % 2)))
                        by_channel(("fa", f), w, f % 2, hT)
                        by_channel(("fb", f), w, 2 + f % 2, hT)
                        if f % 2:
                            fill_frees(("up", f - 1), ("fb", f))
                    for d in range(DT):
                        open_bank(pe, ("fy", half, d), d)
                    for f in range(f0, f1, 4):
                        m = min(4, f1 - f)
                        pe.wait_ge(*weights(("down", f)))
                        for q in range(m):
                            pe.wait_ge(*drained(("fb", f + q)))
                        last = f + m == f1
                        w = slot(where["down", f])[:, 0:m * D].rearrange("p (q n) -> p q n", q=m)
                        for d in range(DT):
                            for q in range(m):
                                ins = mm(psum[d][:, :], w[:, q, d * P:(d + 1) * P], hidT(f + q - f0),
                                         f == f0 and q == 0, last and q == m - 1)
                            if last:
                                ins.then_inc(*filled(("fy", half, d)))
                        if last:
                            fill_frees(("down", f), ("fy", half, DT - 1))
                        else:
                            ins.then_inc(*mark("down_slot_used", f))
                            L.note("released", ("down", f), ("down_slot_used", f))

            def phase_end(k, last):
                pe.wait_ge(*full_here(last))
                pe.sem_inc(phase_done, 1)
                pe.wait_ge(phase_done, 4 * k)

            def full_here(key):
                return L.sem(f"bank_full{L.at['bank', key]}"), L.at[f"bank_full{L.at['bank', key]}", key]

            for l in range(2):
                ada(l)
                norm(2 * l)
                project(l)
                window(l)
                retention(l)
                delta_prepare(l)
                phase_end(2 * l + 1, ("gsum", l))
                delta(l, 0)
                delta(l, 1)
                delta_finish(l)
                phase_end(2 * l + 2, ("gvar", l, 1))
                if l == 1:
                    pe.sem_inc(moe_gate_done, EC)
                    pe.sem_inc(moe_up_done, EC)
                    pe.sem_inc(moe_down_done, EC - 2)
                out_project(l, 0 if l == 0 else CTX)
                norm(2 * l + 1, 0 if l == 0 else CTX)
                if l == 0:
                    ffn()
            pe.wait_ge(*full_here(("wo", 1, 7)))
            pe.sem_inc(moe_down_done, 2)
            pe.wait_ge(*when("mod", (3, DT - 1)))
            pe.wait_ge(*when("router_in", 0))
            key = "logits"
            o = product(key)
            for t in range(2):
                for k in range(DT):
                    ins = mm(o[:, t * 8:t * 8 + 8], hT[:, k, CTX + t * P:CTX + (t + 1) * P], router[:, k, :],
                             k == 0, k == DT - 1)
            ins.then_inc(*filled(key))
            for t in range(2):
                for q in range(2):
                    key = ("row", t, q)
                    o = product(key)
                    for j in range(4):
                        ins = turn(o[:, j * P:(j + 1) * P], hT[:, 4 * q + j, CTX + t * P:CTX + (t + 1) * P])
                    ins.then_inc(*filled(key))
            pe.wait_ge(*when("chosen", 0))
            key = "places"
            o = product(key)
            mm(o[:, 0:8], const("before"), sel[:, 0, :])
            mm(o[:, 8:16], const("ones"), sel[:, 0, :], True, False)
            mm(o[:, 8:16], const("before"), sel[:, 1, :], False, True)
            mm(o[:, 16:24], const("ones"), sel[:, 0, :], True, False)
            mm(o[:, 16:24], const("ones"), sel[:, 1, :], False, True).then_inc(*filled(key))
            for b in range(8):
                pe.wait_ge(L.sem(f"bank_read{b}"), uses[b])
            for t in range(2):
                for q in range(2):
                    pe.wait_ge(*drained(("row", t, q)))

            def item(u):
                pe.wait_ge(moe_sel_ready, u + 1)
                pe.wait_ge(moe_added, u * 4 + 1)
                for q in range(2):
                    for j in range(4):
                        for t in range(2):
                            ins = mm(psum[4 + q][:, j * P:(j + 1) * P], hrow[:, t, (4 * q + j) * P:(4 * q + j + 1) * P],
                                     pick[:, t * P:(t + 1) * P], t == 0, t == 1)
                    ins.then_inc(moe_gathered, 1)
                pe.wait_ge(moe_rows_ready, u * 2 + 1)
                for t in range(2):
                    ins = turn(psum[4][:, t * P:(t + 1) * P], wpick[:, t * P:(t + 1) * P])
                ins.then_inc(moe_spread, 1)
                pe.wait_ge(moe_rows_ready, u * 2 + 2)

                def up(c, kind, b, read_sem, done):
                    s = MOE_SLOT[kind, c]
                    pe.wait_ge(moe_slot_full[s], u * 48 + (MOE_USE[kind, c] + 1) * 16)
                    pe.wait_ge(read_sem, u * EC + max(c, 1))
                    for k in range(DT):
                        ins = mm(psum[b][:, :], hg[:, k, 0:P], kslot(s)[:, k, :], k == 0, k == DT - 1)
                    ins.then_inc(done, 1)

                def gate_up(c):
                    up(c, "w1", c % 2, moe_silu_ready, moe_gate_done)

                def lin_up(c):
                    up(c, "w3", 2 + c % 2, moe_hid_ready, moe_up_done)

                def turn_hidden(c):
                    pe.wait_ge(moe_hid_ready, u * EC + (c + 2))
                    pe.wait_ge(moe_hidT_ready, u * EC + (c + 1))
                    if c == 0:
                        pe.wait_ge(moe_spread_ready, u + 1)
                    for q in range(4):
                        ins = turn(psum[4][:, q * P:(q + 1) * P], hid[:, (c % 2) * 512 + q * P:(c % 2) * 512 + (q + 1) * P])
                    ins.then_inc(moe_turned, 1)

                def down(c):
                    s = MOE_SLOT["w2", c]
                    pe.wait_ge(moe_slot_full[s], u * 48 + (MOE_USE["w2", c] + 1) * 16)
                    pe.wait_ge(moe_hidT_ready, u * EC + (c + 2))
                    if c == 0:
                        pe.wait_ge(moe_y_ready, u + 1)
                    w = slot(s).rearrange("p (q n) -> p q n", q=4)
                    for q in range(4):
                        for n in range(2):
                            ins = mm(psum[6 + n][:, :], mhT[:, (c % 2) * 512 + q * P:(c % 2) * 512 + (q + 1) * P],
                                     w[:, q, n * 512:(n + 1) * 512], c == 0 and q == 0, c == EC - 1 and q == 3)
                    ins.then_inc(moe_down_done, 1)

                gate_up(0)
                lin_up(0)
                for c in range(EC):
                    if c + 1 < EC:
                        gate_up(c + 1)
                    turn_hidden(c)
                    if c + 1 < EC:
                        lin_up(c + 1)
                    down(c)
                pe.wait_ge(moe_y_ready, u + 2)
                for j in range(4):
                    if j == 0:
                        pe.wait_ge(moe_hidT_ready, u * EC + EC + 1)
                    if j >= 2:
                        pe.wait_ge(moe_added, u * 4 + j)
                    for n in range(2):
                        k = 2 * j + n
                        ins = mm(psum[4 + j % 2][:, n * 256:(n + 1) * 256], yrow[:, k * P:(k + 1) * P], spread[:, :])
                    ins.then_inc(moe_scattered, 1)

            pe.sem_inc(moe_turned, 1)
            with pe.Fori(0, EXPERTS) as e:
                item(e)
            pe.wait_ge(ints_ready, 1)
            n_over = pe.value_load(ints[0:1, 0:1], min_val=0, max_val=3)
            with pe.Fori(0, ITEMS - EXPERTS) as o:
                with pe.If(o < n_over):
                    item(o + EXPERTS)

            norm(4, CTX)
            pe.wait_ge(*when("mod", (4, DT - 1)))
            for t in range(2):
                for q in range(2):
                    key = ("out", t, q)
                    o = product(key)
                    for j in range(4):
                        ins = turn(o[:, j * P:(j + 1) * P], hT[:, 4 * q + j, CTX + t * P:CTX + (t + 1) * P])
                    ins.then_inc(*filled(key))

        @block.scalar
        def _(act):
            step, settle = stepper(act, "act_step")

            def fn(o, i, f, **kw):
                return nc.scalar.activation(o, i, f, **kw)

            act.dma_start(table[:, :], ctab).then_inc(*mark("table_in", 0, 16))
            for t in range(2):
                act.dma_start(xin[:, t * D:(t + 1) * D], A["ctx"][0, t * P:(t + 1) * P, :])\
                    .then_inc(*mark("x_in", ("c", t), 16))
            for t in range(2):
                act.dma_start(xin[:, (2 + t) * D:(3 + t) * D], A["x"][0, t * P:(t + 1) * P, :])\
                    .then_inc(*mark("x_in", ("x", t) if t == 0 else 0, 16))
            for l in range(2):
                def vec(r, n, src, last=False):
                    act.dma_start(vrows[r:r + n, l * P:(l + 1) * P], src)\
                        .then_inc(*mark(f"vec_in{l}", l if last else (l, r), 16))

                def by_row(ap):
                    return ap.rearrange("(r p) -> r p", p=P)
                vec(V_ADAB, 48, by_row(A["ada_b"][l]))
                vec(V_N1, 8, by_row(A["norm1_g"][l]))
                vec(V_N2, 8, by_row(A["norm2_g"][l]))
                vec(V_CONV, 30, A["gdn_conv_w"][l].rearrange("a (c p) -> (a c) p", p=P))
                vec(V_RETG, 2, by_row(A["ret_gn_g"][l]))
                vec(V_FIN, 8, by_row(A["final_g"]))
                for p in range(2):
                    act.dma_start(vrows[V_GDNG:V_GDNG + 1, l * P + p * HD:l * P + (p + 1) * HD],
                                  A["gdn_norm_g"][l:l + 1, :]).then_inc(*mark(f"vec_in{l}", (l, "g", p), 16))
                vec(V_C, 8, by_row(A["c"][0]))
                vec(V_CC, 8, by_row(A["c_ctx"]), True)
                for i, src in enumerate((A["ret_decay"][l].rearrange("d h -> (d h)"),
                                         A["gdn_a_log"][l].rearrange("d h -> (d h)"),
                                         A["gdn_dt_bias"][l].rearrange("d h -> (d h)"), A["swa_sink"][l])):
                    act.dma_start(rows[:, 32 * l + 8 * i:32 * l + 8 * i + 8], src.partition_broadcast(P))\
                        .then_inc(*mark("rows_in", (l, i), 16))
            act.dma_start(router[:, :, :], A["router_w"][0].rearrange("(k p) e -> p k e", p=P))\
                .then_inc(*mark("router_in", 0, 16))
            act.wait_ge(*drained(("vec", 0)))
            fn(csil[:, :], VEC[0][:, V_C:V_C + 16], ACT.Silu).then_inc(*mark("cond", 0))
            for k in range(1, DT, 2):
                act.wait_ge(*full(("x", k)))
                fn(xT[:, k, :], bank(("x", k))[:, :], ACT.Copy).then_inc(*read(("x", k)))

            def norm(n, lo=0):
                l, w = divmod(n, 2)
                if n in (1, 3):
                    act.wait_ge(*drained(("wo", l, DT - 1)))
                if n == 2:
                    act.wait_ge(*drained(("fy", 1, DT - 1)))
                if n == 4:
                    act.wait_ge(*when("final_residual", DT - 1))
                for k in range(DT):
                    if n == 0:
                        act.wait_ge(*drained(("x", k)))
                        if k == 0:
                            act.wait_ge(*full(("x", DT - 1)))
                    fn(hT[:, k, lo:TOK], xT[:, k, lo:TOK], ACT.Square).then_inc(*mark("square", (n, k)))
                act.wait_ge(*full(("ss", n)))
                fn(tmpA[:, lo:TOK], bank(("ss", n))[:, lo:TOK], ACT.Sqrt, bias=eps, scale=1.0 / D)\
                    .then_inc(*read(("ss", n)))
                if n == 4:
                    return
                act.wait_ge(*when("scales", l))
                for k in range(DT):
                    act.wait_ge(*when("normed", (n, k)))
                    if lo == 0:
                        step(fn(hT[:, k, 0:CTX], hT[:, k, 0:CTX], ACT.Identity,
                                bias=modv[:, 24 * w + k, 1:2], scale=sclv[:, w, k, 1:2]))
                    fn(hT[:, k, CTX:TOK], hT[:, k, CTX:TOK], ACT.Identity, bias=modv[:, 24 * w + k, 0:1],
                       scale=sclv[:, w, k, 0:1]).then_inc(*mark("mod", (n, k)))

            def project(l):
                act.wait_ge(*when("pads", l))
                for c in range(6):
                    key = ("gc", l, c)
                    act.wait_ge(*full(key))
                    fn(cin[:, c, :, 2:258], bank(key)[:, :].rearrange("p (s n) -> p s n", s=2), ACT.Copy)\
                        .then_inc(*read(key))
                for i in range(2):
                    key = ("z", l, i)
                    act.wait_ge(*full(key))
                    fn(zgate[:, i, :], bank(key)[:, :], ACT.Silu).then_inc(*read(key))
                for i in range(2):
                    key = ("rg", l, i)
                    act.wait_ge(*full(key))
                    fn(rgate[:, i, :], bank(key)[:, :], ACT.Silu).then_inc(*read(key))
                act.wait_ge(*when("rows_in", (1, 3)))
                act.wait_ge(*when("gate_args", l))
                r = 32 * l
                step(fn(lgt, rows[:, r:r + 8], ACT.Exp))
                step(fn(ealog, rows[:, r + 8:r + 16], ACT.Exp))
                step(fn(spe, spz, ACT.Abs))
                settle()
                step(fn(spe, spe, ACT.Exp, scale=-1.0))
                for d in range(2):
                    step(fn(beta[:, 16 * d:16 * d + 16].rearrange("p (t h) -> p t h", t=TT),
                            ab.rearrange("p (t c) -> p t c", t=TT)[:, :, 8 + 4 * d:12 + 4 * d], ACT.Exp, scale=-1.0))
                settle()
                fn(spl, spe, ACT.Ln, bias=table[:, CONST["ones"][0]:CONST["ones"][0] + 1])\
                    .then_inc(*mark("gate_exps", l))

            def window(l):
                units = [(h, t) for h in range(8) for t in range(0 if l == 0 else 2, TT)]

                def turned(i):
                    h, t = units[i]
                    key = ("pt", l, h, t)
                    nk = CTX if t < 2 else TOK
                    act.wait_ge(*full(key))
                    fn(pT[:, (i % 2) * 512:(i % 2) * 512 + nk], bank(key)[:, 0:nk], ACT.Copy).then_inc(*read(key))

                def out_tile(m):
                    lo = 0 if l == 0 else CTX
                    key = ("so", l, m)
                    act.wait_ge(*full(key))
                    fn(oT[:, 4 + m, lo:TOK], bank(key)[:, lo:TOK], ACT.Copy).then_inc(*read(key))

                nu = len(units)
                per = nu // 4
                for i in range(nu + 4):
                    if i < nu:
                        h, t = units[i]
                        nk = CTX if t < 2 else TOK
                        j = i % 2
                        act.wait_ge(*when("scored", (l, i)))
                        if i >= 2:
                            act.wait_ge(*full(("pt", l) + units[i - 2]))
                        step(fn(pr[:, j * 512:j * 512 + nk], sc[:, j * 512:j * 512 + nk], ACT.Exp,
                                bias=nmx[:, i % 4:i % 4 + 1], accum_out=rsm[:, i % 4:i % 4 + 1]))
                        fn(es[:, i % 4:i % 4 + 1], rows[:, 32 * l + 24 + h:32 * l + 25 + h], ACT.Exp,
                           bias=nmx[:, i % 4:i % 4 + 1]).then_inc(*mark("exped", (l, i)))
                    if 0 <= i - 2 < nu:
                        turned(i - 2)
                    if i >= 4 and (i - 4) % per == per - 1:
                        out_tile((i - 4) // per)

            def retention(l):
                for h in range(4):
                    act.wait_ge(*when("decay_args", (l, h)))
                    m = dec(h)
                    step(fn(m[:, 512:1024], m[:, 512:1024], ACT.Exp))
                    step(fn(m[:, 0:512], const("diff"), ACT.Exp, scale=lgt[:, h:h + 1], bias=l256[:, h:h + 1]))
                    fn(tmpB[:, :], const("diff"), ACT.Exp, scale=ln1[:, h:h + 1], bias=l256[:, 4 + h:5 + h])\
                        .then_inc(*mark("decays_exp", (l, h)))
                for i in range(2):
                    key = ("ro", l, i)
                    act.wait_ge(*full(key))
                    if i:
                        act.wait_ge(*when("ret_out", (l, 0)))
                    fn(oraw, bank(key)[:, :], ACT.Copy).then_inc(*read(key))
                    act.wait_ge(*drained(("rmean", l, i)))
                    fn(tmpB[:, :], oraw, ACT.Square).then_inc(*mark("head_square", ("r", l, i)))
                    act.wait_ge(*full(("rvar", l, i)))
                    fn(tmpA[:, :], bank(("rvar", l, i))[:, :], ACT.Sqrt, bias=eps).then_inc(*read(("rvar", l, i)))

            def delta_prepare(l):
                for c in range(6):
                    act.wait_ge(*when("conv", (l, c)))
                    fn(acc2[:, c, :], acc2[:, c, :], ACT.Silu).then_inc(*mark("conv_silu", (l, c)))
                act.wait_ge(*when("ret_out", (l, 1)))
                for t in range(TT):
                    key = ("ct", l, t, 0)
                    act.wait_ge(*full(key))
                    if t >= 2:
                        act.wait_ge(*when("squares_summed", (l, t - 2)))
                    fn((tmpA, tmpB)[t % 2][:, :], bank(key)[:, :], ACT.Square).then_inc(*mark("qk_square", (l, t)))
                    fn(tok[:, t, 0:512], bank(key)[:, :], ACT.Copy).then_inc(*read(key))
                act.wait_ge(*when("squares_summed", (l, 3)))
                fn(ssq, ssq, ACT.Sqrt, bias=eps).then_inc(*mark("qk_root", l))
                for t in range(TT):
                    key = ("qkt", l, t)
                    act.wait_ge(*full(key))
                    fn(qkT[:, :, t * P:(t + 1) * P], bank(key)[:, :].rearrange("p (c n) -> p c n", c=4), ACT.Copy)\
                        .then_inc(*read(key))
                act.wait_ge(*when("gate_sums", l))
                step(fn(gex, gex, ACT.Exp))
                fn(kdf, kdf, ACT.Exp).then_inc(*mark("gate_sums_exp", l))

            def delta(l, d):
                def copy_out(key, dst):
                    act.wait_ge(*full(key))
                    fn(dst, bank(key)[:, :], ACT.Copy).then_inc(*read(key))

                for t in range(TT):
                    copy_out(("kq", l, d, t), grp(gKQ, t))
                for t in range(TT):
                    act.wait_ge(*when("decay_masked", (l, d, t)))
                    fn(grp(gP1, t), grp(gP1, t), ACT.Exp).then_inc(*mark("decay_ready", (l, d, t)))
                for t in range(TT):
                    copy_out(("T0", l, d, t), grp(gT, t))
                for v in range(1, 6):
                    for t in range(TT):
                        copy_out(("P1", l, d, v, t), grp(gP1, t))
                for t in range(TT):
                    copy_out(("wu", l, d, t), grp(gWU, t))

            def delta_finish(l):
                for i in range(2):
                    act.wait_ge(*when("delta_out", l))
                    if i:
                        act.wait_ge(*full(("gvar", l, 0)))
                    fn(tmpB[:, :], oT[:, 2 + i, :], ACT.Square).then_inc(*mark("head_square", ("g", l, i)))
                    act.wait_ge(*full(("gvar", l, i)))
                    if i:
                        act.wait_ge(*when("delta_normed", (l, 0)))
                    fn(tmpA[:, :], bank(("gvar", l, i))[:, :], ACT.Sqrt, bias=eps).then_inc(*read(("gvar", l, i)))

            def ffn():
                for f in range(22):
                    act.wait_ge(*full(("fa", f)))
                    if f >= 2:
                        act.wait_ge(*drained(("fb", f - 2)))
                    fn((tmpA, tmpB)[f % 2][:, :], bank(("fa", f))[:, :], ACT.Silu).then_inc(*read(("fa", f)))

            def phase_end(k):
                step(fn(csil[:, 0:1], csil[:, 0:1], ACT.Copy))
                settle()
                act.sem_inc(phase_done, 1)
                act.wait_ge(phase_done, 4 * k)

            for l in range(2):
                norm(2 * l)
                project(l)
                window(l)
                retention(l)
                delta_prepare(l)
                phase_end(2 * l + 1)
                delta(l, 0)
                delta(l, 1)
                delta_finish(l)
                phase_end(2 * l + 2)
                norm(2 * l + 1, 0 if l == 0 else CTX)
                if l == 0:
                    ffn()
            act.wait_ge(*when("route_max", 0))
            for t in range(2):
                step(fn(wexp[:, t, :], lgts[:, t, :], ACT.Exp, bias=nm1[:, t:t + 1]))
            settle()
            fn(csil[:, 0:1], csil[:, 0:1], ACT.Copy).then_inc(*mark("route_exp", 0))
            for t in range(2):
                for q in range(2):
                    key = ("row", t, q)
                    act.wait_ge(*full(key))
                    fn(hrow[:, t, q * 512:(q + 1) * 512], bank(key)[:, :], ACT.Copy).then_inc(*read(key))

            def item(u):
                for q in range(2):
                    act.wait_ge(moe_gathered, u * 2 + (q + 1))
                    fn(hg[:, 4 * q:4 * q + 4, :], psum[4 + q][:, :].rearrange("p (k n) -> p k n", k=4), ACT.Copy)\
                        .then_inc(moe_rows_ready, 1)
                act.wait_ge(moe_spread, u + 1)
                fn(spread, psum[4][:, 0:256], ACT.Copy).then_inc(moe_spread_ready, 1)

                def turned(c):
                    act.wait_ge(moe_turned, u * EC + (c + 2))
                    act.wait_ge(moe_down_done, u * EC + (EC if c < 2 else EC + c - 1))
                    fn(mhT[:, (c % 2) * 512:(c % 2) * 512 + 512], psum[4][:, :], ACT.Copy).then_inc(moe_hidT_ready, 1)

                for c in range(EC):
                    act.wait_ge(moe_gate_done, u * EC + (EC + c + 1))
                    act.wait_ge(moe_hid_ready, u * EC + max(c, 1))
                    fn((tmpA, tmpB)[c % 2][:, :], psum[c % 2][:, :], ACT.Silu).then_inc(moe_silu_ready, 1)
                    if c:
                        turned(c - 1)
                turned(EC - 1)

            act.sem_inc(moe_silu_ready, 1)
            act.sem_inc(moe_hidT_ready, 1)
            with act.Fori(0, EXPERTS) as e:
                item(e)
            act.wait_ge(ints_ready, 1)
            n_over = act.value_load(ints[0:1, 0:1], min_val=0, max_val=3)
            with act.Fori(0, ITEMS - EXPERTS) as o:
                with act.If(o < n_over):
                    item(o + EXPERTS)
            norm(4, CTX)
            for t in range(2):
                for q in range(2):
                    key = ("out", t, q)
                    act.wait_ge(*full(key))
                    fn(osb[:, t * D + q * 512:t * D + (q + 1) * 512], bank(key)[:, :], ACT.Copy)\
                        .then_inc(*read(key))
            for t in range(2):
                act.wait_ge(*drained(("out", t, 1)))
                act.sem_inc(*mark("out_row", t))

        @block.vector
        def _(dve):
            v = nc.vector
            step, settle = stepper(dve, "dve_step")

            def halves(lo):
                return ([(slice(0, CTX), 1)] if lo == 0 else []) + [(slice(CTX, TOK), 0)]

            dve.wait_ge(*when("table_in", 0))
            for l in range(2):
                dve.wait_ge(*full(("vec", l)))
                v.tensor_copy(VEC[l][:, 0:NVEC], bank(("vec", l))[:, 0:NVEC]).then_inc(*read(("vec", l)))
            for k in range(0, DT, 2):
                dve.wait_ge(*full(("x", k)))
                v.tensor_copy(xT[:, k, :], bank(("x", k))[:, :]).then_inc(*read(("x", k)))

            def ada(l):
                key = ("ada", l)
                dve.wait_ge(*full(key))
                dve.wait_ge(*drained(("vec", l)))
                if l:
                    for k in range(DT):
                        dve.wait_ge(*drained(("fy", 1, k)))
                v.tensor_tensor(modv, bank(key)[:, 0:96].rearrange("p (m v) -> p m v", v=2),
                                VEC[l][:, 0:48].unsqueeze(2).broadcast_to([P, 48, 2]), ALU.add).then_inc(*read(key))
                dve.wait_ge(*drained(key))
                for w, g in enumerate((V_N1, V_N2)):
                    ins = v.scalar_tensor_tensor(
                        out=sclv[:, w], in0=modv[:, 24 * w + 8:24 * w + 16, :], scalar=1.0,
                        in1=VEC[l][:, g:g + 8].unsqueeze(2).broadcast_to([P, 8, 2]), op0=ALU.add, op1=ALU.mult)
                    ins.then_inc(*mark("scales", l if w else (l, 0)))

            def norm(n, lo=0):
                dve.wait_ge(*drained(("ss", n)))
                step(v.reciprocal(tmpB[:, lo:TOK], tmpA[:, lo:TOK]))
                settle()
                for k in range(DT):
                    if n < 4:
                        v.tensor_tensor(hT[:, k, lo:TOK], xT[:, k, lo:TOK], tmpB[:, lo:TOK], ALU.mult)\
                            .then_inc(*mark("normed", (n, k)))
                    else:
                        v.scalar_tensor_tensor(
                            out=hT[:, k, lo:TOK], in0=xT[:, k, lo:TOK], scalar=VEC[0][:, V_FIN + k:V_FIN + k + 1],
                            in1=tmpB[:, lo:TOK], op0=ALU.mult, op1=ALU.mult).then_inc(*mark("mod", (n, k)))

            def rope(key, dst, name, mkey):
                dve.wait_ge(*full(key))
                b = bank(key)
                step(v.tensor_copy(dst[:, 0:CTX], b[:, 0:CTX]))
                step(v.tensor_tensor(tmpA[:, 0:LAT], b[:, CTX:TOK], const("cos"), ALU.mult))
                for q in range(4):
                    o = slice(32 * q, 32 * q + 32)
                    i = slice(32 * (q ^ 1), 32 * (q ^ 1) + 32)
                    ins = v.tensor_tensor(tmpB[o, 0:LAT], b[i, CTX:TOK], const("sin")[o, :], ALU.mult)
                    if q < 3:
                        step(ins)
                ins.then_inc(*read(key))
                dve.wait_ge(*drained(key))
                v.tensor_tensor(dst[:, CTX:TOK], tmpA[:, 0:LAT], tmpB[:, 0:LAT], ALU.add).then_inc(*mark(name, mkey))
                dve.wait_ge(*when(name, mkey))

            def project(l):
                rope(("sk", l), krot, "sk_rot", l)
                for g in range(2):
                    for p in range(2):
                        ins = v.tensor_copy(skd[p * HD:(p + 1) * HD, g, :], krot[g * HD:(g + 1) * HD, :])
                        if (g, p) != (1, 1):
                            step(ins)
                ins.then_inc(*mark("sk_ready", l))
                for t in range(TT):
                    key = ("vab", l, t)
                    dve.wait_ge(*full(key))
                    step(v.tensor_copy(sv[:, t, :], bank(key)[:, 0:P]))
                    v.tensor_copy(ab[:, 16 * t:16 * t + 16], bank(key)[:, P:P + 16]).then_inc(*read(key))
                dve.wait_ge(*when("rows_in", (1, 3)))
                dve.wait_ge(*drained(("vab", l, 3)))
                for d in range(2):
                    ins = (v.tensor_tensor(
                        spz[:, 16 * d:16 * d + 16].rearrange("p (t h) -> p t h", t=TT),
                        ab.rearrange("p (t c) -> p t c", t=TT)[:, :, 4 * d:4 * d + 4],
                        rows[:, 32 * l + 16 + 4 * d:32 * l + 20 + 4 * d].unsqueeze(1).broadcast_to([P, TT, 4]), ALU.add))
                    ins.then_inc(*mark("gate_args", l if d else (l, 0)))
                for c in range(4):
                    rope(("sq", l, c), sq[:, c, :], "sq_ready", (l, c))
                for c in range(4):
                    rope(("rqk", l, c), rqk[:, c, :], "rqk_ready", (l, c))
                for t in range(TT):
                    key = ("rv", l, t)
                    dve.wait_ge(*full(key))
                    v.tensor_copy(rv[:, t, :], bank(key)[:, 0:256]).then_inc(*read(key))
                dve.wait_ge(*when("gate_exps", l))
                step(v.scalar_tensor_tensor(out=gl, in0=spz, scalar=0.0, in1=spl, op0=ALU.max, op1=ALU.add))
                step(v.tensor_scalar(beta, beta, 1.0, None, ALU.add))
                step(v.tensor_scalar(lgt, lgt, -1.0, None, ALU.mult))
                settle()
                step(v.reciprocal(beta, beta))
                step(v.tensor_tensor(lsum, lgt[:, 0:4], lgt[:, 4:8], ALU.add))
                step(v.tensor_scalar(l256, lgt, 256.0, None, ALU.mult))
                step(v.tensor_scalar(ln1, lgt[:, 4:8], -1.0, None, ALU.mult))
                for d in range(2):
                    g = gl[:, 16 * d:16 * d + 16].rearrange("p (t h) -> p t h", t=TT)
                    ins = v.scalar_tensor_tensor(
                        out=g, in0=g, scalar=-1.0, in1=ealog[:, 4 * d:4 * d + 4].unsqueeze(1).broadcast_to([P, TT, 4]),
                        op0=ALU.mult, op1=ALU.mult)
                    ins.then_inc(*mark("log_decay", l if d else (l, 0)))
                settle()

            def window(l):
                units = [(h, t) for h in range(8) for t in range(0 if l == 0 else 2, TT)]

                def score(i):
                    h, t = units[i]
                    key = ("sc", l, h, t)
                    nk = CTX if t < 2 else TOK
                    c = slice(i % 4, i % 4 + 1)
                    o = sc[:, (i % 2) * 512:(i % 2) * 512 + nk]
                    dve.wait_ge(*full(key))
                    if i >= 2:
                        dve.wait_ge(*when("exped", (l, i - 2)))
                    ins = v.tensor_scalar(o[:, 0:CTX], bank(key)[:, 0:CTX], SCALE, None, ALU.mult)
                    if t >= 2:
                        step(ins)
                        ins = v.scalar_tensor_tensor(out=o[:, CTX:TOK], in0=bank(key)[:, CTX:TOK], scalar=SCALE,
                                                     in1=const("band")[:, (t - 2) * 256:(t - 1) * 256],
                                                     op0=ALU.mult, op1=ALU.add)
                    ins.then_inc(*read(key))
                    dve.wait_ge(*drained(key))
                    step(v.reduce_max(mx[:, c], o, AX_X))
                    settle()
                    v.tensor_scalar(nmx[:, c], mx[:, c], rows[:, 32 * l + 24 + h:32 * l + 25 + h], -1.0,
                                    ALU.max, ALU.mult).then_inc(*mark("scored", (l, i)))

                def normalize(i):
                    h, t = units[i]
                    nk = CTX if t < 2 else TOK
                    c = slice(i % 4, i % 4 + 1)
                    dve.wait_ge(*when("exped", (l, i)))
                    step(v.tensor_tensor(den[:, c], rsm[:, c], es[:, c], ALU.add))
                    settle()
                    step(v.reciprocal(den[:, c], den[:, c]))
                    settle()
                    o = pr[:, (i % 2) * 512:(i % 2) * 512 + nk]
                    v.tensor_scalar(o, o, den[:, c], None, ALU.mult).then_inc(*mark("probs", (l,) + units[i]))

                for i in range(len(units) + 1):
                    if i < len(units):
                        score(i)
                    if i:
                        normalize(i - 1)

            def retention(l):
                def args(h):
                    m = dec(h)
                    step(v.tensor_scalar(tmpA[:, :], const("diff"), ln1[:, h:h + 1], None, ALU.mult))
                    settle()
                    v.scalar_tensor_tensor(out=m[:, 512:1024], in0=const("diff_pos"), scalar=lsum[:, h:h + 1],
                                           in1=tmpA[:, :], op0=ALU.mult, op1=ALU.add)\
                        .then_inc(*mark("decay_args", (l, h)))
                args(0)
                for h in range(4):
                    m = dec(h)
                    dve.wait_ge(*when("decays_exp", (l, h)))
                    step(v.tensor_tensor(m[:, 512:1024], m[:, 512:1024], const("diag2"), ALU.mult))
                    step(v.tensor_tensor(m[:, 0:512], m[:, 0:512], tmpB[:, :], ALU.add))
                    settle()
                    if h < 3:
                        args(h + 1)
                    if h == 2:
                        dve.wait_ge(*when("ret_values", (l, 0)))
                    if h == 3:
                        dve.wait_ge(*full(("ro", l, 0)))
                    for part in range(3):
                        key = ("rs", l, h, part)
                        dve.wait_ge(*full(key))
                        v.scalar_tensor_tensor(out=smk(h, part), in0=bank(key)[:, :], scalar=SCALE,
                                               in1=m[:, 0:512] if part == 0 else m[:, 512:1024],
                                               op0=ALU.mult, op1=ALU.mult).then_inc(*read(key))
                    dve.wait_ge(*drained(("rs", l, h, 2)))
                for i in range(2):
                    dve.wait_ge(*drained(("ro", l, i)))
                    dve.wait_ge(*full(("rmean", l, i)))
                    v.tensor_tensor(oraw, oraw, bank(("rmean", l, i))[:, :], ALU.subtract)\
                        .then_inc(*read(("rmean", l, i)))
                    dve.wait_ge(*drained(("rvar", l, i)))
                    step(v.reciprocal(tmpA[:, :], tmpA[:, :]))
                    settle()
                    step(v.scalar_tensor_tensor(out=oraw, in0=oraw, scalar=VEC[l][:, V_RETG + i:V_RETG + i + 1],
                                                in1=tmpA[:, :], op0=ALU.mult, op1=ALU.mult))
                    settle()
                    dve.wait_ge(*drained(("rg", l, i)))
                    v.tensor_tensor(oT[:, i, :], oraw, rgate[:, i, :], ALU.mult).then_inc(*mark("ret_out", (l, i)))

            def delta_prepare(l):
                for t in range(TT):
                    key = ("ct", l, t, 1)
                    dve.wait_ge(*full(key))
                    v.tensor_copy(tok[:, t, 512:768], bank(key)[:, 0:256]).then_inc(*read(key))
                    dve.wait_ge(*when("qk_square", (l, t)))
                    v.reduce_sum(ssq[:, 8 * t:8 * t + 8],
                                 (tmpA, tmpB)[t % 2][:, :].rearrange("p (h n) -> p h n", n=HD), AX_X)\
                        .then_inc(*mark("squares_summed", (l, t)))
                dve.wait_ge(*when("qk_root", l))
                step(v.reciprocal(ssq, ssq))
                settle()
                qs = ssq.rearrange("p (t h) -> p t h", t=TT)[:, :, 0:4]
                step(v.tensor_scalar(qs, qs, SCALE, None, ALU.mult))
                settle()
                for t in range(TT):
                    dve.wait_ge(*drained(("ct", l, t, 0)))
                    x = tok[:, t, 0:512].rearrange("p (h n) -> p h n", n=HD)
                    v.tensor_tensor(x, x, ssq[:, 8 * t:8 * t + 8].unsqueeze(2).broadcast_to([P, 8, HD]), ALU.mult)\
                        .then_inc(*mark("qk_unit", (l, t)))
                key = ("gsum", l)
                dve.wait_ge(*full(key))
                v.tensor_copy(gex, bank(key)[:, 0:128]).then_inc(*read(key))
                dve.wait_ge(*drained(key))
                step(v.tensor_copy(gcs, gex[:, 0:32]))
                v.tensor_tensor(kdf, gex[:, 32:64], gex[:, 0:32], ALU.subtract).then_inc(*mark("gate_sums", l))
                dve.wait_ge(*when("gate_sums_exp", l))
                step(v.tensor_tensor(bgf, beta, gex[:, 0:32], ALU.mult))
                for p in range(2):
                    for c in range(2):
                        hp = slice(p * HD, (p + 1) * HD)
                        step(v.tensor_copy(
                            sdec.rearrange("p (g c i) -> p g c i", c=2, i=2)[hp, :, c, :],
                            gex[:, 64 + 32 * c:96 + 32 * c].rearrange("p (g i q) -> p g i q", i=2, q=2)[hp, :, :, p]))
                settle()
                v.tensor_copy(mx[:, 1:2], gcs[:, 0:1]).then_inc(*mark("decays", l))

            def delta(l, d):
                for t in range(TT):
                    key = ("dec", l, d, t)
                    at = 16 * d + 4 * t
                    dve.wait_ge(*full(key))
                    v.tensor_tensor(grp(gP1, t).rearrange("p (h n) -> p h n", h=4),
                                    bank(key)[:, :].rearrange("p (h n) -> p h n", h=4),
                                    gcs[:, at:at + 4].unsqueeze(2).broadcast_to([P, 4, P]), ALU.subtract)\
                        .then_inc(*read(key))
                for t in range(TT):
                    dve.wait_ge(*when("decay_ready", (l, d, t)))
                    for p in range(2):
                        key = ("kkqk", l, d, t, p)
                        dve.wait_ge(*full(key))
                        for j, dst in enumerate((gAT, gAtt)):
                            def heads(x):
                                return grp(x, t).rearrange("p (i q n) -> p i q n", i=2, q=2)[:, :, p, :]
                            ins = v.tensor_tensor(heads(dst), bank(key)[:, j * 256:(j + 1) * 256].rearrange(
                                "p (i n) -> p i n", i=2), heads(gP1), ALU.mult)
                            if j == 0:
                                step(ins)
                        ins.then_inc(*read(key))
                for t in range(TT):
                    dve.wait_ge(*when("NT", (l, d, 0, t)))
                    v.tensor_tensor(grp(gTT, t).rearrange("p (h n) -> p h n", h=4),
                                    ident.unsqueeze(1).broadcast_to([P, 4, P]),
                                    grp(gNT, t).rearrange("p (h n) -> p h n", h=4), ALU.subtract)\
                        .then_inc(*mark("TT_first", (l, d, t)))
                for lv in range(1, 6):
                    for t in range(TT):
                        for name, dst in (("TP", gT), ("TTP", gTT)):
                            if name == "TP" and lv == 5:
                                continue
                            key = (name, l, d, lv, t)
                            dve.wait_ge(*full(key))
                            if lv == 1:
                                dve.wait_ge(*(drained(("T0", l, d, t)) if name == "TP" else when("TT_first", (l, d, t))))
                            else:
                                dve.wait_ge(*drained((name, l, d, lv - 1, t)))
                            v.tensor_tensor(grp(dst, t), grp(dst, t), bank(key)[:, :], ALU.subtract)\
                                .then_inc(*read(key))
                if d:
                    dve.wait_ge(*drained(("su", l, 0, 7)))
                step(v.memset(vnew, 0.0))
                v.memset(state[:, :, :], 0.0).then_inc(*mark("state_zero", (l, d)))
                for n, (t, c) in enumerate(steps(d)):
                    cs = slice(c * CHUNK, (c + 1) * CHUNK)
                    dve.wait_ge(*full(("vn", l, d, n)))
                    v.tensor_tensor(vnew[cs, :], grp(gWU, t)[cs, 256:512], bank(("vn", l, d, n))[cs, 0:256],
                                    ALU.subtract).then_inc(*read(("vn", l, d, n)))
                    key = ("su", l, d, n)
                    dve.wait_ge(*full(key))
                    dve.wait_ge(*(drained(("su", l, d, n - 1)) if n else when("state_zero", (l, d))))
                    for i in range(2):
                        at = ((d * 4 + t) * 2 + c) * 2 + i
                        for p in range(2):
                            hp = slice(p * HD, (p + 1) * HD)
                            x = state[hp, i, p * HD:(p + 1) * HD]
                            ins = v.scalar_tensor_tensor(out=x, in0=x, scalar=sdec[hp, at:at + 1],
                                                         in1=bank(key)[hp, i * HD:(i + 1) * HD],
                                                         op0=ALU.mult, op1=ALU.add)
                            if (i, p) != (1, 1):
                                step(ins)
                    ins.then_inc(*read(key))
                    if n % 2:
                        key = ("go", l, d, t)
                        dve.wait_ge(*full(key))
                        o = oT[:, 2:4, t * P:(t + 1) * P]
                        b = bank(key)[:, 0:256].rearrange("p (i n) -> p i n", i=2)
                        if d == 0:
                            v.tensor_copy(o, b).then_inc(*read(key))
                        else:
                            dve.wait_ge(*drained(("go", l, 0, t)))
                            v.tensor_tensor(o, o, b, ALU.add).then_inc(*read(key))
                settle()

            def delta_finish(l):
                for t in range(TT):
                    dve.wait_ge(*drained(("go", l, 1, t)))
                v.tensor_copy(mx[:, 2:3], gcs[:, 0:1]).then_inc(*mark("delta_out", l))
                for i in range(2):
                    o = oT[:, 2 + i, :]
                    dve.wait_ge(*drained(("gvar", l, i)))
                    step(v.reciprocal(tmpA[:, :], tmpA[:, :]))
                    settle()
                    v.scalar_tensor_tensor(out=o, in0=o, scalar=VEC[l][:, V_GDNG:V_GDNG + 1], in1=tmpA[:, :],
                                           op0=ALU.mult, op1=ALU.mult).then_inc(*mark("delta_normed", (l, i)))
                    dve.wait_ge(*when("delta_normed", (l, i)))
                    dve.wait_ge(*drained(("z", l, i)))
                    v.tensor_tensor(o, o, zgate[:, i, :], ALU.mult).then_inc(*mark("mixed", l if i else (l, 0)))

            def residual(key, k, gate, lo):
                dve.wait_ge(*full(key))
                for cols, s in halves(lo):
                    ins = v.scalar_tensor_tensor(out=xT[:, k, cols], in0=bank(key)[:, cols],
                                                 scalar=modv[:, gate + k, s:s + 1], in1=xT[:, k, cols],
                                                 op0=ALU.mult, op1=ALU.add)
                    if s:
                        step(ins)
                ins.then_inc(*read(key))

            def ffn():
                for half, (f0, f1) in enumerate(FF_PARTS):
                    for f in range(f0, f1):
                        dve.wait_ge(*full(("fb", f)))
                        dve.wait_ge(*drained(("fa", f)))
                        v.tensor_tensor(hidT(f - f0), (tmpA, tmpB)[f % 2][:, :], bank(("fb", f))[:, :], ALU.mult)\
                            .then_inc(*read(("fb", f)))
                    for k in range(DT):
                        if half:
                            dve.wait_ge(*drained(("fy", 0, k)))
                        residual(("fy", half, k), k, 40, 0)

            def phase_end(k):
                step(v.tensor_copy(mx[:, 0:1], gcs[:, 0:1]))
                settle()
                dve.sem_inc(phase_done, 1)
                dve.wait_ge(phase_done, 4 * k)

            for l in range(2):
                ada(l)
                norm(2 * l)
                project(l)
                window(l)
                retention(l)
                delta_prepare(l)
                phase_end(2 * l + 1)
                delta(l, 0)
                delta(l, 1)
                delta_finish(l)
                phase_end(2 * l + 2)
                for k in range(DT):
                    residual(("wo", l, k), k, 16, 0 if l == 0 else CTX)
                norm(2 * l + 1, 0 if l == 0 else CTX)
                if l == 0:
                    ffn()

            key = "logits"
            dve.wait_ge(*full(key))
            v.tensor_copy(lgts, bank(key)[:, 0:16].rearrange("p (t e) -> p t e", t=2)).then_inc(*read(key))
            dve.wait_ge(*drained(key))
            ex = const("expert")
            step(v.tensor_tensor(less, ex.unsqueeze(1).broadcast_to([P, 8, 8]),
                                 ex.unsqueeze(2).broadcast_to([P, 8, 8]), ALU.is_lt))
            step(v.reduce_max(nm1, lgts, AX_X))
            settle()
            v.tensor_scalar(nm1, nm1, -1.0, None, ALU.mult).then_inc(*mark("route_max", 0))
            for t in range(2):
                a = lgts[:, t, :].unsqueeze(1).broadcast_to([P, 8, 8])
                b = lgts[:, t, :].unsqueeze(2).broadcast_to([P, 8, 8])
                step(v.tensor_tensor(cmp1, a, b, ALU.is_gt))
                step(v.tensor_tensor(cmp2, a, b, ALU.is_equal))
                settle()
                step(v.tensor_tensor(cmp2, cmp2, less, ALU.mult))
                settle()
                step(v.tensor_tensor(cmp1, cmp1, cmp2, ALU.add))
                settle()
                step(v.reduce_sum(rank, cmp1, AX_X))
                settle()
                ins = v.tensor_scalar(sel[:, t, :], rank, 2.0, None, ALU.is_lt)
                ins.then_inc(*mark("chosen", 0 if t else ("first", 0)))
            dve.wait_ge(*when("chosen", 0))
            dve.wait_ge(*when("route_exp", 0))
            step(v.tensor_tensor(wexp, wexp, sel, ALU.mult))
            settle()
            step(v.reduce_sum(wsum, wexp, AX_X))
            settle()
            step(v.reciprocal(wsum, wsum))
            settle()
            step(v.tensor_tensor(wexp, wexp, wsum.unsqueeze(2).broadcast_to([P, 2, 8]), ALU.mult))
            key = "places"
            dve.wait_ge(*full(key))
            v.tensor_copy(place, bank(key)[:, 0:24]).then_inc(*read(key))
            dve.wait_ge(*drained(key))
            settle()
            pos = place[:, 0:16].rearrange("p (t e) -> p t e", t=2)
            step(v.tensor_scalar(over, place[:, 16:24], float(P), None, ALU.is_gt))
            settle()
            step(v.tensor_tensor(cmp1, less, over.unsqueeze(1).broadcast_to([P, 8, 8]), ALU.mult))
            step(v.reduce_sum(intf[:, 0:1], over, AX_X))
            step(v.memset(items[:, :, :, :], 0.0))
            step(v.memset(yacc[:, :, :], 0.0))
            settle()
            step(v.reduce_sum(rank, cmp1, AX_X))
            for i, src in enumerate((pos, sel, wexp)):
                step(v.tensor_copy(items[:, i, 0:8, :], src.rearrange("p t e -> p e t")))
            settle()
            for o in range(3):
                step(v.scalar_tensor_tensor(out=cmp2[:, 0, :], in0=rank, scalar=float(o), in1=over,
                                            op0=ALU.is_equal, op1=ALU.mult))
                settle()
                step(v.tensor_tensor(cmp2[:, 1, :], cmp2[:, 0, :], ex, ALU.mult))
                for i, src in enumerate((pos, sel, wexp)):
                    step(v.tensor_tensor(cmp1[:, 2 * i:2 * i + 2, :], src,
                                         cmp2[:, 0, :].unsqueeze(1).broadcast_to([P, 2, 8]), ALU.mult))
                settle()
                step(v.reduce_sum(intf[:, 1 + o:2 + o], cmp2[:, 1, :], AX_X))
                for i in range(3):
                    step(v.reduce_sum(items[:, i, 8 + o, :], cmp1[:, 2 * i:2 * i + 2, :], AX_X))
                settle()
                step(v.tensor_scalar(items[:, 0, 8 + o, :], items[:, 0, 8 + o, :], float(P), None, ALU.subtract))
                settle()
            v.tensor_copy(ints[:, 0:4], intf).then_inc(ints_ready, 1)

            for i, dst in ((1, pick), (2, wpick)):
                for t in range(2):
                    v.tensor_scalar(dst[:, t * P:(t + 1) * P], const("iota"), itemf[:, t:t + 1],
                                    itemf[:, 24 * i + t:24 * i + t + 1], ALU.is_equal, ALU.mult)\
                        .then_inc(moe_picks, 1)
            dve.wait_ge(moe_picks, 4)
            dve.sem_inc(moe_sel_ready, 1)
            for counted in (moe_hid_ready, moe_y_ready, moe_added):
                dve.sem_inc(counted, 1)

            def item(u):
                for c in range(EC):
                    dve.wait_ge(moe_up_done, u * EC + (EC + c + 1))
                    dve.wait_ge(moe_silu_ready, u * EC + (c + 2))
                    dve.wait_ge(moe_turned, u * EC + max(c, 1))
                    v.tensor_tensor(hid[:, (c % 2) * 512:(c % 2) * 512 + 512], (tmpA, tmpB)[c % 2][:, :],
                                    psum[2 + c % 2][:, :], ALU.mult).then_inc(moe_hid_ready, 1)
                    if c == 2:
                        dve.wait_ge(moe_spread, u + 1)
                        for i, dst in ((1, pick), (2, wpick)):
                            for t in range(2):
                                v.tensor_scalar(dst[:, t * P:(t + 1) * P], const("iota"),
                                                itemf[:, bass.ds(u * 2 + (t + 2), 1)],
                                                itemf[:, bass.ds(u * 2 + (t + 2 + 24 * i), 1)],
                                                ALU.is_equal, ALU.mult).then_inc(moe_picks, 1)
                        dve.wait_ge(moe_picks, u * 4 + 8)
                        dve.sem_inc(moe_sel_ready, 1)
                dve.wait_ge(moe_down_done, u * EC + 2 * EC)
                v.tensor_copy(yrow[:, 0:512], psum[6][:, :]).then_inc(moe_y_half, 1)
                dve.wait_ge(moe_y_half, u + 1)
                v.tensor_copy(yrow[:, 512:1024], psum[7][:, :]).then_inc(moe_y_ready, 1)
                for j in range(4):
                    dve.wait_ge(moe_scattered, u * 4 + (j + 1))
                    if j == 0:
                        dve.wait_ge(moe_added, u * 4 + 1)
                    y = yacc[:, 2 * j:2 * j + 2, :]
                    v.tensor_tensor(y, y, psum[4 + j % 2][:, :].rearrange("p (k n) -> p k n", k=2), ALU.add)\
                        .then_inc(moe_added, 1)

            with dve.Fori(0, EXPERTS) as e:
                item(e)
            n_over = dve.value_load(ints[0:1, 0:1], min_val=0, max_val=3)
            with dve.Fori(0, ITEMS - EXPERTS) as o:
                with dve.If(o < n_over):
                    item(o + EXPERTS)
            settle()
            step(v.memset(wsum, 0.0))
            settle()
            for k in range(DT):
                v.scalar_tensor_tensor(out=xT[:, k, CTX:TOK], in0=yacc[:, k, :], scalar=modv[:, 40 + k, 0:1],
                                       in1=xT[:, k, CTX:TOK], op0=ALU.mult, op1=ALU.add)\
                    .then_inc(*mark("final_residual", k))
            norm(4, CTX)

        @block.gpsimd
        def _(pool):
            g = nc.gpsimd
            step, settle = stepper(pool, "pool_step")

            def conv(l):
                if l:
                    pool.wait_ge(*drained(("fy", 1, DT - 1)))
                step(g.memset(cin[:, :, :, 0:2], 0.0))
                g.memset(cin[:, :, :, 258:260], 0.0).then_inc(*mark("pads", l))
                pool.wait_ge(*drained(("vec", l)))
                pool.wait_ge(*when("pads", l))
                for c in range(6):
                    pool.wait_ge(*drained(("gc", l, c)))
                    for k in range(5):
                        w = VEC[l][:, V_CONV + 6 * k + c:V_CONV + 6 * k + c + 1]
                        x = cin[:, c, :, k:k + 256]
                        tap = taps[:, (k % 2) * 512:(k % 2) * 512 + 512].rearrange("p (s n) -> p s n", s=2)
                        if k == 0:
                            step(g.tensor_scalar(acc[:, c], x, w, None, ALU.mult))
                            continue
                        step(g.tensor_scalar(tap, x, w, None, ALU.mult))
                        settle()
                        ins = g.tensor_tensor(acc[:, c], acc[:, c], tap, ALU.add)
                        if k < 4:
                            step(ins)
                    ins.then_inc(*mark("conv", (l, c)))

            def phase_end(k):
                step(g.memset(poolone[:, :], 0.0))
                settle()
                pool.sem_inc(phase_done, 1)
                pool.wait_ge(phase_done, 4 * k)

            def scaled(dst, src, f, at):
                return g.tensor_tensor(dst.rearrange("p (h n) -> p h n", h=4), src.rearrange("p (h n) -> p h n", h=4),
                                       f[:, at:at + 4].unsqueeze(2).broadcast_to([P, 4, HD]), ALU.mult)

            def delta(l, d):
                if d == 0:
                    pool.wait_ge(*when("decays", l))
                    for t in range(TT):
                        pool.wait_ge(*when("qk_unit", (l, t)))
                        pool.wait_ge(*drained(("ct", l, t, 1)))
                for t in range(TT):
                    at = 16 * d + 4 * t
                    if t >= 2:
                        pool.wait_ge(*full(("kq", l, d, t - 2)))
                    elif d:
                        pool.wait_ge(*full(("kq", l, 0, t + 2)))
                    if d:
                        pool.wait_ge(*full(("wu", l, 0, t)))
                    q, k, vv = tok[:, t, 0:256], tok[:, t, 256:512], tok[:, t, 512:768]
                    step(scaled(kbuf(t)[:, 0:256], k, beta, at))
                    step(scaled(kbuf(t)[:, 256:512], q, gex, at))
                    step(scaled(grp(gRW, t, 256), k, bgf, at))
                    scaled(grp(gRU, t, 256), vv, beta, at).then_inc(*mark("kbqd", (l, d, t)))
                if d:
                    pool.wait_ge(*full(("su", l, 0, 7)))
                for t in range(TT):
                    pool.wait_ge(*drained(("dec", l, d, t)))
                    x = grp(gP1, t).rearrange("p (h n) -> p h n", h=4)
                    g.tensor_tensor(x, x, const(f"neg{d}").unsqueeze(1).broadcast_to([P, 4, P]), ALU.add)\
                        .then_inc(*mark("decay_masked", (l, d, t)))
                for t in range(TT):
                    scaled(grp(gKD, t, 256), tok[:, t, 256:512], kdf, 16 * d + 4 * t)\
                        .then_inc(*mark("kd", (l, d, t)))
                for lv in range(6):
                    for t in range(TT):
                        if lv == 0:
                            for p in range(2):
                                pool.wait_ge(*drained(("kkqk", l, d, t, p)))
                        elif lv == 1:
                            pool.wait_ge(*when("TT_first", (l, d, t)))
                        else:
                            pool.wait_ge(*full(("P1", l, d, lv - 1, t)))
                        g.tensor_tensor(grp(gNT, t).rearrange("p (h n) -> p h n", h=4),
                                        grp(gAT, t).rearrange("p (h n) -> p h n", h=4),
                                        const(f"level{d}", lv).unsqueeze(1).broadcast_to([P, 4, P]), ALU.mult)\
                            .then_inc(*mark("NT", (l, d, lv, t)))

            pool.wait_ge(*when("table_in", 0))
            for l in range(2):
                conv(l)
                phase_end(2 * l + 1)
                delta(l, 0)
                delta(l, 1)
                phase_end(2 * l + 2)
        assert len(was_read) == sum(uses)
        return L


_INS = ['x', 'c', 'ctx', 'c_ctx', 'ada_w', 'ada_b', 'norm1_g', 'w_in', 'ret_decay', 'ret_gn_g', 'gdn_conv_w',
        'gdn_a_log', 'gdn_dt_bias', 'gdn_norm_g', 'swa_sink', 'w_out', 'norm2_g', 'ffn_w1', 'ffn_w3', 'ffn_w2',
        'router_w', 'moe_w1', 'moe_w3', 'moe_w2', 'final_g']


def kernel(**inputs):
    import numpy as _np
    import concourse.bacc as _bacc
    from concourse import mybir as _mybir
    from concourse.bass_utils import run_bass_kernel_spmd as _run

    arrays = {f"in_{n}_dram": _np.ascontiguousarray(inputs[n]) for n in _INS}
    arrays["const_table"] = const_table()
    known = None
    for _ in range(2):
        nc = _bacc.Bacc("TRN2", target_bir_lowering=False, num_devices=1)
        A = {n: nc.dram_tensor(f"in_{n}_dram", inputs[n].shape, _mybir.dt.float32, kind="ExternalInput").ap()
             for n in _INS}
        table = nc.dram_tensor("const_table", (P, NCONST), _mybir.dt.float32, kind="ExternalInput").ap()
        out = nc.dram_tensor("out_0_dram", (1, LAT, D), _mybir.dt.float32, kind="ExternalOutput").ap()
        known = build(nc, A, out, table, known)
    r = _run(nc, [arrays], core_ids=[0])
    return r.results[0]["out_0_dram"]
```

```python
from contextlib import ExitStack

import numpy as np

import concourse.bass as bass
from concourse import mybir

F32 = mybir.dt.float32
I32 = mybir.dt.int32
ALU = mybir.AluOpType
ACT = mybir.ActivationFunctionType
AX_X = mybir.AxisListType.X

P = 128
D = 1024
DT = D // P
CTX = 256
LAT = 256
TOK = CTX + LAT
TT = TOK // P
HD = 64
SCALE = HD ** -0.5
EPS = 1e-6
CHUNK = 64
IN_COLS = 2832
FF = 2816
EXPERTS = 8
EFF = 3584
EC = EFF // 512
ITEMS = EXPERTS + 3
NEG = -1e30
SLOT = 4096
NSLOT = 7
LEVELS = (1, 2, 4, 8, 16, 32)

CONST = {}
_at = 0
for _name, _n in (("ident", P), ("ones", P), ("eps", 1), ("expert", 8), ("head_mean", P), ("incl0", P), ("incl1", P), ("half0", P),
                  ("half1", P), ("neg0", P), ("neg1", P), ("before", P), ("iota", P), ("same", P),
                  ("level0", 6 * P), ("level1", 6 * P), ("diff", 512), ("diag2", 512),
                  ("band", 512), ("cos", LAT), ("sin", LAT)):
    CONST[_name] = (_at, _n)
    _at += _n
NCONST = _at
NEARLY = CONST["head_mean"][0]

FF_PARTS = ((0, 12), (12, 22))


def steps(d):
    return [(t, c) for t in (0, 1, 2, 3) for c in (0, 1)] if d == 0 else \
        [(t, c) for t in (1, 0, 3, 2) for c in (1, 0)]


V_ADAB, V_N1, V_N2, V_CONV, V_RETG, V_FIN, V_GDNG, V_C, V_CC, NVEC = 0, 48, 56, 64, 94, 96, 104, 105, 113, 121


def const_table():
    t = np.zeros((P, NCONST), np.float32)

    def put(name, a):
        o, n = CONST[name]
        t[:, o:o + n] = np.asarray(a, np.float32).reshape(P, n)

    r = np.arange(P)
    row, col = r[:, None], r[None, :]
    same = row // CHUNK == col // CHUNK
    put("ident", np.eye(P))
    put("ones", np.ones((P, P)))
    put("head_mean", (row // HD == col // HD) / HD)
    put("incl0", same & (row <= col))
    put("incl1", same & (row >= col))
    put("half0", np.broadcast_to(row < CHUNK, (P, P)))
    put("half1", np.broadcast_to(row >= CHUNK, (P, P)))
    put("same", same)
    put("neg0", np.where(same & (col >= row), 0.0, NEG))
    put("neg1", np.where(same & (col <= row), 0.0, NEG))
    put("before", row < col)
    put("iota", np.broadcast_to(col, (P, P)))
    lv = [(col // b == row // b + 1) & ((col // b) % 2 == 1) for b in LEVELS]
    put("level0", np.stack(lv, 1))
    put("level1", np.stack([m.T for m in lv], 1))
    j = np.arange(256).reshape(2, P).T[:, :, None]
    i = np.arange(256)[None, None, :]
    put("diff", i - j)
    put("diag2", 1.0 + (i == j))
    put("band", np.where(np.abs(i - j) <= 128, 0.0, NEG))
    n = np.arange(LAT, dtype=np.float32)
    inv = np.float32(10000.0) ** (-np.arange(16, dtype=np.float32) / np.float32(16))
    f = r % 32
    ang = np.where(f[:, None] < 16, (n // 64)[None, :], (n % 64)[None, :]).astype(np.float32) * inv[f % 16][:, None]
    put("cos", np.cos(ang))
    put("sin", np.sin(ang) * np.where(r % 64 < 32, -1.0, 1.0)[:, None])
    put("eps", np.full((P, 1), EPS))
    put("expert", np.broadcast_to(np.arange(8), (P, 8)))
    return t


def needed(l):
    return 0 if l == 0 else CTX


class Ledger:

    def __init__(self, nc, ctx, known):
        self.nc, self.ctx, self.known = nc, ctx, known
        self.sems, self.count, self.at = {}, {}, {}

    def sem(self, name):
        if name not in self.sems:
            self.sems[name] = self.ctx.enter_context(self.nc.semaphore(name))
        return self.sems[name]

    def mark(self, name, key, n=1):
        self.count[name] = self.count.get(name, 0) + n
        assert (name, key) not in self.at, (name, key)
        self.at[name, key] = self.count[name]
        return self.sem(name), n

    def when(self, name, key):
        if self.known is None:
            return self.sem(name), 1
        return self.sem(name), self.known.at[name, key]

    def note(self, name, key, value):
        assert (name, key) not in self.at, (name, key)
        self.at[name, key] = value

    def noted(self, name, key, default):
        return self.at.get((name, key), default) if self.known is None else self.known.at[name, key]


def build(nc, A, out, ctab, known):
    ctx = ExitStack()
    with ctx:
        L = Ledger(nc, ctx, known)
        mark, when = L.mark, L.when

        def sb(name, n, dt=F32):
            return ctx.enter_context(nc.sbuf_tensor(name, [P, n], dt))

        ring = sb("ring", NSLOT * SLOT)
        xT = sb("xT", DT * TOK)[:, :].rearrange("p (k n) -> p k n", k=DT)
        hbuf = sb("hT", DT * TOK)
        hT = hbuf[:, :].rearrange("p (k n) -> p k n", k=DT)
        oT = hT
        table = sb("table", NCONST)
        work = sb("work", 6192)
        gates = sb("gates", 2048)
        tmpA, tmpB = sb("tmpA", 512), sb("tmpB", 512)
        vecT = sb("vecT", 2 * P)
        mods = [sb(f"mods{l}", 96) for l in range(2)]
        cond = sb("cond", DT * 14)
        arow = sb("arow", 512)
        one = sb("one", 1)
        rows = sb("rows", 64)
        small = sb("small", 720)
        ints = sb("ints", 4, I32)
        psum = [ctx.enter_context(nc.psum_tensor(f"bank{i}", [P, 512], F32)) for i in range(8)]

        def const(name, i=None):
            o, n = CONST[name]
            return table[:, o:o + n] if i is None else table[:, o + i * P:o + (i + 1) * P]

        ident = const("ident")
        eps = const("eps")

        def slot(s):
            return ring[:, s * SLOT:(s + 1) * SLOT]

        arena = ring[:, 2 * SLOT:7 * SLOT]

        def carve(base, sizes):
            got = []
            for n in sizes:
                got.append(base[:, carve.at:carve.at + n])
                carve.at += n
            return got

        carve.at = SLOT
        rqk, rv, sq, skd, sv, decay, smask, sc, pr, pT, oraw, taps = carve(
            arena, (2048, 1024, 2048, 1024, 512, 2048, 3072, 1024, 1024, 1024, 512, 1024))
        rqk = rqk.rearrange("p (c n) -> p c n", c=4)
        rv = rv.rearrange("p (t n) -> p t n", t=TT)
        sq = sq.rearrange("p (c n) -> p c n", c=4)
        skd = skd.rearrange("p (c n) -> p c n", c=2)
        sv = sv.rearrange("p (t n) -> p t n", t=TT)
        assert carve.at <= 5 * SLOT
        carve.at = 0
        gT, gTT, gAT, gP1, gNT, gAtt, gWU, gKQ, gKD, gRW, gRU, gKB = carve(
            arena, (2048,) * 8 + (1024,) * 4)
        assert carve.at == 5 * SLOT

        def grp(buf, t, n=512):
            return buf[:, t * n:(t + 1) * n]

        def kbuf(t):
            return grp(gKB, t % 2)

        def smk(h, part):
            return grp(smask, 3 * (h % 2) + part)

        def dec(h):
            return grp(decay, h % 2, 1024)

        cin = work[:, 0:3120].rearrange("p (c s n) -> p c s n", c=6, s=2)
        tok = work[:, 0:3072].rearrange("p (t n) -> p t n", t=TT)
        acc = work[:, 3120:6192].rearrange("p (c s n) -> p c s n", c=6, s=2)
        acc2 = work[:, 3120:6192].rearrange("p (c n) -> p c n", c=6)
        qkT = work[:, 3120:3120 + 2048].rearrange("p (c n) -> p c n", c=4)
        rgate = gates[:, 0:1024].rearrange("p (c n) -> p c n", c=2)
        zgate = gates[:, 1024:2048].rearrange("p (c n) -> p c n", c=2)

        vrows = gates[:, 0:2 * P]
        xin = hbuf[:, :]

        def squares(n):
            return work[:, 0:DT * TOK].rearrange("p (k n) -> p k n", k=DT) if n in (0, 1, 3) else hT

        def hidT(f):
            return work[:, f * 512:(f + 1) * 512]

        hrow = work[:, 0:2048].rearrange("p (t n) -> p t n", t=2)
        osb = work[:, 0:2048]
        yrow = work[:, 2048:3072]
        yacc = work[:, 3072:5120].rearrange("p (k n) -> p k n", k=DT)
        pick, wpick, spread = (work[:, a:a + 256] for a in (5120, 5376, 5632))
        hid, mhT = gates[:, 0:1024], gates[:, 1024:2048]
        hg = hT[:, :, 0:P]

        sm_at = [0]

        def sml(n):
            sm_at[0] += n
            return small[:, sm_at[0] - n:sm_at[0]]

        ab = sml(64)
        spz, spe, spl = sml(32), sml(32), sml(32)
        gl = sml(32)
        beta = sml(32)
        gex = sml(128)
        gcs = sml(32)
        kdf = sml(32)
        bgf = sml(32)
        sdec = sml(32)
        ssq = sml(32)
        mx, nmx, rsm, es, den = (sml(4) for _ in range(5))
        lgt, lsum, l256, ln1, ealog = sml(8), sml(4), sml(8), sml(4), sml(8)
        router = sb("router", 64)[:, :].rearrange("p (k e) -> p k e", k=DT)
        rt = small[:, 0:352]
        rt_at = [0]

        def rts(n):
            rt_at[0] += n
            return rt[:, rt_at[0] - n:rt_at[0]]
        lgts = rts(16).rearrange("p (t e) -> p t e", t=2)
        sel = rts(16).rearrange("p (t e) -> p t e", t=2)
        wexp = rts(16).rearrange("p (t e) -> p t e", t=2)
        less, cmp1, cmp2 = (rts(64).rearrange("p (e f) -> p e f", e=8) for _ in range(3))
        rank, over, nm1, wsum, place, intf = rts(8), rts(8), rts(2), rts(2), rts(24), rts(4)
        itemf = small[:, 352:424]
        items = itemf[:, :].rearrange("p (i u t) -> p i u t", i=3, u=12)
        poolone = sb("poolone", 1)
        krot = oraw
        state = tmpB[:, 0:256].rearrange("p (c n) -> p c n", c=2)
        vnew = tmpA[:, 0:256]

        VEC = [vecT[:, l * P:(l + 1) * P] for l in range(2)]
        modv = [m[:, :].rearrange("p (m v) -> p m v", v=2) for m in mods]
        condv = cond[:, :].rearrange("p (k n) -> p k n", k=DT)

        loads = []
        where = {}

        def load(key, s, pieces):
            loads.append((key, s, pieces))
            where[key] = s

        def wtile(ap, c0, n):
            return ap[:, c0:c0 + n].rearrange("(k p) n -> p k n", p=P)

        def kslot(s, n=512):
            return slot(s)[:, 0:DT * n].rearrange("p (k n) -> p k n", k=DT)

        def load_ada(l, n, s):
            load(("ada", l, n), s, [(kslot(s), wtile(A["ada_w"][l], n * 512, 512))])

        for l in range(2):
            if l == 0:
                for n in range(4):
                    load_ada(0, n, 3 + n)
            W = A["w_in"][l]
            for n, (name, c0) in enumerate((("gqk", 1024), ("gvz", 1536), ("kvab", None), ("sq", 2064),
                                            ("rqk", 0), ("rvg", 512))):
                v = kslot(n % 3)
                if name == "kvab":
                    pieces = [(v[:, :, 0:256], wtile(W, 2576, 256)), (v[:, :, 256:272], wtile(W, 2048, 16))]
                else:
                    pieces = [(v, wtile(W, c0, 512))]
                load((name, l), n % 3, pieces)
            if l == 0:
                for i, (la, n) in enumerate([(0, n) for n in range(4, 12)] + [(1, n) for n in range(12)]):
                    load_ada(la, n, i % 2)
            for n in range(2):
                load(("wo", l, n), n, [(kslot(n), wtile(A["w_out"][l], n * 512, 512))])
            if l == 0:
                s = 2
                for f0, f1 in FF_PARTS:
                    for f in range(f0, f1, 2):
                        v = kslot(s)
                        load(("up", f), s, [(v[:, :, 0:256], wtile(A["ffn_w1"][0], f * P, 256)),
                                            (v[:, :, 256:512], wtile(A["ffn_w3"][0], f * P, 256))])
                        s = (s + 1) % NSLOT
                    for f in range(f0, f1, 4):
                        m = min(4, f1 - f)
                        v = slot(s)[:, 0:m * D].rearrange("p (q n) -> p q n", q=m)
                        load(("down", f), s, [(v, A["ffn_w2"][0][f * P:(f + m) * P, :].rearrange(
                            "(q p) n -> p q n", p=P))])
                        s = (s + 1) % NSLOT

        phase_done = ctx.enter_context(nc.semaphore("phase_done"))
        AFTER_PHASE = {("up", 0): 2}
        moe_gate_done = ctx.enter_context(nc.semaphore("moe_gate_done"))
        moe_up_done = ctx.enter_context(nc.semaphore("moe_up_done"))
        moe_down_done = ctx.enter_context(nc.semaphore("moe_down_done"))
        moe_slot_full = [ctx.enter_context(nc.semaphore(f"moe_slot_full{s}")) for s in range(NSLOT)]
        (moe_sel_ready, moe_gathered, moe_rows_ready, moe_spread, moe_spread_ready, moe_silu_ready,
         moe_hid_ready, moe_turned, moe_hidT_ready, moe_y_ready, moe_scattered, moe_added, ints_ready,
         out_stored, moe_picks, moe_y_half) = [ctx.enter_context(nc.semaphore(n)) for n in (
             "moe_sel_ready", "moe_gathered", "moe_rows_ready", "moe_spread", "moe_spread_ready",
             "moe_silu_ready", "moe_hid_ready", "moe_turned", "moe_hidT_ready", "moe_y_ready",
             "moe_scattered", "moe_added", "ints_ready", "out_stored", "moe_picks", "moe_y_half")]
        PRODUCT_DONE = {"w1": moe_gate_done, "w3": moe_up_done, "w2": moe_down_done}
        STREAM = [("w1", 0), ("w3", 0)]
        for c in range(EC):
            STREAM += [("w1", c + 1), ("w3", c + 1)] if c + 1 < EC else []
            STREAM += [("w2", c)]
        assert len(STREAM) == 3 * NSLOT
        MOE_SLOT = {k: (n + 2) % NSLOT for n, k in enumerate(STREAM)}
        MOE_USE = {k: n // NSLOT for n, k in enumerate(STREAM)}

        block = ctx.enter_context(nc.Block())

        uses = [0] * 8
        was_read = set()

        def open_bank(pe, key, b):
            if uses[b]:
                pe.wait_ge(L.sem(f"bank_read{b}"), uses[b])
            uses[b] += 1
            L.note("bank", key, b)
            L.note("turn", key, uses[b])
            return psum[b]

        def filled(key):
            return mark(f"bank_full{L.at['bank', key]}", key)

        def bank(key):
            return psum[L.noted("bank", key, 0)]

        def full(key):
            return when(f"bank_full{L.noted('bank', key, 0)}", key)

        def read(key):
            assert key not in was_read, key
            was_read.add(key)
            return L.sem(f"bank_read{L.noted('bank', key, 0)}"), 1

        def drained(key):
            return L.sem(f"bank_read{L.noted('bank', key, 0)}"), L.noted("turn", key, 1)

        def weights(key):
            return when(f"slot_full{where[key]}", key)

        def fill_frees(key, product):
            L.note("released", key, (f"bank_full{L.at['bank', product]}", product))

        def stepper(eng, name):
            sem = L.sem(name)
            n = [0]

            def step(ins):
                n[0] += 1
                ins.then_inc(sem, 1)

            def settle():
                eng.wait_ge(sem, n[0])
            return step, settle

        @block.sync
        def _(sp):
            for t in range(TT):
                src = A["ctx"] if t < 2 else A["x"]
                sp.dma_start(xin[:, t * D:(t + 1) * D], src[0, (t % 2) * P:(t % 2 + 1) * P, :])\
                    .then_inc(*mark("x_in", t, 16))
            sp.wait_ge(*when("vec_in0", 0))
            held = {}
            for key, s, pieces in loads:
                if key == ("gqk", 0):
                    sp.dma_start(table[:, NEARLY:NCONST], ctab[:, NEARLY:NCONST])\
                        .then_inc(*mark("table_in", "all", 16))
                if s in held:
                    sp.wait_ge(*when(*L.noted("released", held[s], ("bank_full0", "-"))))
                if key in AFTER_PHASE:
                    sp.wait_ge(phase_done, 4 * AFTER_PHASE[key])
                for i, (dst, src) in enumerate(pieces):
                    sp.dma_start(dst, src).then_inc(
                        *mark(f"slot_full{s}", key if i == len(pieces) - 1 else (key, i), 16))
                held[s] = key
            sp.wait_ge(phase_done, 4 * 4)
            w1, w3, w2 = A["moe_w1"][0], A["moe_w3"][0], A["moe_w2"][0]

            def expert(item, e):
                w1e = w1[bass.ds(e, 1)].rearrange("o (k p) n -> p (o k) n", p=P)
                w3e = w3[bass.ds(e, 1)].rearrange("o (k p) n -> p (o k) n", p=P)
                w2e = w2[bass.ds(e, 1)].rearrange("o (k p) n -> p (o k) n", p=P)
                for n, (kind, c) in enumerate(STREAM):
                    s = MOE_SLOT[kind, c]
                    if n < NSLOT:
                        k0, c0 = STREAM[n + 2 * NSLOT]
                        sp.wait_ge(PRODUCT_DONE[k0], item * EC + (c0 + 1))
                    else:
                        k0, c0 = STREAM[n - NSLOT]
                        sp.wait_ge(PRODUCT_DONE[k0], item * EC + (EC + c0 + 1))
                    if kind == "w2":
                        dst = slot(s).rearrange("p (q n) -> p q n", q=4)
                        src = w2e[:, 4 * c:4 * c + 4, :]
                    else:
                        dst = kslot(s)
                        src = (w1e if kind == "w1" else w3e)[:, :, c * 512:(c + 1) * 512]
                    sp.dma_start(dst, src).then_inc(moe_slot_full[s], 16)

            with sp.Fori(0, EXPERTS) as e:
                expert(e, e)
            sp.wait_ge(ints_ready, 1)
            n_over = sp.value_load(ints[0:1, 0:1], min_val=0, max_val=3)
            with sp.Fori(0, ITEMS - EXPERTS) as o:
                with sp.If(o < n_over):
                    e = sp.value_load(ints[0:1, bass.ds(o + 1, 1)], min_val=0, max_val=EXPERTS - 1)
                    expert(o + EXPERTS, e)
            for t in range(2):
                sp.wait_ge(*when("out_row", t))
                sp.dma_start(out[0, t * P:(t + 1) * P, :], osb[:, t * D:(t + 1) * D]).then_inc(out_stored, 16)
            sp.wait_ge(out_stored, 32)

        @block.tensor
        def _(pe):
            rot = [0]

            ada_bank = [None]

            def product(key, banks=range(8)):
                banks = [b for b in banks if b != ada_bank[0]]
                rot[0] += 1
                return open_bank(pe, key, banks[rot[0] % len(banks)])

            def mm(o, w, x, start=True, stop=True):
                return nc.tensor.matmul(o, w, x, start=start, stop=stop)

            def turn(o, x, n=P):
                return nc.tensor.transpose(o, x, ident[0:n, 0:n])

            def turn_vectors(l):
                pe.wait_ge(*when(f"vec_in{l}", l))
                o = product(("vec", l))
                turn(o[:, 0:NVEC], vrows[0:NVEC, l * P:(l + 1) * P], NVEC).then_inc(*filled(("vec", l)))

            pe.wait_ge(*when("early_in", 0))
            turn_vectors(0)
            pe.wait_ge(*when("x_in", 3))
            for k in range(DT):
                o = product(("x", k))
                for t in range(TT):
                    ins = turn(o[:, t * P:(t + 1) * P], xin[:, t * D + k * P:t * D + (k + 1) * P])
                ins.then_inc(*filled(("x", k)))

            ada_at = [0]

            def ada(count):
                for _ in range(count):
                    l, n, k = ada_at[0] // (12 * DT), ada_at[0] // DT % 12, ada_at[0] % DT
                    ada_at[0] += 1
                    g, j = divmod(n, 4)
                    key = ("ada", l, g)
                    if (j, k) == (0, 0):
                        open_bank(pe, key, 5)
                    if k == 0:
                        pe.wait_ge(*weights(("ada", l, n)))
                    ins = mm(psum[5][0:8, :], condv[:, k, 6 - 2 * j:14 - 2 * j], kslot(where["ada", l, n])[:, k, :],
                             (j, k) == (0, 0), (j, k) == (3, DT - 1))
                    if k == DT - 1:
                        if j < 3:
                            ins.then_inc(*mark("ada_slot_used", (l, n)))
                            L.note("released", ("ada", l, n), ("ada_slot_used", (l, n)))
                        else:
                            ins.then_inc(*filled(key))
                            fill_frees(("ada", l, n), key)

            def ada_turn(l, g):
                pe.wait_ge(*drained(("ada", l, g)))
                o = product(("adaT", l, g), range(6))
                for c in range(4):
                    ins = turn(o[:, 8 * c:8 * c + 8], arow[0:8, c * P:(c + 1) * P], 8)
                ins.then_inc(*filled(("adaT", l, g)))

            def sum_squares(n, k, lo=0, bank_of=None):
                key = ("ss", n)
                if k == 0:
                    if bank_of is None:
                        product(key)
                    else:
                        open_bank(pe, key, bank_of)
                pe.wait_ge(*when("square", (n, k)))
                ins = mm(psum[L.at["bank", key]][:, lo:TOK], const("ones"), squares(n)[:, k, lo:TOK],
                         k == 0, k == DT - 1)
                if k == DT - 1:
                    ins.then_inc(*filled(key))

            def norm(n, lo=0):
                for k in range(DT):
                    sum_squares(n, k, lo)

            def by_channel(key, w, c, x, lo=0, n=None):
                o = product(key)
                for k in range(DT):
                    if n is not None:
                        pe.wait_ge(*when("mod", (n, k)))
                    ins = mm(o[:, lo:TOK], w[:, k, c * P:(c + 1) * P], x[:, k, lo:TOK], k == 0, k == DT - 1)
                ins.then_inc(*filled(key))

            def by_token(key, w, c0, n, t):
                o = product(key)
                for k in range(DT):
                    ins = mm(o[:, 0:n], hT[:, k, t * P:(t + 1) * P], w[:, k, c0:c0 + n], k == 0, k == DT - 1)
                ins.then_inc(*filled(key))

            def project(l):
                for name in ("gqk", "gvz", "kvab", "sq", "rqk", "rvg"):
                    if (name, l) == ("gvz", 0):
                        turn_vectors(1)
                    pe.wait_ge(*weights((name, l)))
                    w = kslot(where[name, l])
                    if name == "gqk":
                        keys = [(("gc", l, c), c) for c in range(4)]
                    elif name == "gvz":
                        keys = [(("gc", l, 4), 0), (("gc", l, 5), 1), (("z", l, 0), 2), (("z", l, 1), 3)]
                    elif name == "kvab":
                        keys = [(("sk", l), 0)]
                    elif name == "rvg":
                        keys = [(("rg", l, 0), 2), (("rg", l, 1), 3)]
                    else:
                        keys = [((name, l, c), c) for c in range(4)]
                    for key, c in keys:
                        keys_values = name in ("kvab", "gqk", "gvz", "rqk") and \
                            not (key[0] == "z" or key[0] in ("gc", "rqk") and c < 2 and name != "gvz")
                        by_channel(key, w, c, hT, 0 if keys_values else needed(l),
                                   2 * l if key == ("gc", l, 0) else None)
                    if name == "kvab":
                        for t in range(TT):
                            key = ("vab", l, t)
                            by_token(key, w, P, 144, t)
                    if name == "rvg":
                        for t in range(TT):
                            key = ("rv", l, t)
                            by_token(key, w, 0, 256, t)
                    fill_frees((name, l), key)

            def window(l):
                q0 = 0 if l == 0 else 2
                units = [(h, t) for h in range(8) for t in range(q0, TT)]

                def score(h, t):
                    m, p = divmod(h, 2)
                    nk = CTX if t < 2 else TOK
                    if (h, t) == units[0]:
                        pe.wait_ge(*drained(("sk", l)))
                        for c in range(4):
                            pe.wait_ge(*when("sq_ready", (l, c)))
                        pe.wait_ge(*when("sk_ready", l))
                    o = product(("sc", l, h, t), range(6))
                    mm(o[:, 0:nk], sq[p * HD:p * HD + HD, m, t * P:(t + 1) * P], skd[p * HD:p * HD + HD, m // 2, 0:nk]
                       ).then_inc(*filled(("sc", l, h, t)))

                def turn_probs(h, t):
                    pe.wait_ge(*when("probs", (l, h, t)))
                    o = product(("pt", l, h, t), range(6))
                    i = units.index((h, t))
                    for k in range(2 if t < 2 else 4):
                        ins = turn(o[:, k * P:(k + 1) * P], pr[:, (i % 2) * 512 + k * P:(i % 2) * 512 + (k + 1) * P])
                    ins.then_inc(*filled(("pt", l, h, t)))

                def values(h, t):
                    m, p = divmod(h, 2)
                    i = units.index((h, t))
                    key = ("so", l, m)
                    if p == 0 and t == q0:
                        open_bank(pe, key, 6 + m % 2)
                    o = psum[6 + m % 2]
                    pe.wait_ge(*drained(("pt", l, h, t)))
                    nk = 2 if t < 2 else 4
                    for k in range(nk):
                        ins = mm(o[p * HD:p * HD + HD, t * P:(t + 1) * P], sv[:, k, (h // 4) * HD:(h // 4) * HD + HD],
                                 pT[:, (i % 2) * 512 + k * P:(i % 2) * 512 + (k + 1) * P], k == 0, k == nk - 1)
                    if (p, t) == (1, TT - 1):
                        ins.then_inc(*filled(key))

                for i in range(len(units) + 3):
                    if i < len(units):
                        score(*units[i])
                    if l == 0 and i < 4 * DT:
                        ada(1)
                    if 0 <= i - 2 < len(units):
                        turn_probs(*units[i - 2])
                    if 0 <= i - 3 < len(units):
                        values(*units[i - 3])

            def retention(l):
                parts, lo = (2 if l else 3), needed(l)
                for c in range(4):
                    pe.wait_ge(*when("rqk_ready", (l, c)))
                for t in range(TT):
                    pe.wait_ge(*drained(("rv", l, t)))

                def scores(h):
                    i, p = divmod(h, 2)
                    hp = slice(p * HD, p * HD + HD)
                    for part in range(parts):
                        key = ("rs", l, h, part)
                        o = product(key, range(6))
                        qs = slice(0, CTX) if part == 2 else slice(CTX, TOK)
                        for j in range(2):
                            kt = j if part != 1 else 2 + j
                            ins = mm(o[:, j * 256:(j + 1) * 256], rqk[hp, 2 + i, kt * P:(kt + 1) * P], rqk[hp, i, qs])
                        ins.then_inc(*filled(key))

                def values(h):
                    i, p = divmod(h, 2)
                    key = ("ro", l, i)
                    if p == 0:
                        open_bank(pe, key, 6 + i)
                    o = psum[6 + i]
                    for part in range(parts):
                        pe.wait_ge(*drained(("rs", l, h, part)))
                    hp = slice(p * HD, p * HD + HD)
                    hv = slice(h * HD, h * HD + HD)
                    for j in range(2 if l == 0 else 0):
                        mm(o[hp, 0:CTX], rv[:, j, hv], smk(h, 2)[:, j * 256:(j + 1) * 256], j == 0, j == 1)
                    for j in range(4):
                        ins = mm(o[hp, CTX:TOK], rv[:, j, hv], smk(h, j // 2)[:, (j % 2) * 256:(j % 2 + 1) * 256],
                                 j == 0, j == 3)
                    if p == 1:
                        ins.then_inc(*filled(key))
                    else:
                        ins.then_inc(*mark("ret_values", (l, h)))

                for h in range(4 + 1):
                    if h < 4:
                        scores(h)
                    if l == 0:
                        ada(3)
                    if h == 1 and l == 0:
                        ada_turn(0, 1)
                    if h >= 1:
                        values(h - 1)
                for i in range(2):
                    if l == 0:
                        ada(2)
                    pe.wait_ge(*drained(("ro", l, i)))
                    mm(product(("rmean", l, i), range(6))[:, lo:TOK], const("head_mean"), oraw[:, lo:TOK])\
                        .then_inc(*filled(("rmean", l, i)))
                    if l == 0:
                        ada(2)
                    pe.wait_ge(*when("head_square", ("r", l, i)))
                    mm(product(("rvar", l, i), range(6))[:, lo:TOK], const("head_mean"), tmpB[:, lo:TOK])\
                        .then_inc(*filled(("rvar", l, i)))

            def delta_prepare(l):
                if l == 0:
                    ada(5)
                for c in range(6):
                    pe.wait_ge(*when("conv_silu", (l, c)))
                for t in range(TT):
                    for part, cs in enumerate((range(4), range(4, 6))):
                        key = ("ct", l, t, part)
                        o = product(key)
                        for j, c in enumerate(cs):
                            ins = turn(o[:, j * P:(j + 1) * P], acc2[:, c, t * P:(t + 1) * P])
                        ins.then_inc(*filled(key))
                if l == 0:
                    ada(2)
                for t in range(TT):
                    key = ("qkt", l, t)
                    pe.wait_ge(*when("qk_unit", (l, t)))
                    o = product(key)
                    for j in range(4):
                        ins = turn(o[:, j * P:(j + 1) * P], tok[:, t, j * P:(j + 1) * P])
                    ins.then_inc(*filled(key))
                if l == 0:
                    ada(2)
                pe.wait_ge(*when("log_decay", l))
                key = ("gsum", l)
                o = product(key)
                for d in range(2):
                    mm(o[:, 16 * d:16 * d + 16], const(f"incl{d}"), gl[:, 16 * d:16 * d + 16])
                for j, name in enumerate(("same", "half0", "half1")):
                    ins = mm(o[:, 32 + 32 * j:64 + 32 * j], const(name), gl)
                ins.then_inc(*filled(key))

            def delta(l, d):
                R6 = range(6)
                for t in range(TT):
                    key = ("kq", l, d, t)
                    pe.wait_ge(*when("kbqd", (l, d, t)))
                    o = product(key, R6)
                    for j in range(4):
                        ins = turn(o[:, j * P:(j + 1) * P], kbuf(t)[:, j * P:(j + 1) * P])
                    ins.then_inc(*filled(key))
                    key = ("dec", l, d, t)
                    o = product(key, R6)
                    for h in range(4):
                        at = 16 * d + 4 * t + h
                        ins = mm(o[:, h * P:(h + 1) * P], gl[:, at:at + 1].to_broadcast([P, P]), const(f"incl{d}"))
                    ins.then_inc(*filled(key))
                for t in range(TT):
                    if l == 0:
                        ada(2 if d == 0 else 4)
                    pe.wait_ge(*drained(("kq", l, d, t)))
                    for p in range(2):
                        key = ("kkqk", l, d, t, p)
                        o = product(key, R6)
                        hp = slice(p * HD, p * HD + HD)
                        ts = slice(t * P, (t + 1) * P)
                        for i in range(2):
                            ins = mm(o[:, i * P:(i + 1) * P], qkT[hp, 2 + i, ts], grp(gKQ, t)[hp, i * P:(i + 1) * P])
                            if l and t < 2:
                                continue
                            ins = mm(o[:, (2 + i) * P:(3 + i) * P], qkT[hp, 2 + i, ts], qkT[hp, i, ts])
                        ins.then_inc(*filled(key))
                for t in range(TT):
                    key = ("T0", l, d, t)
                    pe.wait_ge(*when("TT_first", (l, d, t)))
                    o = product(key, R6)
                    for h in range(4):
                        ins = turn(o[:, h * P:(h + 1) * P], grp(gTT, t)[:, h * P:(h + 1) * P])
                    ins.then_inc(*filled(key))

                def by_head(key, a, b, t):
                    o = product(key, R6)
                    for h in range(4):
                        hs = slice(h * P, (h + 1) * P)
                        ins = mm(o[:, hs], grp(a, t)[:, hs], grp(b, t)[:, hs])
                    ins.then_inc(*filled(key))

                for v in range(1, 6):
                    for t in range(TT):
                        pe.wait_ge(*when("NT", (l, d, v, t)))
                        if v == 1:
                            pe.wait_ge(*drained(("T0", l, d, t)))
                        else:
                            pe.wait_ge(*drained(("TP", l, d, v - 1, t)))
                        by_head(("P1", l, d, v, t), gNT, gT, t)
                    for t in range(TT):
                        pe.wait_ge(*drained(("P1", l, d, v, t)))
                        if v > 1:
                            pe.wait_ge(*drained(("TTP", l, d, v - 1, t)))
                        if v < 5:
                            by_head(("TP", l, d, v, t), gTT, gP1, t)
                        by_head(("TTP", l, d, v, t), gP1, gTT, t)
                for t in range(TT):
                    key = ("wu", l, d, t)
                    pe.wait_ge(*drained(("TTP", l, d, 5, t)))
                    o = product(key, R6)
                    for h in range(4):
                        i, p = divmod(h, 2)
                        th = grp(gTT, t)[:, h * P:(h + 1) * P]
                        hs = slice(h * HD, h * HD + HD)
                        mm(o[p * HD:p * HD + HD, i * P:(i + 1) * P], grp(gRW, t, 256)[:, hs], th)
                        ins = mm(o[:, 256 + h * HD:256 + h * HD + HD], th, grp(gRU, t, 256)[:, hs])
                    ins.then_inc(*filled(key))
                pe.wait_ge(*when("state_zero", (l, d)))
                for n, (t, c) in enumerate(steps(d)):
                    cs = slice(c * CHUNK, c * CHUNK + CHUNK)
                    key = ("vn", l, d, n)
                    if l == 0:
                        ada(5 if d == 0 else 4)
                    if (l, d, n) == (0, 1, 4):
                        ada_turn(1, 1)
                    pe.wait_ge(*drained(("wu", l, d, t)))
                    if n:
                        pe.wait_ge(*drained(("su", l, d, n - 1)))
                    o = product(key, R6)
                    for i in range(2):
                        ins = mm(o[cs, i * P:(i + 1) * P], grp(gWU, t)[:, i * P + c * CHUNK:i * P + (c + 1) * CHUNK],
                                 state[:, i, :])
                    ins.then_inc(*filled(key))
                    pe.wait_ge(*when("kd", (l, d, t)))
                    go = ("go", l, d, t)
                    if n % 2 == 0 and (l == 0 or t >= 2):
                        open_bank(pe, go, 6 + (n // 2) % 2)
                    og = psum[6 + (n // 2) % 2]
                    pe.wait_ge(*drained(("vn", l, d, n)))
                    for i in range(2 if l == 0 or t >= 2 else 0):
                        cols = slice(i * P + c * CHUNK, i * P + (c + 1) * CHUNK)
                        mm(og[:, cols], state[:, i, :],
                           grp(gKQ, t)[:, (2 + i) * P + c * CHUNK:(2 + i) * P + (c + 1) * CHUNK], True, False)
                        for p in range(2):
                            h = 2 * i + p
                            ins = mm(og[p * HD:p * HD + HD, cols], vnew[:, h * HD:h * HD + HD],
                                     grp(gAtt, t)[:, h * P + c * CHUNK:h * P + (c + 1) * CHUNK], False, True)
                    if n % 2 == 1 and (l == 0 or t >= 2):
                        ins.then_inc(*filled(go))
                    key = ("su", l, d, n)
                    o = product(key, R6)
                    for h in range(4):
                        i, p = divmod(h, 2)
                        hs = slice(h * HD, h * HD + HD)
                        ins = mm(o[p * HD:p * HD + HD, i * HD:(i + 1) * HD], grp(gKD, t, 256)[cs, hs], vnew[cs, hs])
                    ins.then_inc(*filled(key))

            def delta_finish(l):
                for i in range(2):
                    pe.wait_ge(*when("head_square", ("g", l, i)))
                    mm(product(("gvar", l, i))[:, needed(l):TOK], const("head_mean"), tmpB[:, needed(l):TOK])\
                        .then_inc(*filled(("gvar", l, i)))

            def out_project(l, lo):
                pe.wait_ge(*when("mixed", l))
                for m in range(4):
                    pe.wait_ge(*drained(("so", l, m)))
                for n in range(2):
                    pe.wait_ge(*weights(("wo", l, n)))
                    for c in range(4):
                        by_channel(("wo", l, 4 * n + c), kslot(where["wo", l, n]), c, oT, lo)
                        if 4 * n + c:
                            sum_squares(2 * l + 1, 4 * n + c - 1, lo)
                    fill_frees(("wo", l, n), ("wo", l, 4 * n + 3))
                sum_squares(2 * l + 1, DT - 1, lo)

            def ffn():
                for half, (f0, f1) in enumerate(FF_PARTS):
                    for f in range(f0, f1):
                        w = kslot(where["up", f - f % 2])
                        pe.wait_ge(*weights(("up", f - f % 2)))
                        by_channel(("fa", f), w, f % 2, hT, n=None if f else 1)
                        by_channel(("fb", f), w, 2 + f % 2, hT)
                        if f % 2:
                            fill_frees(("up", f - 1), ("fb", f))
                    for d in range(DT):
                        open_bank(pe, ("fy", half, d), d)
                    for f in range(f0, f1, 4):
                        m = min(4, f1 - f)
                        pe.wait_ge(*weights(("down", f)))
                        for q in range(m):
                            pe.wait_ge(*drained(("fb", f + q)))
                        last = f + m == f1
                        w = slot(where["down", f])[:, 0:m * D].rearrange("p (q n) -> p q n", q=m)
                        for d in range(DT):
                            for q in range(m):
                                ins = mm(psum[d][:, :], w[:, q, d * P:(d + 1) * P], hidT(f + q - f0),
                                         f == f0 and q == 0, last and q == m - 1)
                            if last:
                                ins.then_inc(*filled(("fy", half, d)))
                            if last and half and d >= 2:
                                sum_squares(2, d - 2, 0, 0)
                        if last:
                            fill_frees(("down", f), ("fy", half, DT - 1))
                            if half:
                                sum_squares(2, DT - 2)
                                sum_squares(2, DT - 1)
                        else:
                            ins.then_inc(*mark("down_slot_used", f))
                            L.note("released", ("down", f), ("down_slot_used", f))

            def phase_end(k, last):
                pe.wait_ge(*full_here(last))
                pe.sem_inc(phase_done, 1)
                pe.wait_ge(phase_done, 4 * k)

            def full_here(key):
                return L.sem(f"bank_full{L.at['bank', key]}"), L.at[f"bank_full{L.at['bank', key]}", key]

            pe.wait_ge(*when("cond", 0))
            ada_bank[0] = 5
            ada(DT)
            norm(0)
            ada(3 * DT)
            ada_turn(0, 0)
            pe.wait_ge(*when("table_in", "all"))
            for l in range(2):
                ada_bank[0] = None
                project(l)
                if l == 0:
                    ada_bank[0] = 5
                window(l)
                retention(l)
                delta_prepare(l)
                phase_end(2 * l + 1, ("gsum", l))
                if l == 0:
                    ada_turn(0, 2)
                delta(l, 0)
                if l == 0:
                    ada_turn(1, 0)
                delta(l, 1)
                delta_finish(l)
                if l == 0:
                    ada_turn(1, 2)
                    assert ada_at[0] == 24 * DT
                phase_end(2 * l + 2, ("gvar", l, 1))
                ada_bank[0] = None
                if l == 1:
                    pe.sem_inc(moe_gate_done, EC)
                    pe.sem_inc(moe_up_done, EC)
                    pe.sem_inc(moe_down_done, EC - 2)
                out_project(l, needed(l))
                if l == 0:
                    ffn()
            pe.wait_ge(*full_here(("wo", 1, 7)))
            pe.sem_inc(moe_down_done, 2)
            pe.wait_ge(*when("mod", (3, DT - 1)))
            pe.wait_ge(*when("router_in", 0))
            key = "logits"
            o = product(key)
            for t in range(2):
                for k in range(DT):
                    ins = mm(o[:, t * 8:t * 8 + 8], hT[:, k, CTX + t * P:CTX + (t + 1) * P], router[:, k, :],
                             k == 0, k == DT - 1)
            ins.then_inc(*filled(key))
            for t in range(2):
                for q in range(2):
                    key = ("row", t, q)
                    o = product(key)
                    for j in range(4):
                        ins = turn(o[:, j * P:(j + 1) * P], hT[:, 4 * q + j, CTX + t * P:CTX + (t + 1) * P])
                    ins.then_inc(*filled(key))
            pe.wait_ge(*when("chosen", 0))
            key = "places"
            o = product(key)
            mm(o[:, 0:8], const("before"), sel[:, 0, :])
            mm(o[:, 8:16], const("ones"), sel[:, 0, :], True, False)
            mm(o[:, 8:16], const("before"), sel[:, 1, :], False, True)
            mm(o[:, 16:24], const("ones"), sel[:, 0, :], True, False)
            mm(o[:, 16:24], const("ones"), sel[:, 1, :], False, True).then_inc(*filled(key))
            for b in range(8):
                pe.wait_ge(L.sem(f"bank_read{b}"), uses[b])
            for t in range(2):
                for q in range(2):
                    pe.wait_ge(*drained(("row", t, q)))

            def item(u):
                pe.wait_ge(moe_sel_ready, u + 1)
                pe.wait_ge(moe_added, u * 4 + 1)
                for q in range(2):
                    for j in range(4):
                        for t in range(2):
                            ins = mm(psum[4 + q][:, j * P:(j + 1) * P], hrow[:, t, (4 * q + j) * P:(4 * q + j + 1) * P],
                                     pick[:, t * P:(t + 1) * P], t == 0, t == 1)
                    ins.then_inc(moe_gathered, 1)
                pe.wait_ge(moe_rows_ready, u * 2 + 1)
                for t in range(2):
                    ins = turn(psum[4][:, t * P:(t + 1) * P], wpick[:, t * P:(t + 1) * P])
                ins.then_inc(moe_spread, 1)
                pe.wait_ge(moe_rows_ready, u * 2 + 2)

                def up(c, kind, b, read_sem, done):
                    s = MOE_SLOT[kind, c]
                    pe.wait_ge(moe_slot_full[s], u * 48 + (MOE_USE[kind, c] + 1) * 16)
                    pe.wait_ge(read_sem, u * EC + max(c, 1))
                    for k in range(DT):
                        ins = mm(psum[b][:, :], hg[:, k, 0:P], kslot(s)[:, k, :], k == 0, k == DT - 1)
                    ins.then_inc(done, 1)

                def gate_up(c):
                    up(c, "w1", c % 2, moe_silu_ready, moe_gate_done)

                def lin_up(c):
                    up(c, "w3", 2 + c % 2, moe_hid_ready, moe_up_done)

                def turn_hidden(c):
                    pe.wait_ge(moe_hid_ready, u * EC + (c + 2))
                    pe.wait_ge(moe_hidT_ready, u * EC + (c + 1))
                    if c == 0:
                        pe.wait_ge(moe_spread_ready, u + 1)
                    for q in range(4):
                        ins = turn(psum[4][:, q * P:(q + 1) * P], hid[:, (c % 2) * 512 + q * P:(c % 2) * 512 + (q + 1) * P])
                    ins.then_inc(moe_turned, 1)

                def down(c):
                    s = MOE_SLOT["w2", c]
                    pe.wait_ge(moe_slot_full[s], u * 48 + (MOE_USE["w2", c] + 1) * 16)
                    pe.wait_ge(moe_hidT_ready, u * EC + (c + 2))
                    if c == 0:
                        pe.wait_ge(moe_y_ready, u + 1)
                    w = slot(s).rearrange("p (q n) -> p q n", q=4)
                    for q in range(4):
                        for n in range(2):
                            ins = mm(psum[6 + n][:, :], mhT[:, (c % 2) * 512 + q * P:(c % 2) * 512 + (q + 1) * P],
                                     w[:, q, n * 512:(n + 1) * 512], c == 0 and q == 0, c == EC - 1 and q == 3)
                    ins.then_inc(moe_down_done, 1)

                gate_up(0)
                lin_up(0)
                for c in range(EC):
                    if c + 1 < EC:
                        gate_up(c + 1)
                    turn_hidden(c)
                    if c + 1 < EC:
                        lin_up(c + 1)
                    down(c)
                pe.wait_ge(moe_y_ready, u + 2)
                for j in range(4):
                    if j == 0:
                        pe.wait_ge(moe_hidT_ready, u * EC + EC + 1)
                    if j >= 2:
                        pe.wait_ge(moe_added, u * 4 + j)
                    for n in range(2):
                        k = 2 * j + n
                        ins = mm(psum[4 + j % 2][:, n * 256:(n + 1) * 256], yrow[:, k * P:(k + 1) * P], spread[:, :])
                    ins.then_inc(moe_scattered, 1)

            pe.sem_inc(moe_turned, 1)
            with pe.Fori(0, EXPERTS) as e:
                item(e)
            pe.wait_ge(ints_ready, 1)
            n_over = pe.value_load(ints[0:1, 0:1], min_val=0, max_val=3)
            with pe.Fori(0, ITEMS - EXPERTS) as o:
                with pe.If(o < n_over):
                    item(o + EXPERTS)

            norm(4, CTX)
            pe.wait_ge(*when("mod", (4, DT - 1)))
            for t in range(2):
                for q in range(2):
                    key = ("out", t, q)
                    o = product(key)
                    for j in range(4):
                        ins = turn(o[:, j * P:(j + 1) * P], hT[:, 4 * q + j, CTX + t * P:CTX + (t + 1) * P])
                    ins.then_inc(*filled(key))

        @block.scalar
        def _(act):
            step, settle = stepper(act, "act_step")

            def fn(o, i, f, **kw):
                return nc.scalar.activation(o, i, f, **kw)

            act.dma_start(table[:, 0:NEARLY], ctab[:, 0:NEARLY]).then_inc(*mark("early_in", 0, 16))
            for l in range(2):
                def vec(r, n, src, last=False):
                    act.dma_start(vrows[r:r + n, l * P:(l + 1) * P], src)\
                        .then_inc(*mark(f"vec_in{l}", l if last else (l, r), 16))

                def by_row(ap):
                    return ap.rearrange("(r p) -> r p", p=P)
                vec(V_ADAB, 48, by_row(A["ada_b"][l]))
                vec(V_N1, 8, by_row(A["norm1_g"][l]))
                vec(V_N2, 8, by_row(A["norm2_g"][l]))
                vec(V_CONV, 30, A["gdn_conv_w"][l].rearrange("a (c p) -> (a c) p", p=P))
                vec(V_RETG, 2, by_row(A["ret_gn_g"][l]))
                vec(V_FIN, 8, by_row(A["final_g"]))
                for p in range(2):
                    act.dma_start(vrows[V_GDNG:V_GDNG + 1, l * P + p * HD:l * P + (p + 1) * HD],
                                  A["gdn_norm_g"][l:l + 1, :]).then_inc(*mark(f"vec_in{l}", (l, "g", p), 16))
                vec(V_C, 8, by_row(A["c"][0]))
                vec(V_CC, 8, by_row(A["c_ctx"]), True)
                for i, src in enumerate((A["ret_decay"][l].rearrange("d h -> (d h)"),
                                         A["gdn_a_log"][l].rearrange("d h -> (d h)"),
                                         A["gdn_dt_bias"][l].rearrange("d h -> (d h)"), A["swa_sink"][l])):
                    act.dma_start(rows[:, 32 * l + 8 * i:32 * l + 8 * i + 8], src.partition_broadcast(P))\
                        .then_inc(*mark("rows_in", (l, i), 16))
            act.dma_start(router[:, :, :], A["router_w"][0].rearrange("(k p) e -> p k e", p=P))\
                .then_inc(*mark("router_in", 0, 16))
            act.wait_ge(*drained(("vec", 0)))
            act.wait_ge(*when("cond_zero", 0))
            fn(condv[:, :, 6:8], VEC[0][:, V_C:V_C + 16].rearrange("p (v k) -> p k v", v=2), ACT.Silu)\
                .then_inc(*mark("cond", 0))
            for k in range(1, DT, 2):
                act.wait_ge(*full(("x", k)))
                fn(xT[:, k, :], bank(("x", k))[:, :], ACT.Copy).then_inc(*read(("x", k)))

            def ada_rows(l, g):
                act.wait_ge(*full(("ada", l, g)))
                if (l, g) != (0, 0):
                    act.wait_ge(*full(("adaT", l if g else 0, (g - 1) % 3)))
                fn(arow[0:8, :], bank(("ada", l, g))[0:8, :], ACT.Copy).then_inc(*read(("ada", l, g)))

            def norm(n, lo=0):
                l, w = divmod(n, 2)
                for k in range(DT):
                    if n == 4:
                        act.wait_ge(*when("final_residual", k))
                    else:
                        act.wait_ge(*drained(("x", k) if n == 0 else ("fy", 1, k) if n == 2 else ("wo", l, k)))
                    fn(squares(n)[:, k, lo:TOK], xT[:, k, lo:TOK], ACT.Square).then_inc(*mark("square", (n, k)))
                act.wait_ge(*full(("ss", n)))
                fn(tmpA[:, lo:TOK], bank(("ss", n))[:, lo:TOK], ACT.Sqrt, bias=eps, scale=1.0 / D)\
                    .then_inc(*read(("ss", n)))
                if n == 4:
                    return
                if n == 0:
                    ada_rows(0, 0)
                act.wait_ge(*when("scales", (l, w)))
                mod = modv[l][:, 24 * w:24 * w + 16, :]
                for k in range(DT):
                    act.wait_ge(*when("normed", (n, k)))
                    if lo == 0:
                        step(fn(hT[:, k, 0:CTX], hT[:, k, 0:CTX], ACT.Identity,
                                bias=mod[:, k, 1:2], scale=mod[:, DT + k, 1:2]))
                    fn(hT[:, k, CTX:TOK], hT[:, k, CTX:TOK], ACT.Identity, bias=mod[:, k, 0:1],
                       scale=mod[:, DT + k, 0:1]).then_inc(*mark("mod", (n, k)))

            def project(l):
                lo = needed(l)
                act.wait_ge(*when("pads", l))
                for c in range(6):
                    key = ("gc", l, c)
                    act.wait_ge(*full(key))
                    s0 = 1 if l and c < 2 else 0
                    fn(cin[:, c, s0:2, 2:258], bank(key)[:, s0 * CTX:TOK].rearrange("p (s n) -> p s n", n=CTX),
                       ACT.Copy).then_inc(*read(key))
                for i in range(2):
                    key = ("z", l, i)
                    act.wait_ge(*full(key))
                    fn(zgate[:, i, lo:TOK], bank(key)[:, lo:TOK], ACT.Silu).then_inc(*read(key))
                for i in range(2):
                    key = ("rg", l, i)
                    act.wait_ge(*full(key))
                    fn(rgate[:, i, lo:TOK], bank(key)[:, lo:TOK], ACT.Silu).then_inc(*read(key))
                act.wait_ge(*when("rows_in", (1, 3)))
                act.wait_ge(*when("gate_args", l))
                r = 32 * l
                step(fn(lgt, rows[:, r:r + 8], ACT.Exp))
                step(fn(ealog, rows[:, r + 8:r + 16], ACT.Exp))
                step(fn(spe, spz, ACT.Abs))
                settle()
                step(fn(spe, spe, ACT.Exp, scale=-1.0))
                for d in range(2):
                    step(fn(beta[:, 16 * d:16 * d + 16].rearrange("p (t h) -> p t h", t=TT),
                            ab.rearrange("p (t c) -> p t c", t=TT)[:, :, 8 + 4 * d:12 + 4 * d], ACT.Exp, scale=-1.0))
                settle()
                fn(spl, spe, ACT.Ln, bias=table[:, CONST["ones"][0]:CONST["ones"][0] + 1])\
                    .then_inc(*mark("gate_exps", l))

            def window(l):
                units = [(h, t) for h in range(8) for t in range(0 if l == 0 else 2, TT)]

                def turned(i):
                    h, t = units[i]
                    key = ("pt", l, h, t)
                    nk = CTX if t < 2 else TOK
                    act.wait_ge(*full(key))
                    fn(pT[:, (i % 2) * 512:(i % 2) * 512 + nk], bank(key)[:, 0:nk], ACT.Copy).then_inc(*read(key))

                def out_tile(m):
                    lo = needed(l)
                    key = ("so", l, m)
                    act.wait_ge(*full(key))
                    fn(oT[:, 4 + m, lo:TOK], bank(key)[:, lo:TOK], ACT.Copy).then_inc(*read(key))

                nu = len(units)
                per = nu // 4
                for i in range(nu + 4):
                    if i < nu:
                        h, t = units[i]
                        nk = CTX if t < 2 else TOK
                        j = i % 2
                        act.wait_ge(*when("scored", (l, i)))
                        if i >= 2:
                            act.wait_ge(*full(("pt", l) + units[i - 2]))
                        step(fn(pr[:, j * 512:j * 512 + nk], sc[:, j * 512:j * 512 + nk], ACT.Exp,
                                bias=nmx[:, i % 4:i % 4 + 1], accum_out=rsm[:, i % 4:i % 4 + 1]))
                        fn(es[:, i % 4:i % 4 + 1], rows[:, 32 * l + 24 + h:32 * l + 25 + h], ACT.Exp,
                           bias=nmx[:, i % 4:i % 4 + 1]).then_inc(*mark("exped", (l, i)))
                    if 0 <= i - 2 < nu:
                        turned(i - 2)
                    if i >= 4 and (i - 4) % per == per - 1:
                        out_tile((i - 4) // per)

            def retention(l):
                lo = needed(l)
                if l == 0:
                    act.wait_ge(*when("table_in", "all"))
                    ada_rows(0, 1)
                for h in range(4):
                    act.wait_ge(*when("decay_args", (l, h)))
                    m = dec(h)
                    step(fn(m[:, 512:1024], m[:, 512:1024], ACT.Exp))
                    step(fn(m[:, 0:512], const("diff"), ACT.Exp, scale=lgt[:, h:h + 1], bias=l256[:, h:h + 1]))
                    fn(tmpB[:, :], const("diff"), ACT.Exp, scale=ln1[:, h:h + 1], bias=l256[:, 4 + h:5 + h])\
                        .then_inc(*mark("decays_exp", (l, h)))
                for i in range(2):
                    key = ("ro", l, i)
                    act.wait_ge(*full(key))
                    if i:
                        act.wait_ge(*when("ret_out", (l, 0)))
                    fn(oraw[:, lo:TOK], bank(key)[:, lo:TOK], ACT.Copy).then_inc(*read(key))
                    act.wait_ge(*drained(("rmean", l, i)))
                    fn(tmpB[:, lo:TOK], oraw[:, lo:TOK], ACT.Square).then_inc(*mark("head_square", ("r", l, i)))
                    act.wait_ge(*full(("rvar", l, i)))
                    fn(tmpA[:, lo:TOK], bank(("rvar", l, i))[:, lo:TOK], ACT.Sqrt, bias=eps).then_inc(*read(("rvar", l, i)))

            def delta_prepare(l):
                for c in range(6):
                    act.wait_ge(*when("conv", (l, c)))
                    fn(acc2[:, c, :], acc2[:, c, :], ACT.Silu).then_inc(*mark("conv_silu", (l, c)))
                act.wait_ge(*when("ret_out", (l, 1)))
                for t in range(TT):
                    key = ("ct", l, t, 0)
                    act.wait_ge(*full(key))
                    if t >= 2:
                        act.wait_ge(*when("squares_summed", (l, t - 2)))
                    fn((tmpA, tmpB)[t % 2][:, :], bank(key)[:, :], ACT.Square).then_inc(*mark("qk_square", (l, t)))
                    fn(tok[:, t, 0:512], bank(key)[:, :], ACT.Copy).then_inc(*read(key))
                act.wait_ge(*when("squares_summed", (l, 3)))
                fn(ssq, ssq, ACT.Sqrt, bias=eps).then_inc(*mark("qk_root", l))
                for t in range(TT):
                    key = ("qkt", l, t)
                    act.wait_ge(*full(key))
                    fn(qkT[:, :, t * P:(t + 1) * P], bank(key)[:, :].rearrange("p (c n) -> p c n", c=4), ACT.Copy)\
                        .then_inc(*read(key))
                act.wait_ge(*when("gate_sums", l))
                step(fn(gex, gex, ACT.Exp))
                fn(kdf, kdf, ACT.Exp).then_inc(*mark("gate_sums_exp", l))

            def delta(l, d):
                def copy_out(key, dst):
                    act.wait_ge(*full(key))
                    fn(dst, bank(key)[:, :], ACT.Copy).then_inc(*read(key))

                for t in range(TT):
                    copy_out(("kq", l, d, t), grp(gKQ, t))
                for t in range(TT):
                    act.wait_ge(*when("decay_masked", (l, d, t)))
                    fn(grp(gP1, t), grp(gP1, t), ACT.Exp).then_inc(*mark("decay_ready", (l, d, t)))
                for t in range(TT):
                    copy_out(("T0", l, d, t), grp(gT, t))
                for v in range(1, 6):
                    for t in range(TT):
                        copy_out(("P1", l, d, v, t), grp(gP1, t))
                for t in range(TT):
                    copy_out(("wu", l, d, t), grp(gWU, t))

            def delta_finish(l):
                lo = needed(l)
                for i in range(2):
                    act.wait_ge(*when("delta_out", l))
                    if i:
                        act.wait_ge(*full(("gvar", l, 0)))
                    fn(tmpB[:, lo:TOK], oT[:, 2 + i, lo:TOK], ACT.Square).then_inc(*mark("head_square", ("g", l, i)))
                    act.wait_ge(*full(("gvar", l, i)))
                    if i:
                        act.wait_ge(*when("delta_normed", (l, 0)))
                    fn(tmpA[:, lo:TOK], bank(("gvar", l, i))[:, lo:TOK], ACT.Sqrt, bias=eps).then_inc(*read(("gvar", l, i)))

            def ffn():
                for f in range(22):
                    act.wait_ge(*full(("fa", f)))
                    if f >= 2:
                        act.wait_ge(*drained(("fb", f - 2)))
                    fn((tmpA, tmpB)[f % 2][:, :], bank(("fa", f))[:, :], ACT.Silu).then_inc(*read(("fa", f)))

            def phase_end(k):
                step(fn(one[:, 0:1], eps, ACT.Copy))
                settle()
                act.sem_inc(phase_done, 1)
                act.wait_ge(phase_done, 4 * k)

            for l in range(2):
                norm(2 * l)
                project(l)
                window(l)
                retention(l)
                delta_prepare(l)
                if l == 0:
                    ada_rows(0, 2)
                phase_end(2 * l + 1)
                delta(l, 0)
                if l == 0:
                    ada_rows(1, 0)
                delta(l, 1)
                if l == 0:
                    ada_rows(1, 1)
                delta_finish(l)
                if l == 0:
                    ada_rows(1, 2)
                phase_end(2 * l + 2)
                norm(2 * l + 1, needed(l))
                if l == 0:
                    ffn()
            act.wait_ge(*when("route_max", 0))
            for t in range(2):
                step(fn(wexp[:, t, :], lgts[:, t, :], ACT.Exp, bias=nm1[:, t:t + 1]))
            settle()
            fn(one[:, 0:1], eps, ACT.Copy).then_inc(*mark("route_exp", 0))
            for t in range(2):
                for q in range(2):
                    key = ("row", t, q)
                    act.wait_ge(*full(key))
                    fn(hrow[:, t, q * 512:(q + 1) * 512], bank(key)[:, :], ACT.Copy).then_inc(*read(key))

            def item(u):
                for q in range(2):
                    act.wait_ge(moe_gathered, u * 2 + (q + 1))
                    fn(hg[:, 4 * q:4 * q + 4, :], psum[4 + q][:, :].rearrange("p (k n) -> p k n", k=4), ACT.Copy)\
                        .then_inc(moe_rows_ready, 1)
                act.wait_ge(moe_spread, u + 1)
                fn(spread, psum[4][:, 0:256], ACT.Copy).then_inc(moe_spread_ready, 1)

                def turned(c):
                    act.wait_ge(moe_turned, u * EC + (c + 2))
                    act.wait_ge(moe_down_done, u * EC + (EC if c < 2 else EC + c - 1))
                    fn(mhT[:, (c % 2) * 512:(c % 2) * 512 + 512], psum[4][:, :], ACT.Copy).then_inc(moe_hidT_ready, 1)

                for c in range(EC):
                    act.wait_ge(moe_gate_done, u * EC + (EC + c + 1))
                    act.wait_ge(moe_hid_ready, u * EC + max(c, 1))
                    fn((tmpA, tmpB)[c % 2][:, :], psum[c % 2][:, :], ACT.Silu).then_inc(moe_silu_ready, 1)
                    if c:
                        turned(c - 1)
                turned(EC - 1)

            act.sem_inc(moe_silu_ready, 1)
            act.sem_inc(moe_hidT_ready, 1)
            with act.Fori(0, EXPERTS) as e:
                item(e)
            act.wait_ge(ints_ready, 1)
            n_over = act.value_load(ints[0:1, 0:1], min_val=0, max_val=3)
            with act.Fori(0, ITEMS - EXPERTS) as o:
                with act.If(o < n_over):
                    item(o + EXPERTS)
            norm(4, CTX)
            for t in range(2):
                for q in range(2):
                    key = ("out", t, q)
                    act.wait_ge(*full(key))
                    fn(osb[:, t * D + q * 512:t * D + (q + 1) * 512], bank(key)[:, :], ACT.Copy)\
                        .then_inc(*read(key))
            for t in range(2):
                act.wait_ge(*drained(("out", t, 1)))
                act.sem_inc(*mark("out_row", t))

        @block.vector
        def _(dve):
            v = nc.vector
            step, settle = stepper(dve, "dve_step")

            def halves(lo):
                return ([(slice(0, CTX), 1)] if lo == 0 else []) + [(slice(CTX, TOK), 0)]

            v.memset(cond[:, :], 0.0).then_inc(*mark("cond_zero", 0))

            def vectors(l):
                dve.wait_ge(*full(("vec", l)))
                v.tensor_copy(VEC[l][:, 0:NVEC], bank(("vec", l))[:, 0:NVEC]).then_inc(*read(("vec", l)))
            vectors(0)
            for k in range(0, DT, 2):
                dve.wait_ge(*full(("x", k)))
                v.tensor_copy(xT[:, k, :], bank(("x", k))[:, :]).then_inc(*read(("x", k)))

            def ada(l, g):
                key = ("adaT", l, g)
                dve.wait_ge(*full(key))
                dve.wait_ge(*drained(("vec", l)))
                ms = slice(16 * g, 16 * g + 16)
                v.tensor_tensor(modv[l][:, ms, :].rearrange("p (j c) v -> p j c v", j=4),
                                bank(key)[:, 0:32].rearrange("p (c j v) -> p j c v", c=4, j=4),
                                VEC[l][:, ms].rearrange("p (j c) -> p j c", j=4).unsqueeze(3)
                                .broadcast_to([P, 4, 4, 2]), ALU.add).then_inc(*read(key))
                dve.wait_ge(*drained(key))
                if g != 1:
                    w = g // 2
                    m = modv[l][:, 24 * w + 8:24 * w + 16, :]
                    gain = VEC[l][:, V_N2 if w else V_N1:][:, 0:8].unsqueeze(2).broadcast_to([P, 8, 2])
                    v.scalar_tensor_tensor(out=m, in0=m, scalar=1.0, in1=gain, op0=ALU.add, op1=ALU.mult)\
                        .then_inc(*mark("scales", (l, w)))

            def norm(n, lo=0):
                dve.wait_ge(*drained(("ss", n)))
                step(v.reciprocal(tmpB[:, lo:TOK], tmpA[:, lo:TOK]))
                if n == 0:
                    ada(0, 0)
                    dve.wait_ge(*full(("x", DT - 1)))
                settle()
                for k in range(DT):
                    if n < 4:
                        v.tensor_tensor(hT[:, k, lo:TOK], xT[:, k, lo:TOK], tmpB[:, lo:TOK], ALU.mult)\
                            .then_inc(*mark("normed", (n, k)))
                    else:
                        v.scalar_tensor_tensor(
                            out=hT[:, k, lo:TOK], in0=xT[:, k, lo:TOK], scalar=VEC[0][:, V_FIN + k:V_FIN + k + 1],
                            in1=tmpB[:, lo:TOK], op0=ALU.mult, op1=ALU.mult).then_inc(*mark("mod", (n, k)))

            def rope(key, dst, name, mkey, lo=0):
                dve.wait_ge(*full(key))
                b = bank(key)
                if lo == 0:
                    step(v.tensor_copy(dst[:, 0:CTX], b[:, 0:CTX]))
                step(v.tensor_tensor(tmpA[:, 0:LAT], b[:, CTX:TOK], const("cos"), ALU.mult))
                for q in range(4):
                    o = slice(32 * q, 32 * q + 32)
                    i = slice(32 * (q ^ 1), 32 * (q ^ 1) + 32)
                    ins = v.tensor_tensor(tmpB[o, 0:LAT], b[i, CTX:TOK], const("sin")[o, :], ALU.mult)
                    if q < 3:
                        step(ins)
                ins.then_inc(*read(key))
                dve.wait_ge(*drained(key))
                v.tensor_tensor(dst[:, CTX:TOK], tmpA[:, 0:LAT], tmpB[:, 0:LAT], ALU.add).then_inc(*mark(name, mkey))
                dve.wait_ge(*when(name, mkey))

            def project(l):
                rope(("sk", l), krot, "sk_rot", l)
                for g in range(2):
                    for p in range(2):
                        ins = v.tensor_copy(skd[p * HD:(p + 1) * HD, g, :], krot[g * HD:(g + 1) * HD, :])
                        if (g, p) != (1, 1):
                            step(ins)
                ins.then_inc(*mark("sk_ready", l))
                for t in range(TT):
                    key = ("vab", l, t)
                    dve.wait_ge(*full(key))
                    step(v.tensor_copy(sv[:, t, :], bank(key)[:, 0:P]))
                    v.tensor_copy(ab[:, 16 * t:16 * t + 16], bank(key)[:, P:P + 16]).then_inc(*read(key))
                dve.wait_ge(*when("rows_in", (1, 3)))
                dve.wait_ge(*drained(("vab", l, 3)))
                for d in range(2):
                    ins = (v.tensor_tensor(
                        spz[:, 16 * d:16 * d + 16].rearrange("p (t h) -> p t h", t=TT),
                        ab.rearrange("p (t c) -> p t c", t=TT)[:, :, 4 * d:4 * d + 4],
                        rows[:, 32 * l + 16 + 4 * d:32 * l + 20 + 4 * d].unsqueeze(1).broadcast_to([P, TT, 4]), ALU.add))
                    ins.then_inc(*mark("gate_args", l if d else (l, 0)))
                for c in range(4):
                    rope(("sq", l, c), sq[:, c, :], "sq_ready", (l, c), needed(l))
                for c in range(4):
                    rope(("rqk", l, c), rqk[:, c, :], "rqk_ready", (l, c), needed(l) if c < 2 else 0)
                for t in range(TT):
                    key = ("rv", l, t)
                    dve.wait_ge(*full(key))
                    v.tensor_copy(rv[:, t, :], bank(key)[:, 0:256]).then_inc(*read(key))
                dve.wait_ge(*when("gate_exps", l))
                step(v.scalar_tensor_tensor(out=gl, in0=spz, scalar=0.0, in1=spl, op0=ALU.max, op1=ALU.add))
                step(v.tensor_scalar(beta, beta, 1.0, None, ALU.add))
                step(v.tensor_scalar(lgt, lgt, -1.0, None, ALU.mult))
                settle()
                step(v.reciprocal(beta, beta))
                step(v.tensor_tensor(lsum, lgt[:, 0:4], lgt[:, 4:8], ALU.add))
                step(v.tensor_scalar(l256, lgt, 256.0, None, ALU.mult))
                step(v.tensor_scalar(ln1, lgt[:, 4:8], -1.0, None, ALU.mult))
                for d in range(2):
                    g = gl[:, 16 * d:16 * d + 16].rearrange("p (t h) -> p t h", t=TT)
                    ins = v.scalar_tensor_tensor(
                        out=g, in0=g, scalar=-1.0, in1=ealog[:, 4 * d:4 * d + 4].unsqueeze(1).broadcast_to([P, TT, 4]),
                        op0=ALU.mult, op1=ALU.mult)
                    ins.then_inc(*mark("log_decay", l if d else (l, 0)))
                settle()

            def window(l):
                units = [(h, t) for h in range(8) for t in range(0 if l == 0 else 2, TT)]

                def score(i):
                    h, t = units[i]
                    key = ("sc", l, h, t)
                    nk = CTX if t < 2 else TOK
                    c = slice(i % 4, i % 4 + 1)
                    o = sc[:, (i % 2) * 512:(i % 2) * 512 + nk]
                    dve.wait_ge(*full(key))
                    if i >= 2:
                        dve.wait_ge(*when("exped", (l, i - 2)))
                    ins = v.tensor_scalar(o[:, 0:CTX], bank(key)[:, 0:CTX], SCALE, None, ALU.mult)
                    if t >= 2:
                        step(ins)
                        ins = v.scalar_tensor_tensor(out=o[:, CTX:TOK], in0=bank(key)[:, CTX:TOK], scalar=SCALE,
                                                     in1=const("band")[:, (t - 2) * 256:(t - 1) * 256],
                                                     op0=ALU.mult, op1=ALU.add)
                    ins.then_inc(*read(key))
                    dve.wait_ge(*drained(key))
                    step(v.reduce_max(mx[:, c], o, AX_X))
                    settle()
                    v.tensor_scalar(nmx[:, c], mx[:, c], rows[:, 32 * l + 24 + h:32 * l + 25 + h], -1.0,
                                    ALU.max, ALU.mult).then_inc(*mark("scored", (l, i)))

                def normalize(i):
                    h, t = units[i]
                    nk = CTX if t < 2 else TOK
                    c = slice(i % 4, i % 4 + 1)
                    dve.wait_ge(*when("exped", (l, i)))
                    step(v.tensor_tensor(den[:, c], rsm[:, c], es[:, c], ALU.add))
                    settle()
                    step(v.reciprocal(den[:, c], den[:, c]))
                    settle()
                    o = pr[:, (i % 2) * 512:(i % 2) * 512 + nk]
                    v.tensor_scalar(o, o, den[:, c], None, ALU.mult).then_inc(*mark("probs", (l,) + units[i]))

                for i in range(len(units) + 1):
                    if i < len(units):
                        score(i)
                    if i:
                        normalize(i - 1)

            def retention(l):
                def args(h):
                    m = dec(h)
                    step(v.tensor_scalar(tmpA[:, :], const("diff"), lsum[:, h:h + 1], 0.0, ALU.mult, ALU.min))
                    settle()
                    v.scalar_tensor_tensor(out=m[:, 512:1024], in0=const("diff"), scalar=ln1[:, h:h + 1],
                                           in1=tmpA[:, :], op0=ALU.mult, op1=ALU.add)\
                        .then_inc(*mark("decay_args", (l, h)))
                args(0)
                for h in range(4):
                    m = dec(h)
                    dve.wait_ge(*when("decays_exp", (l, h)))
                    step(v.tensor_tensor(m[:, 512:1024], m[:, 512:1024], const("diag2"), ALU.mult))
                    step(v.tensor_tensor(m[:, 0:512], m[:, 0:512], tmpB[:, :], ALU.add))
                    settle()
                    if h < 3:
                        args(h + 1)
                    if h == 2:
                        dve.wait_ge(*when("ret_values", (l, 0)))
                    if h == 3:
                        dve.wait_ge(*full(("ro", l, 0)))
                    for part in range(2 if l else 3):
                        key = ("rs", l, h, part)
                        dve.wait_ge(*full(key))
                        v.scalar_tensor_tensor(out=smk(h, part), in0=bank(key)[:, :], scalar=SCALE,
                                               in1=m[:, 0:512] if part == 0 else m[:, 512:1024],
                                               op0=ALU.mult, op1=ALU.mult).then_inc(*read(key))
                    dve.wait_ge(*drained(("rs", l, h, 1 if l else 2)))
                    if (l, h) == (0, 0):
                        ada(0, 1)
                for i in range(2):
                    dve.wait_ge(*drained(("ro", l, i)))
                    dve.wait_ge(*full(("rmean", l, i)))
                    cols = slice(needed(l), TOK)
                    v.tensor_tensor(oraw[:, cols], oraw[:, cols], bank(("rmean", l, i))[:, cols], ALU.subtract)\
                        .then_inc(*read(("rmean", l, i)))
                    dve.wait_ge(*drained(("rvar", l, i)))
                    step(v.reciprocal(tmpA[:, cols], tmpA[:, cols]))
                    settle()
                    step(v.scalar_tensor_tensor(
                        out=oraw[:, cols], in0=oraw[:, cols], scalar=VEC[l][:, V_RETG + i:V_RETG + i + 1],
                        in1=tmpA[:, cols], op0=ALU.mult, op1=ALU.mult))
                    settle()
                    dve.wait_ge(*drained(("rg", l, i)))
                    v.tensor_tensor(oT[:, i, cols], oraw[:, cols], rgate[:, i, cols], ALU.mult).then_inc(*mark("ret_out", (l, i)))

            def delta_prepare(l):
                for t in range(TT):
                    key = ("ct", l, t, 1)
                    dve.wait_ge(*full(key))
                    v.tensor_copy(tok[:, t, 512:768], bank(key)[:, 0:256]).then_inc(*read(key))
                    dve.wait_ge(*when("qk_square", (l, t)))
                    v.reduce_sum(ssq[:, 8 * t:8 * t + 8],
                                 (tmpA, tmpB)[t % 2][:, :].rearrange("p (h n) -> p h n", n=HD), AX_X)\
                        .then_inc(*mark("squares_summed", (l, t)))
                dve.wait_ge(*when("qk_root", l))
                step(v.reciprocal(ssq, ssq))
                settle()
                qs = ssq.rearrange("p (t h) -> p t h", t=TT)[:, :, 0:4]
                step(v.tensor_scalar(qs, qs, SCALE, None, ALU.mult))
                settle()
                for t in range(TT):
                    dve.wait_ge(*drained(("ct", l, t, 0)))
                    x = tok[:, t, 0:512].rearrange("p (h n) -> p h n", n=HD)
                    v.tensor_tensor(x, x, ssq[:, 8 * t:8 * t + 8].unsqueeze(2).broadcast_to([P, 8, HD]), ALU.mult)\
                        .then_inc(*mark("qk_unit", (l, t)))
                key = ("gsum", l)
                dve.wait_ge(*full(key))
                v.tensor_copy(gex, bank(key)[:, 0:128]).then_inc(*read(key))
                dve.wait_ge(*drained(key))
                step(v.tensor_copy(gcs, gex[:, 0:32]))
                v.tensor_tensor(kdf, gex[:, 32:64], gex[:, 0:32], ALU.subtract).then_inc(*mark("gate_sums", l))
                dve.wait_ge(*when("gate_sums_exp", l))
                step(v.tensor_tensor(bgf, beta, gex[:, 0:32], ALU.mult))
                for p in range(2):
                    for c in range(2):
                        hp = slice(p * HD, (p + 1) * HD)
                        step(v.tensor_copy(
                            sdec.rearrange("p (g c i) -> p g c i", c=2, i=2)[hp, :, c, :],
                            gex[:, 64 + 32 * c:96 + 32 * c].rearrange("p (g i q) -> p g i q", i=2, q=2)[hp, :, :, p]))
                settle()
                v.tensor_copy(mx[:, 1:2], gcs[:, 0:1]).then_inc(*mark("decays", l))

            def delta(l, d):
                for t in range(TT):
                    key = ("dec", l, d, t)
                    at = 16 * d + 4 * t
                    dve.wait_ge(*full(key))
                    v.tensor_tensor(grp(gP1, t).rearrange("p (h n) -> p h n", h=4),
                                    bank(key)[:, :].rearrange("p (h n) -> p h n", h=4),
                                    gcs[:, at:at + 4].unsqueeze(2).broadcast_to([P, 4, P]), ALU.subtract)\
                        .then_inc(*read(key))
                for t in range(TT):
                    dve.wait_ge(*when("decay_ready", (l, d, t)))
                    for p in range(2):
                        key = ("kkqk", l, d, t, p)
                        dve.wait_ge(*full(key))
                        for j, dst in enumerate((gAT,) if l and t < 2 else (gAT, gAtt)):
                            def heads(x):
                                return grp(x, t).rearrange("p (i q n) -> p i q n", i=2, q=2)[:, :, p, :]
                            ins = v.tensor_tensor(heads(dst), bank(key)[:, j * 256:(j + 1) * 256].rearrange(
                                "p (i n) -> p i n", i=2), heads(gP1), ALU.mult)
                            if j == 0 and not (l and t < 2):
                                step(ins)
                        ins.then_inc(*read(key))
                for t in range(TT):
                    dve.wait_ge(*when("NT", (l, d, 0, t)))
                    v.tensor_tensor(grp(gTT, t).rearrange("p (h n) -> p h n", h=4),
                                    ident.unsqueeze(1).broadcast_to([P, 4, P]),
                                    grp(gNT, t).rearrange("p (h n) -> p h n", h=4), ALU.subtract)\
                        .then_inc(*mark("TT_first", (l, d, t)))
                for lv in range(1, 6):
                    for t in range(TT):
                        for name, dst in (("TP", gT), ("TTP", gTT)):
                            if name == "TP" and lv == 5:
                                continue
                            key = (name, l, d, lv, t)
                            dve.wait_ge(*full(key))
                            if lv == 1:
                                dve.wait_ge(*(drained(("T0", l, d, t)) if name == "TP" else when("TT_first", (l, d, t))))
                            else:
                                dve.wait_ge(*drained((name, l, d, lv - 1, t)))
                            v.tensor_tensor(grp(dst, t), grp(dst, t), bank(key)[:, :], ALU.subtract)\
                                .then_inc(*read(key))
                if d:
                    dve.wait_ge(*drained(("su", l, 0, 7)))
                step(v.memset(vnew, 0.0))
                v.memset(state[:, :, :], 0.0).then_inc(*mark("state_zero", (l, d)))
                for n, (t, c) in enumerate(steps(d)):
                    cs = slice(c * CHUNK, (c + 1) * CHUNK)
                    dve.wait_ge(*full(("vn", l, d, n)))
                    v.tensor_tensor(vnew[cs, :], grp(gWU, t)[cs, 256:512], bank(("vn", l, d, n))[cs, 0:256],
                                    ALU.subtract).then_inc(*read(("vn", l, d, n)))
                    key = ("su", l, d, n)
                    dve.wait_ge(*full(key))
                    dve.wait_ge(*(drained(("su", l, d, n - 1)) if n else when("state_zero", (l, d))))
                    for i in range(2):
                        at = ((d * 4 + t) * 2 + c) * 2 + i
                        for p in range(2):
                            hp = slice(p * HD, (p + 1) * HD)
                            x = state[hp, i, p * HD:(p + 1) * HD]
                            ins = v.scalar_tensor_tensor(out=x, in0=x, scalar=sdec[hp, at:at + 1],
                                                         in1=bank(key)[hp, i * HD:(i + 1) * HD],
                                                         op0=ALU.mult, op1=ALU.add)
                            if (i, p) != (1, 1):
                                step(ins)
                    ins.then_inc(*read(key))
                    if (l, d, n) == (0, 1, 4):
                        ada(1, 1)
                    if n % 2 and (l == 0 or t >= 2):
                        key = ("go", l, d, t)
                        dve.wait_ge(*full(key))
                        o = oT[:, 2:4, t * P:(t + 1) * P]
                        b = bank(key)[:, 0:256].rearrange("p (i n) -> p i n", i=2)
                        if d == 0:
                            v.tensor_copy(o, b).then_inc(*read(key))
                        else:
                            dve.wait_ge(*drained(("go", l, 0, t)))
                            v.tensor_tensor(o, o, b, ALU.add).then_inc(*read(key))
                settle()

            def delta_finish(l):
                lo = needed(l)
                for t in range(2 if l else 0, TT):
                    dve.wait_ge(*drained(("go", l, 1, t)))
                v.tensor_copy(mx[:, 2:3], gcs[:, 0:1]).then_inc(*mark("delta_out", l))
                for i in range(2):
                    o = oT[:, 2 + i, lo:TOK]
                    dve.wait_ge(*drained(("gvar", l, i)))
                    step(v.reciprocal(tmpA[:, lo:TOK], tmpA[:, lo:TOK]))
                    settle()
                    v.scalar_tensor_tensor(out=o, in0=o, scalar=VEC[l][:, V_GDNG:V_GDNG + 1], in1=tmpA[:, lo:TOK],
                                           op0=ALU.mult, op1=ALU.mult).then_inc(*mark("delta_normed", (l, i)))
                    dve.wait_ge(*when("delta_normed", (l, i)))
                    dve.wait_ge(*drained(("z", l, i)))
                    v.tensor_tensor(o, o, zgate[:, i, lo:TOK], ALU.mult).then_inc(*mark("mixed", l if i else (l, 0)))

            def residual(l, key, k, gate, lo):
                dve.wait_ge(*full(key))
                for cols, s in halves(lo):
                    ins = v.scalar_tensor_tensor(out=xT[:, k, cols], in0=bank(key)[:, cols],
                                                 scalar=modv[l][:, gate + k, s:s + 1], in1=xT[:, k, cols],
                                                 op0=ALU.mult, op1=ALU.add)
                    if s:
                        step(ins)
                ins.then_inc(*read(key))

            def ffn():
                for half, (f0, f1) in enumerate(FF_PARTS):
                    for f in range(f0, f1):
                        dve.wait_ge(*full(("fb", f)))
                        dve.wait_ge(*drained(("fa", f)))
                        v.tensor_tensor(hidT(f - f0), (tmpA, tmpB)[f % 2][:, :], bank(("fb", f))[:, :], ALU.mult)\
                            .then_inc(*read(("fb", f)))
                    for k in range(DT):
                        if half:
                            dve.wait_ge(*drained(("fy", 0, k)))
                        residual(0, ("fy", half, k), k, 40, 0)

            def phase_end(k):
                step(v.tensor_copy(mx[:, 0:1], gcs[:, 0:1]))
                settle()
                dve.sem_inc(phase_done, 1)
                dve.wait_ge(phase_done, 4 * k)

            for l in range(2):
                norm(2 * l)
                if l == 0:
                    dve.wait_ge(*when("table_in", "all"))
                    vectors(1)
                project(l)
                window(l)
                retention(l)
                delta_prepare(l)
                phase_end(2 * l + 1)
                if l == 0:
                    ada(0, 2)
                delta(l, 0)
                if l == 0:
                    ada(1, 0)
                delta(l, 1)
                delta_finish(l)
                if l == 0:
                    ada(1, 2)
                phase_end(2 * l + 2)
                for k in range(DT):
                    residual(l, ("wo", l, k), k, 16, needed(l))
                norm(2 * l + 1, needed(l))
                if l == 0:
                    ffn()

            key = "logits"
            dve.wait_ge(*full(key))
            v.tensor_copy(lgts, bank(key)[:, 0:16].rearrange("p (t e) -> p t e", t=2)).then_inc(*read(key))
            dve.wait_ge(*drained(key))
            ex = const("expert")
            step(v.tensor_tensor(less, ex.unsqueeze(1).broadcast_to([P, 8, 8]),
                                 ex.unsqueeze(2).broadcast_to([P, 8, 8]), ALU.is_lt))
            step(v.reduce_max(nm1, lgts, AX_X))
            settle()
            v.tensor_scalar(nm1, nm1, -1.0, None, ALU.mult).then_inc(*mark("route_max", 0))
            for t in range(2):
                a = lgts[:, t, :].unsqueeze(1).broadcast_to([P, 8, 8])
                b = lgts[:, t, :].unsqueeze(2).broadcast_to([P, 8, 8])
                step(v.tensor_tensor(cmp1, a, b, ALU.is_gt))
                step(v.tensor_tensor(cmp2, a, b, ALU.is_equal))
                settle()
                step(v.tensor_tensor(cmp2, cmp2, less, ALU.mult))
                settle()
                step(v.tensor_tensor(cmp1, cmp1, cmp2, ALU.add))
                settle()
                step(v.reduce_sum(rank, cmp1, AX_X))
                settle()
                ins = v.tensor_scalar(sel[:, t, :], rank, 2.0, None, ALU.is_lt)
                ins.then_inc(*mark("chosen", 0 if t else ("first", 0)))
            dve.wait_ge(*when("chosen", 0))
            dve.wait_ge(*when("route_exp", 0))
            step(v.tensor_tensor(wexp, wexp, sel, ALU.mult))
            settle()
            step(v.reduce_sum(wsum, wexp, AX_X))
            settle()
            step(v.reciprocal(wsum, wsum))
            settle()
            step(v.tensor_tensor(wexp, wexp, wsum.unsqueeze(2).broadcast_to([P, 2, 8]), ALU.mult))
            key = "places"
            dve.wait_ge(*full(key))
            v.tensor_copy(place, bank(key)[:, 0:24]).then_inc(*read(key))
            dve.wait_ge(*drained(key))
            settle()
            pos = place[:, 0:16].rearrange("p (t e) -> p t e", t=2)
            step(v.tensor_scalar(over, place[:, 16:24], float(P), None, ALU.is_gt))
            settle()
            step(v.tensor_tensor(cmp1, less, over.unsqueeze(1).broadcast_to([P, 8, 8]), ALU.mult))
            step(v.reduce_sum(intf[:, 0:1], over, AX_X))
            step(v.memset(items[:, :, :, :], 0.0))
            step(v.memset(yacc[:, :, :], 0.0))
            settle()
            step(v.reduce_sum(rank, cmp1, AX_X))
            for i, src in enumerate((pos, sel, wexp)):
                step(v.tensor_copy(items[:, i, 0:8, :], src.rearrange("p t e -> p e t")))
            settle()
            for o in range(3):
                step(v.scalar_tensor_tensor(out=cmp2[:, 0, :], in0=rank, scalar=float(o), in1=over,
                                            op0=ALU.is_equal, op1=ALU.mult))
                settle()
                step(v.tensor_tensor(cmp2[:, 1, :], cmp2[:, 0, :], ex, ALU.mult))
                for i, src in enumerate((pos, sel, wexp)):
                    step(v.tensor_tensor(cmp1[:, 2 * i:2 * i + 2, :], src,
                                         cmp2[:, 0, :].unsqueeze(1).broadcast_to([P, 2, 8]), ALU.mult))
                settle()
                step(v.reduce_sum(intf[:, 1 + o:2 + o], cmp2[:, 1, :], AX_X))
                for i in range(3):
                    step(v.reduce_sum(items[:, i, 8 + o, :], cmp1[:, 2 * i:2 * i + 2, :], AX_X))
                settle()
                step(v.tensor_scalar(items[:, 0, 8 + o, :], items[:, 0, 8 + o, :], float(P), None, ALU.subtract))
                settle()
            v.tensor_copy(ints[:, 0:4], intf).then_inc(ints_ready, 1)

            for i, dst in ((1, pick), (2, wpick)):
                for t in range(2):
                    v.tensor_scalar(dst[:, t * P:(t + 1) * P], const("iota"), itemf[:, t:t + 1],
                                    itemf[:, 24 * i + t:24 * i + t + 1], ALU.is_equal, ALU.mult)\
                        .then_inc(moe_picks, 1)
            dve.wait_ge(moe_picks, 4)
            dve.sem_inc(moe_sel_ready, 1)
            for counted in (moe_hid_ready, moe_y_ready, moe_added):
                dve.sem_inc(counted, 1)

            def item(u):
                for c in range(EC):
                    dve.wait_ge(moe_up_done, u * EC + (EC + c + 1))
                    dve.wait_ge(moe_silu_ready, u * EC + (c + 2))
                    dve.wait_ge(moe_turned, u * EC + max(c, 1))
                    v.tensor_tensor(hid[:, (c % 2) * 512:(c % 2) * 512 + 512], (tmpA, tmpB)[c % 2][:, :],
                                    psum[2 + c % 2][:, :], ALU.mult).then_inc(moe_hid_ready, 1)
                    if c == 2:
                        dve.wait_ge(moe_spread, u + 1)
                        for i, dst in ((1, pick), (2, wpick)):
                            for t in range(2):
                                v.tensor_scalar(dst[:, t * P:(t + 1) * P], const("iota"),
                                                itemf[:, bass.ds(u * 2 + (t + 2), 1)],
                                                itemf[:, bass.ds(u * 2 + (t + 2 + 24 * i), 1)],
                                                ALU.is_equal, ALU.mult).then_inc(moe_picks, 1)
                        dve.wait_ge(moe_picks, u * 4 + 8)
                        dve.sem_inc(moe_sel_ready, 1)
                dve.wait_ge(moe_down_done, u * EC + 2 * EC)
                v.tensor_copy(yrow[:, 0:512], psum[6][:, :]).then_inc(moe_y_half, 1)
                dve.wait_ge(moe_y_half, u + 1)
                v.tensor_copy(yrow[:, 512:1024], psum[7][:, :]).then_inc(moe_y_ready, 1)
                for j in range(4):
                    dve.wait_ge(moe_scattered, u * 4 + (j + 1))
                    if j == 0:
                        dve.wait_ge(moe_added, u * 4 + 1)
                    y = yacc[:, 2 * j:2 * j + 2, :]
                    v.tensor_tensor(y, y, psum[4 + j % 2][:, :].rearrange("p (k n) -> p k n", k=2), ALU.add)\
                        .then_inc(moe_added, 1)

            with dve.Fori(0, EXPERTS) as e:
                item(e)
            n_over = dve.value_load(ints[0:1, 0:1], min_val=0, max_val=3)
            with dve.Fori(0, ITEMS - EXPERTS) as o:
                with dve.If(o < n_over):
                    item(o + EXPERTS)
            settle()
            step(v.memset(wsum, 0.0))
            settle()
            for k in range(DT):
                v.scalar_tensor_tensor(out=xT[:, k, CTX:TOK], in0=yacc[:, k, :], scalar=modv[1][:, 40 + k, 0:1],
                                       in1=xT[:, k, CTX:TOK], op0=ALU.mult, op1=ALU.add)\
                    .then_inc(*mark("final_residual", k))
            norm(4, CTX)

        @block.gpsimd
        def _(pool):
            g = nc.gpsimd
            step, settle = stepper(pool, "pool_step")

            def conv(l):
                pool.wait_ge(*(drained(("fy", 1, DT - 1)) if l else full(("ss", 0))))
                if l:
                    step(g.memset(cin[:, 0:2, 0, :], 0.0))
                    settle()
                step(g.memset(cin[:, :, :, 0:2], 0.0))
                g.memset(cin[:, :, :, 258:260], 0.0).then_inc(*mark("pads", l))
                pool.wait_ge(*drained(("vec", l)))
                pool.wait_ge(*when("pads", l))
                for c in range(6):
                    pool.wait_ge(*drained(("gc", l, c)))
                    for k in range(5):
                        w = VEC[l][:, V_CONV + 6 * k + c:V_CONV + 6 * k + c + 1]
                        x = cin[:, c, :, k:k + 256]
                        tap = taps[:, (k % 2) * 512:(k % 2) * 512 + 512].rearrange("p (s n) -> p s n", s=2)
                        if k == 0:
                            step(g.tensor_scalar(acc[:, c], x, w, None, ALU.mult))
                            continue
                        step(g.tensor_scalar(tap, x, w, None, ALU.mult))
                        settle()
                        ins = g.tensor_tensor(acc[:, c], acc[:, c], tap, ALU.add)
                        if k < 4:
                            step(ins)
                    ins.then_inc(*mark("conv", (l, c)))

            def phase_end(k):
                step(g.memset(poolone[:, :], 0.0))
                settle()
                pool.sem_inc(phase_done, 1)
                pool.wait_ge(phase_done, 4 * k)

            def scaled(dst, src, f, at):
                return g.tensor_tensor(dst.rearrange("p (h n) -> p h n", h=4), src.rearrange("p (h n) -> p h n", h=4),
                                       f[:, at:at + 4].unsqueeze(2).broadcast_to([P, 4, HD]), ALU.mult)

            def delta(l, d):
                if d == 0:
                    pool.wait_ge(*when("decays", l))
                    for t in range(TT):
                        pool.wait_ge(*when("qk_unit", (l, t)))
                        pool.wait_ge(*drained(("ct", l, t, 1)))
                for t in range(TT):
                    at = 16 * d + 4 * t
                    if t >= 2:
                        pool.wait_ge(*full(("kq", l, d, t - 2)))
                    elif d:
                        pool.wait_ge(*full(("kq", l, 0, t + 2)))
                    if d:
                        pool.wait_ge(*full(("wu", l, 0, t)))
                    q, k, vv = tok[:, t, 0:256], tok[:, t, 256:512], tok[:, t, 512:768]
                    step(scaled(kbuf(t)[:, 0:256], k, beta, at))
                    step(scaled(kbuf(t)[:, 256:512], q, gex, at))
                    step(scaled(grp(gRW, t, 256), k, bgf, at))
                    scaled(grp(gRU, t, 256), vv, beta, at).then_inc(*mark("kbqd", (l, d, t)))
                if d:
                    pool.wait_ge(*full(("su", l, 0, 7)))
                for t in range(TT):
                    pool.wait_ge(*drained(("dec", l, d, t)))
                    x = grp(gP1, t).rearrange("p (h n) -> p h n", h=4)
                    g.tensor_tensor(x, x, const(f"neg{d}").unsqueeze(1).broadcast_to([P, 4, P]), ALU.add)\
                        .then_inc(*mark("decay_masked", (l, d, t)))
                for t in range(TT):
                    scaled(grp(gKD, t, 256), tok[:, t, 256:512], kdf, 16 * d + 4 * t)\
                        .then_inc(*mark("kd", (l, d, t)))
                for lv in range(6):
                    for t in range(TT):
                        if lv == 0:
                            for p in range(2):
                                pool.wait_ge(*drained(("kkqk", l, d, t, p)))
                        elif lv == 1:
                            pool.wait_ge(*when("TT_first", (l, d, t)))
                        else:
                            pool.wait_ge(*full(("P1", l, d, lv - 1, t)))
                        g.tensor_tensor(grp(gNT, t).rearrange("p (h n) -> p h n", h=4),
                                        grp(gAT, t).rearrange("p (h n) -> p h n", h=4),
                                        const(f"level{d}", lv).unsqueeze(1).broadcast_to([P, 4, P]), ALU.mult)\
                            .then_inc(*mark("NT", (l, d, lv, t)))

            pool.wait_ge(*when("table_in", "all"))
            for l in range(2):
                conv(l)
                phase_end(2 * l + 1)
                delta(l, 0)
                delta(l, 1)
                phase_end(2 * l + 2)
        assert len(was_read) == sum(uses)
        return L


_INS = ['x', 'c', 'ctx', 'c_ctx', 'ada_w', 'ada_b', 'norm1_g', 'w_in', 'ret_decay', 'ret_gn_g', 'gdn_conv_w',
        'gdn_a_log', 'gdn_dt_bias', 'gdn_norm_g', 'swa_sink', 'w_out', 'norm2_g', 'ffn_w1', 'ffn_w3', 'ffn_w2',
        'router_w', 'moe_w1', 'moe_w3', 'moe_w2', 'final_g']


def kernel(**inputs):
    import numpy as _np
    import concourse.bacc as _bacc
    from concourse import mybir as _mybir
    from concourse.bass_utils import run_bass_kernel_spmd as _run

    arrays = {f"in_{n}_dram": _np.ascontiguousarray(inputs[n]) for n in _INS}
    arrays["const_table"] = const_table()
    known = None
    for _ in range(2):
        nc = _bacc.Bacc("TRN2", target_bir_lowering=False, num_devices=1)
        A = {n: nc.dram_tensor(f"in_{n}_dram", inputs[n].shape, _mybir.dt.float32, kind="ExternalInput").ap()
             for n in _INS}
        table = nc.dram_tensor("const_table", (P, NCONST), _mybir.dt.float32, kind="ExternalInput").ap()
        out = nc.dram_tensor("out_0_dram", (1, LAT, D), _mybir.dt.float32, kind="ExternalOutput").ap()
        known = build(nc, A, out, table, known)
    r = _run(nc, [arrays], core_ids=[0])
    return r.results[0]["out_0_dram"]
```

```python
from contextlib import ExitStack

import numpy as np

import concourse.bass as bass
from concourse import mybir

F32 = mybir.dt.float32
I32 = mybir.dt.int32
ALU = mybir.AluOpType
ACT = mybir.ActivationFunctionType
AX_X = mybir.AxisListType.X

P = 128
D = 1024
DT = D // P
CTX = 256
LAT = 256
TOK = CTX + LAT
TT = TOK // P
HD = 64
SCALE = HD ** -0.5
EPS = 1e-6
CHUNK = 64
IN_COLS = 2832
FF = 2816
EXPERTS = 8
EFF = 3584
EC = EFF // 512
ITEMS = EXPERTS + 3
NEG = -1e30
SLOT = 4096
NSLOT = 7
LEVELS = (1, 2, 4, 8, 16, 32)

CONST = {}
_at = 0
for _name, _n in (("ident", P), ("ones", P), ("eps", 1), ("expert", 8), ("head_mean", P), ("incl0", P), ("incl1", P), ("half0", P),
                  ("half1", P), ("neg0", P), ("neg1", P), ("before", P), ("iota", P), ("same", P),
                  ("level0", 6 * P), ("level1", 6 * P), ("diff", 512), ("diag2", 512),
                  ("band", 512), ("cos", LAT), ("sin", LAT)):
    CONST[_name] = (_at, _n)
    _at += _n
NCONST = _at
NEARLY = CONST["head_mean"][0]

FF_PARTS = ((0, 12), (12, 22))


def steps(d):
    return [(t, c) for t in (0, 1, 2, 3) for c in (0, 1)] if d == 0 else \
        [(t, c) for t in (1, 0, 3, 2) for c in (1, 0)]


V_ADAB, V_N1, V_N2, V_CONV, V_RETG, V_FIN, V_GDNG, V_C, V_CC, NVEC = 0, 48, 56, 64, 94, 96, 104, 105, 113, 121


def const_table():
    t = np.zeros((P, NCONST), np.float32)

    def put(name, a):
        o, n = CONST[name]
        t[:, o:o + n] = np.asarray(a, np.float32).reshape(P, n)

    r = np.arange(P)
    row, col = r[:, None], r[None, :]
    same = row // CHUNK == col // CHUNK
    put("ident", np.eye(P))
    put("ones", np.ones((P, P)))
    put("head_mean", (row // HD == col // HD) / HD)
    put("incl0", same & (row <= col))
    put("incl1", same & (row >= col))
    put("half0", np.broadcast_to(row < CHUNK, (P, P)))
    put("half1", np.broadcast_to(row >= CHUNK, (P, P)))
    put("same", same)
    put("neg0", np.where(same & (col >= row), 0.0, NEG))
    put("neg1", np.where(same & (col <= row), 0.0, NEG))
    put("before", row < col)
    put("iota", np.broadcast_to(col, (P, P)))
    lv = [(col // b == row // b + 1) & ((col // b) % 2 == 1) for b in LEVELS]
    put("level0", np.stack(lv, 1))
    put("level1", np.stack([m.T for m in lv], 1))
    j = np.arange(256).reshape(2, P).T[:, :, None]
    i = np.arange(256)[None, None, :]
    put("diff", i - j)
    put("diag2", 1.0 + (i == j))
    put("band", np.where(np.abs(i - j) <= 128, 0.0, NEG))
    n = np.arange(LAT, dtype=np.float32)
    inv = np.float32(10000.0) ** (-np.arange(16, dtype=np.float32) / np.float32(16))
    f = r % 32
    ang = np.where(f[:, None] < 16, (n // 64)[None, :], (n % 64)[None, :]).astype(np.float32) * inv[f % 16][:, None]
    put("cos", np.cos(ang))
    put("sin", np.sin(ang) * np.where(r % 64 < 32, -1.0, 1.0)[:, None])
    put("eps", np.full((P, 1), EPS))
    put("expert", np.broadcast_to(np.arange(8), (P, 8)))
    return t


def needed(l):
    return 0 if l == 0 else CTX


class Ledger:

    def __init__(self, nc, ctx, known):
        self.nc, self.ctx, self.known = nc, ctx, known
        self.sems, self.count, self.at = {}, {}, {}

    def sem(self, name):
        if name not in self.sems:
            self.sems[name] = self.ctx.enter_context(self.nc.semaphore(name))
        return self.sems[name]

    def mark(self, name, key, n=1):
        self.count[name] = self.count.get(name, 0) + n
        assert (name, key) not in self.at, (name, key)
        self.at[name, key] = self.count[name]
        return self.sem(name), n

    def when(self, name, key):
        if self.known is None:
            return self.sem(name), 1
        return self.sem(name), self.known.at[name, key]

    def note(self, name, key, value):
        assert (name, key) not in self.at, (name, key)
        self.at[name, key] = value

    def noted(self, name, key, default):
        return self.at.get((name, key), default) if self.known is None else self.known.at[name, key]


def build(nc, A, out, ctab, known):
    ctx = ExitStack()
    with ctx:
        L = Ledger(nc, ctx, known)
        mark, when = L.mark, L.when

        def sb(name, n, dt=F32):
            return ctx.enter_context(nc.sbuf_tensor(name, [P, n], dt))

        ring = sb("ring", NSLOT * SLOT)
        xT = sb("xT", DT * TOK)[:, :].rearrange("p (k n) -> p k n", k=DT)
        hbuf = sb("hT", DT * TOK)
        hT = hbuf[:, :].rearrange("p (k n) -> p k n", k=DT)
        oT = hT
        table = sb("table", NCONST)
        work = sb("work", 6192)
        gates = sb("gates", 2048)
        tmpA, tmpB = sb("tmpA", 512), sb("tmpB", 512)
        vecT = sb("vecT", 2 * P)
        mods = [sb(f"mods{l}", 96) for l in range(2)]
        cond = sb("cond", DT * 14)
        arow = sb("arow", 512)
        one = sb("one", 1)
        rows = sb("rows", 64)
        small = sb("small", 720)
        ints = sb("ints", 4, I32)
        psum = [ctx.enter_context(nc.psum_tensor(f"bank{i}", [P, 512], F32)) for i in range(8)]

        def const(name, i=None):
            o, n = CONST[name]
            return table[:, o:o + n] if i is None else table[:, o + i * P:o + (i + 1) * P]

        ident = const("ident")
        eps = const("eps")

        def slot(s):
            return ring[:, s * SLOT:(s + 1) * SLOT]

        arena = ring[:, 2 * SLOT:7 * SLOT]

        def carve(base, sizes):
            got = []
            for n in sizes:
                got.append(base[:, carve.at:carve.at + n])
                carve.at += n
            return got

        SC_AT = SLOT + 2048 + 1024 + 2048 + 1024 + 512 + 2048 + 3072
        carve.at = SLOT
        rqk, rv, sq, skd, sv, decay, smask, sc, pr, pT, krot, taps = carve(
            arena, (2048, 1024, 2048, 1024, 512, 2048, 3072, 1024, 1024, 1024, 512, 1024))
        oraw2, osq2, odev2 = ([x[:, i * 512:(i + 1) * 512] for i in range(2)] for x in (sc, pr, pT))
        rqk = rqk.rearrange("p (c n) -> p c n", c=4)
        rv = rv.rearrange("p (t n) -> p t n", t=TT)
        sq = sq.rearrange("p (c n) -> p c n", c=4)
        skd = skd.rearrange("p (c n) -> p c n", c=2)
        sv = sv.rearrange("p (t n) -> p t n", t=TT)
        assert carve.at <= 5 * SLOT
        carve.at = 0
        gT, gTT, gAT, gP1, gNT, gAtt, gWU, gKQ, gKD, gRW, gRU, gKB = carve(
            arena, (2048,) * 8 + (1024,) * 4)
        assert carve.at == 5 * SLOT

        def prob(i, nk):
            at = SC_AT + (i % 4) * 512
            return arena[:, at:at + nk]

        def grp(buf, t, n=512):
            return buf[:, t * n:(t + 1) * n]

        def kbuf(t):
            return grp(gKB, t % 2)

        def smk(h, part):
            return grp(smask, 3 * (h % 2) + part)

        def dec(h):
            return grp(decay, h % 2, 1024)

        cin = work[:, 0:3120].rearrange("p (c s n) -> p c s n", c=6, s=2)
        tok = work[:, 0:3072].rearrange("p (t n) -> p t n", t=TT)
        acc = work[:, 3120:6192].rearrange("p (c s n) -> p c s n", c=6, s=2)
        acc2 = work[:, 3120:6192].rearrange("p (c n) -> p c n", c=6)
        qkT = work[:, 3120:3120 + 2048].rearrange("p (c n) -> p c n", c=4)
        rgate = gates[:, 0:1024].rearrange("p (c n) -> p c n", c=2)
        zgate = gates[:, 1024:2048].rearrange("p (c n) -> p c n", c=2)

        vrows = gates[:, 0:2 * P]
        xin = hbuf[:, :]

        def squares(n):
            return work[:, 0:DT * TOK].rearrange("p (k n) -> p k n", k=DT) if n in (0, 1, 3) else hT

        def hidT(f):
            return work[:, f * 512:(f + 1) * 512]

        hrow = work[:, 0:2048].rearrange("p (t n) -> p t n", t=2)
        osb = work[:, 0:2048]
        yrow = work[:, 2048:3072]
        yacc = work[:, 3072:5120].rearrange("p (k n) -> p k n", k=DT)
        pick, wpick, spread = (work[:, a:a + 256] for a in (5120, 5376, 5632))
        hid, mhT = gates[:, 0:1024], gates[:, 1024:2048]
        hg = hT[:, :, 0:P]

        sm_at = [0]

        def sml(n):
            sm_at[0] += n
            return small[:, sm_at[0] - n:sm_at[0]]

        ab = sml(64)
        spz, spe, spl = sml(32), sml(32), sml(32)
        gl = sml(32)
        beta = sml(32)
        gex = sml(128)
        gcs = sml(32)
        kdf = sml(32)
        bgf = sml(32)
        sdec = sml(32)
        ssq = sml(32)
        mx, nmx, rsm, es, den = (sml(4) for _ in range(5))
        lgt, lsum, l256, ln1, ealog = sml(8), sml(4), sml(8), sml(4), sml(8)
        sink8 = sml(8)
        root, rstd = sml(TT), sml(TT)
        assert sm_at[0] <= 720, sm_at
        router = sb("router", 64)[:, :].rearrange("p (k e) -> p k e", k=DT)
        rt = small[:, 0:352]
        rt_at = [0]

        def rts(n):
            rt_at[0] += n
            return rt[:, rt_at[0] - n:rt_at[0]]
        lgts = rts(16).rearrange("p (t e) -> p t e", t=2)
        sel = rts(16).rearrange("p (t e) -> p t e", t=2)
        wexp = rts(16).rearrange("p (t e) -> p t e", t=2)
        less, cmp1, cmp2 = (rts(64).rearrange("p (e f) -> p e f", e=8) for _ in range(3))
        rank, over, nm1, wsum, place, intf = rts(8), rts(8), rts(2), rts(2), rts(24), rts(4)
        itemf = small[:, 352:424]
        items = itemf[:, :].rearrange("p (i u t) -> p i u t", i=3, u=12)
        poolone = sb("poolone", 1)
        state = tmpB[:, 0:256].rearrange("p (c n) -> p c n", c=2)
        vnew = tmpA[:, 0:256]

        VEC = [vecT[:, l * P:(l + 1) * P] for l in range(2)]
        modv = [m[:, :].rearrange("p (m v) -> p m v", v=2) for m in mods]
        condv = cond[:, :].rearrange("p (k n) -> p k n", k=DT)

        loads = []
        where = {}

        def load(key, s, pieces):
            loads.append((key, s, pieces))
            where[key] = s

        def wtile(ap, c0, n):
            return ap[:, c0:c0 + n].rearrange("(k p) n -> p k n", p=P)

        def kslot(s, n=512):
            return slot(s)[:, 0:DT * n].rearrange("p (k n) -> p k n", k=DT)

        def load_ada(l, n, s):
            load(("ada", l, n), s, [(kslot(s), wtile(A["ada_w"][l], n * 512, 512))])

        for l in range(2):
            if l == 0:
                for n in range(4):
                    load_ada(0, n, 3 + n)
            W = A["w_in"][l]
            for n, (name, c0) in enumerate((("gqk", 1024), ("gvz", 1536), ("kvab", None), ("sq", 2064),
                                            ("rqk", 0), ("rvg", 512))):
                v = kslot(n % 3)
                if name == "kvab":
                    pieces = [(v[:, :, 0:256], wtile(W, 2576, 256)), (v[:, :, 256:272], wtile(W, 2048, 16))]
                else:
                    pieces = [(v, wtile(W, c0, 512))]
                load((name, l), n % 3, pieces)
            if l == 0:
                for i, (la, n) in enumerate([(0, n) for n in range(4, 12)] + [(1, n) for n in range(12)]):
                    load_ada(la, n, i % 2)
            for n in range(2):
                load(("wo", l, n), n, [(kslot(n), wtile(A["w_out"][l], n * 512, 512))])
            if l == 0:
                s = 2
                for f0, f1 in FF_PARTS:
                    for f in range(f0, f1, 2):
                        v = kslot(s)
                        load(("up", f), s, [(v[:, :, 0:256], wtile(A["ffn_w1"][0], f * P, 256)),
                                            (v[:, :, 256:512], wtile(A["ffn_w3"][0], f * P, 256))])
                        s = (s + 1) % NSLOT
                    for f in range(f0, f1, 4):
                        m = min(4, f1 - f)
                        v = slot(s)[:, 0:m * D].rearrange("p (q n) -> p q n", q=m)
                        load(("down", f), s, [(v, A["ffn_w2"][0][f * P:(f + m) * P, :].rearrange(
                            "(q p) n -> p q n", p=P))])
                        s = (s + 1) % NSLOT

        phase_done = ctx.enter_context(nc.semaphore("phase_done"))
        AFTER_PHASE = {("up", 0): 2}
        moe_gate_done = ctx.enter_context(nc.semaphore("moe_gate_done"))
        moe_up_done = ctx.enter_context(nc.semaphore("moe_up_done"))
        moe_down_done = ctx.enter_context(nc.semaphore("moe_down_done"))
        moe_slot_full = [ctx.enter_context(nc.semaphore(f"moe_slot_full{s}")) for s in range(NSLOT)]
        (moe_sel_ready, moe_gathered, moe_rows_ready, moe_spread, moe_spread_ready, moe_silu_ready,
         moe_hid_ready, moe_turned, moe_hidT_ready, moe_y_ready, moe_scattered, moe_added, ints_ready,
         out_stored, moe_picks, moe_y_half) = [ctx.enter_context(nc.semaphore(n)) for n in (
             "moe_sel_ready", "moe_gathered", "moe_rows_ready", "moe_spread", "moe_spread_ready",
             "moe_silu_ready", "moe_hid_ready", "moe_turned", "moe_hidT_ready", "moe_y_ready",
             "moe_scattered", "moe_added", "ints_ready", "out_stored", "moe_picks", "moe_y_half")]
        GATHER_BANK = (5, 1)
        PRODUCT_DONE = {"w1": moe_gate_done, "w3": moe_up_done, "w2": moe_down_done}
        STREAM = [("w1", 0), ("w3", 0)]
        for c in range(EC):
            STREAM += [("w1", c + 1), ("w3", c + 1)] if c + 1 < EC else []
            STREAM += [("w2", c)]
        assert len(STREAM) == 3 * NSLOT
        MOE_SLOT = {k: (n + 2) % NSLOT for n, k in enumerate(STREAM)}
        MOE_USE = {k: n // NSLOT for n, k in enumerate(STREAM)}

        block = ctx.enter_context(nc.Block())

        uses = [0] * 8
        was_read = set()

        def open_bank(pe, key, b):
            if uses[b]:
                pe.wait_ge(L.sem(f"bank_read{b}"), uses[b])
            uses[b] += 1
            L.note("bank", key, b)
            L.note("turn", key, uses[b])
            return psum[b]

        def filled(key):
            return mark(f"bank_full{L.at['bank', key]}", key)

        def bank(key):
            return psum[L.noted("bank", key, 0)]

        def full(key):
            return when(f"bank_full{L.noted('bank', key, 0)}", key)

        def read(key):
            assert key not in was_read, key
            was_read.add(key)
            return L.sem(f"bank_read{L.noted('bank', key, 0)}"), 1

        def drained(key):
            return L.sem(f"bank_read{L.noted('bank', key, 0)}"), L.noted("turn", key, 1)

        def weights(key):
            return when(f"slot_full{where[key]}", key)

        def fill_frees(key, product):
            L.note("released", key, (f"bank_full{L.at['bank', product]}", product))

        def stepper(eng, name):
            sem = L.sem(name)
            n = [0]

            def step(ins):
                n[0] += 1
                ins.then_inc(sem, 1)

            def settle():
                eng.wait_ge(sem, n[0])
            return step, settle

        @block.sync
        def _(sp):
            key, s, pieces = loads[0]
            for dst, src in pieces:
                sp.dma_start(dst, src).then_inc(*mark(f"slot_full{s}", key, 16))
            sp.wait_ge(*when("vec_in0", 0))
            for t in range(TT):
                src = A["ctx"] if t < 2 else A["x"]
                sp.dma_start(xin[:, t * D:(t + 1) * D], src[0, (t % 2) * P:(t % 2 + 1) * P, :])\
                    .then_inc(*mark("x_in", t, 16))
            held = {s: key}
            for key, s, pieces in loads[1:]:
                if key == ("gqk", 0):
                    sp.dma_start(table[:, NEARLY:NCONST], ctab[:, NEARLY:NCONST])\
                        .then_inc(*mark("table_in", "all", 16))
                if s in held:
                    sp.wait_ge(*when(*L.noted("released", held[s], ("bank_full0", "-"))))
                if key in AFTER_PHASE:
                    sp.wait_ge(phase_done, 4 * AFTER_PHASE[key])
                for i, (dst, src) in enumerate(pieces):
                    sp.dma_start(dst, src).then_inc(
                        *mark(f"slot_full{s}", key if i == len(pieces) - 1 else (key, i), 16))
                held[s] = key
            sp.wait_ge(phase_done, 4 * 4)
            w1, w3, w2 = A["moe_w1"][0], A["moe_w3"][0], A["moe_w2"][0]

            def expert(item, e):
                w1e = w1[bass.ds(e, 1)].rearrange("o (k p) n -> p (o k) n", p=P)
                w3e = w3[bass.ds(e, 1)].rearrange("o (k p) n -> p (o k) n", p=P)
                w2e = w2[bass.ds(e, 1)].rearrange("o (k p) n -> p (o k) n", p=P)
                for n, (kind, c) in enumerate(STREAM):
                    s = MOE_SLOT[kind, c]
                    if n < NSLOT:
                        k0, c0 = STREAM[n + 2 * NSLOT]
                        sp.wait_ge(PRODUCT_DONE[k0], item * EC + (c0 + 1))
                    else:
                        k0, c0 = STREAM[n - NSLOT]
                        sp.wait_ge(PRODUCT_DONE[k0], item * EC + (EC + c0 + 1))
                    if kind == "w2":
                        dst = slot(s).rearrange("p (q n) -> p q n", q=4)
                        src = w2e[:, 4 * c:4 * c + 4, :]
                    else:
                        dst = kslot(s)
                        src = (w1e if kind == "w1" else w3e)[:, :, c * 512:(c + 1) * 512]
                    sp.dma_start(dst, src).then_inc(moe_slot_full[s], 16)

            with sp.Fori(0, EXPERTS) as e:
                expert(e, e)
            sp.wait_ge(ints_ready, 1)
            n_over = sp.value_load(ints[0:1, 0:1], min_val=0, max_val=3)
            with sp.Fori(0, ITEMS - EXPERTS) as o:
                with sp.If(o < n_over):
                    e = sp.value_load(ints[0:1, bass.ds(o + 1, 1)], min_val=0, max_val=EXPERTS - 1)
                    expert(o + EXPERTS, e)
            for t in range(2):
                sp.wait_ge(*when("out_row", t))
                sp.dma_start(out[0, t * P:(t + 1) * P, :], osb[:, t * D:(t + 1) * D]).then_inc(out_stored, 16)
            sp.wait_ge(out_stored, 32)

        @block.tensor
        def _(pe):
            rot = [0]

            ada_bank = [None]

            def product(key, banks=range(8)):
                banks = [b for b in banks if b != ada_bank[0]]
                rot[0] += 1
                return open_bank(pe, key, banks[rot[0] % len(banks)])

            def mm(o, w, x, start=True, stop=True):
                return nc.tensor.matmul(o, w, x, start=start, stop=stop)

            def turn(o, x, n=P):
                return nc.tensor.transpose(o, x, ident[0:n, 0:n])

            def turn_vectors(l):
                pe.wait_ge(*when(f"vec_in{l}", l))
                o = product(("vec", l))
                turn(o[:, 0:NVEC], vrows[0:NVEC, l * P:(l + 1) * P], NVEC).then_inc(*filled(("vec", l)))

            pe.wait_ge(*when("early_in", 0))
            turn_vectors(0)
            ada_at = [0]

            def ada(count):
                for _ in range(count):
                    l, n, k = ada_at[0] // (12 * DT), ada_at[0] // DT % 12, ada_at[0] % DT
                    ada_at[0] += 1
                    g, j = divmod(n, 4)
                    key = ("ada", l, g)
                    if (j, k) == (0, 0):
                        open_bank(pe, key, 5)
                    if k == 0:
                        pe.wait_ge(*weights(("ada", l, n)))
                    ins = mm(psum[5][0:8, :], condv[:, k, 6 - 2 * j:14 - 2 * j], kslot(where["ada", l, n])[:, k, :],
                             (j, k) == (0, 0), (j, k) == (3, DT - 1))
                    if k == DT - 1:
                        if j < 3:
                            ins.then_inc(*mark("ada_slot_used", (l, n)))
                            L.note("released", ("ada", l, n), ("ada_slot_used", (l, n)))
                        else:
                            ins.then_inc(*filled(key))
                            fill_frees(("ada", l, n), key)

            def ada_turn(l, g):
                pe.wait_ge(*drained(("ada", l, g)))
                o = product(("adaT", l, g), range(6))
                for c in range(4):
                    ins = turn(o[:, 8 * c:8 * c + 8], arow[0:8, c * P:(c + 1) * P], 8)
                ins.then_inc(*filled(("adaT", l, g)))

            def norm(n, lo=0):
                pe.wait_ge(*when("squares_added", (n, DT - 1)))
                o = product(("ss", n))
                for t in range(lo // P, TT):
                    ins = mm(o[:, t:t + 1], squares(n)[:, 0, t * P:(t + 1) * P], const("ones")[:, 0:1])
                ins.then_inc(*filled(("ss", n)))
                if n == 0:
                    ada(2)
                pe.wait_ge(*when("inverse_root", n))
                o = product(("rstd", n))
                for t in range(lo // P, TT):
                    ins = mm(o[:, t * P:(t + 1) * P], rstd[:, t:t + 1].to_broadcast([P, P]), ident)
                ins.then_inc(*filled(("rstd", n)))

            def by_channel(key, w, c, x, lo=0, n=None, ks=range(DT), banks=range(8)):
                o = product(key, banks)
                for k in ks:
                    if n is not None:
                        pe.wait_ge(*when("mod", (n, k)))
                    ins = mm(o[:, lo:TOK], w[:, k, c * P:(c + 1) * P], x[:, k, lo:TOK], k == ks[0], k == ks[-1])
                ins.then_inc(*filled(key))

            def by_token(key, w, c0, n, t):
                o = product(key)
                for k in range(DT):
                    ins = mm(o[:, 0:n], hT[:, k, t * P:(t + 1) * P], w[:, k, c0:c0 + n], k == 0, k == DT - 1)
                ins.then_inc(*filled(key))

            def project(l):
                for name in ("gqk", "gvz", "kvab", "sq", "rqk", "rvg"):
                    if (name, l) == ("gvz", 0):
                        turn_vectors(1)
                    pe.wait_ge(*weights((name, l)))
                    w = kslot(where[name, l])
                    if name == "gqk":
                        keys = [(("gc", l, c), c) for c in range(4)]
                    elif name == "gvz":
                        keys = [(("gc", l, 4), 0), (("gc", l, 5), 1), (("z", l, 0), 2), (("z", l, 1), 3)]
                    elif name == "kvab":
                        keys = [(("sk", l), 0)]
                    elif name == "rvg":
                        keys = [(("rg", l, 0), 2), (("rg", l, 1), 3)]
                    else:
                        keys = [((name, l, c), c) for c in range(4)]
                    for key, c in keys:
                        keys_values = name in ("kvab", "gqk", "gvz", "rqk") and \
                            not (key[0] == "z" or key[0] in ("gc", "rqk") and c < 2 and name != "gvz")
                        by_channel(key, w, c, hT, 0 if keys_values else needed(l),
                                   2 * l if key == ("gc", l, 0) else None)
                    if name == "kvab":
                        for t in range(TT):
                            key = ("vab", l, t)
                            by_token(key, w, P, 144, t)
                    if name == "rvg":
                        for t in range(TT):
                            key = ("rv", l, t)
                            by_token(key, w, 0, 256, t)
                    fill_frees((name, l), key)

            def window(l):
                q0 = 0 if l == 0 else 2
                units = [(h, t) for h in range(8) for t in range(q0, TT)]

                def score(h, t):
                    m, p = divmod(h, 2)
                    nk = CTX if t < 2 else TOK
                    if (h, t) == units[0]:
                        pe.wait_ge(*drained(("sk", l)))
                        for c in range(4):
                            pe.wait_ge(*when("sq_ready", (l, c)))
                        pe.wait_ge(*when("sk_ready", l))
                    o = product(("sc", l, h, t), range(6))
                    mm(o[:, 0:nk], sq[p * HD:p * HD + HD, m, t * P:(t + 1) * P], skd[p * HD:p * HD + HD, m // 2, 0:nk]
                       ).then_inc(*filled(("sc", l, h, t)))

                def turn_probs(h, t):
                    pe.wait_ge(*when("probs", (l, h, t)))
                    o = product(("pt", l, h, t), range(6))
                    i = units.index((h, t))
                    for k in range(2 if t < 2 else 4):
                        ins = turn(o[:, k * P:(k + 1) * P], prob(i, 512)[:, k * P:(k + 1) * P])
                    ins.then_inc(*filled(("pt", l, h, t)))

                def values(h, t):
                    m, p = divmod(h, 2)
                    i = units.index((h, t))
                    key = ("so", l, m)
                    if p == 0 and t == q0:
                        open_bank(pe, key, 6 + m % 2)
                    o = psum[6 + m % 2]
                    pe.wait_ge(*drained(("pt", l, h, t)))
                    nk = 2 if t < 2 else 4
                    for k in range(nk):
                        ins = mm(o[p * HD:p * HD + HD, t * P:(t + 1) * P], sv[:, k, (h // 4) * HD:(h // 4) * HD + HD],
                                 pT[:, (i % 2) * 512 + k * P:(i % 2) * 512 + (k + 1) * P], k == 0, k == nk - 1)
                    if (p, t) == (1, TT - 1):
                        ins.then_inc(*filled(key))

                for i in range(len(units) + 4):
                    if i < len(units):
                        score(*units[i])
                    if l == 0 and i < 4 * DT:
                        ada(1)
                    if 0 <= i - 3 < len(units):
                        turn_probs(*units[i - 3])
                    if 0 <= i - 4 < len(units):
                        values(*units[i - 4])

            def retention(l):
                parts, lo = (2 if l else 3), needed(l)
                for c in range(4):
                    pe.wait_ge(*when("rqk_ready", (l, c)))
                for t in range(TT):
                    pe.wait_ge(*drained(("rv", l, t)))

                def scores(h):
                    i, p = divmod(h, 2)
                    hp = slice(p * HD, p * HD + HD)
                    for part in range(parts):
                        key = ("rs", l, h, part)
                        o = product(key, range(6))
                        qs = slice(0, CTX) if part == 2 else slice(CTX, TOK)
                        for j in range(2):
                            kt = j if part != 1 else 2 + j
                            ins = mm(o[:, j * 256:(j + 1) * 256], rqk[hp, 2 + i, kt * P:(kt + 1) * P], rqk[hp, i, qs])
                        ins.then_inc(*filled(key))

                def values(h):
                    i, p = divmod(h, 2)
                    key = ("ro", l, i)
                    if p == 0:
                        open_bank(pe, key, 6 + i)
                    o = psum[6 + i]
                    for part in range(parts):
                        pe.wait_ge(*drained(("rs", l, h, part)))
                    hp = slice(p * HD, p * HD + HD)
                    hv = slice(h * HD, h * HD + HD)
                    for j in range(2 if l == 0 else 0):
                        mm(o[hp, 0:CTX], rv[:, j, hv], smk(h, 2)[:, j * 256:(j + 1) * 256], j == 0, j == 1)
                    for j in range(4):
                        ins = mm(o[hp, CTX:TOK], rv[:, j, hv], smk(h, j // 2)[:, (j % 2) * 256:(j % 2 + 1) * 256],
                                 j == 0, j == 3)
                    if p == 1:
                        ins.then_inc(*filled(key))
                    else:
                        ins.then_inc(*mark("ret_values", (l, h)))

                pe.wait_ge(*when("log_decay", l))
                key = ("gsum", l)
                o = product(key, range(6))
                for d in range(2):
                    mm(o[:, 16 * d:16 * d + 16], const(f"incl{d}"), gl[:, 16 * d:16 * d + 16])
                for j, name in enumerate(("same", "half0", "half1")):
                    ins = mm(o[:, 32 + 32 * j:64 + 32 * j], const(name), gl)
                ins.then_inc(*filled(key))
                for h in range(4 + 1):
                    if h < 4:
                        scores(h)
                    if l == 0:
                        ada(2)
                    if h == 1 and l == 0:
                        ada_turn(0, 1)
                    if h >= 1:
                        values(h - 1)
                for i in range(2):
                    if l == 0:
                        ada(2)
                    pe.wait_ge(*drained(("ro", l, i)))
                    mm(product(("rmean", l, i), range(6))[:, lo:TOK], const("head_mean"), oraw2[i][:, lo:TOK])\
                        .then_inc(*filled(("rmean", l, i)))
                for i in range(2):
                    if l == 0:
                        ada(2)
                    pe.wait_ge(*when("head_square", ("r", l, i)))
                    mm(product(("rvar", l, i), range(6))[:, lo:TOK], const("head_mean"), osq2[i][:, lo:TOK])\
                        .then_inc(*filled(("rvar", l, i)))

            def delta_prepare(l):
                for c in range(6):
                    pe.wait_ge(*when("conv_silu", (l, c)))
                for t in range(TT):
                    for part, cs in enumerate((range(4), range(4, 6))):
                        key = ("ct", l, t, part)
                        o = product(key)
                        for j, c in enumerate(cs):
                            ins = turn(o[:, j * P:(j + 1) * P], acc2[:, c, t * P:(t + 1) * P])
                        ins.then_inc(*filled(key))
                if l == 0:
                    ada(7)
                for t in range(TT):
                    key = ("qkt", l, t)
                    pe.wait_ge(*when("qk_unit", (l, t)))
                    o = product(key)
                    for j in range(4):
                        ins = turn(o[:, j * P:(j + 1) * P], tok[:, t, j * P:(j + 1) * P])
                    ins.then_inc(*filled(key))
                if l == 0:
                    ada(2)

            def between(l, d, n, part):
                if l == 0:
                    ada((2 if d else 3, 2)[1 - part])
                    return
                ks = (0, 1, 4, 5, 6, 7)
                m = 4 * d + n // 2
                at = 3 * (n % 2) + part
                if at == 0:
                    if m == 0:
                        for i in range(2):
                            pe.wait_ge(*when("ret_out", (l, i)))
                        for i in range(4):
                            pe.wait_ge(*drained(("so", l, i)))
                    if m % 4 == 0:
                        pe.wait_ge(*weights(("wo", l, m // 4)))
                    product(("woe", l, m), range(6))
                w = kslot(where["wo", l, m // 4])
                for k in ks[at:at + 1 + part]:
                    ins = mm(psum[L.at["bank", ("woe", l, m)]][:, CTX:TOK], w[:, k, (m % 4) * P:(m % 4 + 1) * P],
                             oT[:, k, CTX:TOK], k == 0, k == 7)
                if k == 7:
                    ins.then_inc(*filled(("woe", l, m)))

            def delta(l, d):
                R6 = range(6)
                for t in range(TT):
                    key = ("kq", l, d, t)
                    pe.wait_ge(*when("kbqd", (l, d, t)))
                    o = product(key, R6)
                    for j in range(4):
                        ins = turn(o[:, j * P:(j + 1) * P], kbuf(t)[:, j * P:(j + 1) * P])
                    ins.then_inc(*filled(key))
                    key = ("dec", l, d, t)
                    o = product(key, R6)
                    for h in range(4):
                        at = 16 * d + 4 * t + h
                        ins = mm(o[:, h * P:(h + 1) * P], gl[:, at:at + 1].to_broadcast([P, P]), const(f"incl{d}"))
                    ins.then_inc(*filled(key))
                for t in range(TT):
                    if l == 0 and t:
                        ada(2 if d == 0 else 4)
                    pe.wait_ge(*drained(("kq", l, d, t)))
                    for p in range(2):
                        key = ("kkqk", l, d, t, p)
                        o = product(key, R6)
                        hp = slice(p * HD, p * HD + HD)
                        ts = slice(t * P, (t + 1) * P)
                        for i in range(2):
                            ins = mm(o[:, i * P:(i + 1) * P], qkT[hp, 2 + i, ts], grp(gKQ, t)[hp, i * P:(i + 1) * P])
                            if l and t < 2:
                                continue
                            ins = mm(o[:, (2 + i) * P:(3 + i) * P], qkT[hp, 2 + i, ts], qkT[hp, i, ts])
                        ins.then_inc(*filled(key))
                if l == 0:
                    ada(2 if d == 0 else 4)
                for t in range(TT):
                    key = ("T0", l, d, t)
                    pe.wait_ge(*when("TT_first", (l, d, t)))
                    o = product(key, R6)
                    for h in range(4):
                        ins = turn(o[:, h * P:(h + 1) * P], grp(gTT, t)[:, h * P:(h + 1) * P])
                    ins.then_inc(*filled(key))

                def by_head(key, a, b, t):
                    o = product(key, R6)
                    for h in range(4):
                        hs = slice(h * P, (h + 1) * P)
                        ins = mm(o[:, hs], grp(a, t)[:, hs], grp(b, t)[:, hs])
                    ins.then_inc(*filled(key))

                for v in range(1, 6):
                    for t in range(TT):
                        pe.wait_ge(*when("NT", (l, d, v, t)))
                        if v == 1:
                            pe.wait_ge(*drained(("T0", l, d, t)))
                        else:
                            pe.wait_ge(*drained(("TP", l, d, v - 1, t)))
                        by_head(("P1", l, d, v, t), gNT, gT, t)
                    for t in range(TT):
                        pe.wait_ge(*drained(("P1", l, d, v, t)))
                        if v > 1:
                            pe.wait_ge(*drained(("TTP", l, d, v - 1, t)))
                        if v < 5:
                            by_head(("TP", l, d, v, t), gTT, gP1, t)
                        by_head(("TTP", l, d, v, t), gP1, gTT, t)
                for t in range(TT):
                    key = ("wu", l, d, t)
                    pe.wait_ge(*drained(("TTP", l, d, 5, t)))
                    pe.wait_ge(*when("rhs", (l, d, t)))
                    o = product(key, R6)
                    for h in range(4):
                        i, p = divmod(h, 2)
                        th = grp(gTT, t)[:, h * P:(h + 1) * P]
                        hs = slice(h * HD, h * HD + HD)
                        mm(o[p * HD:p * HD + HD, i * P:(i + 1) * P], grp(gRW, t, 256)[:, hs], th)
                        ins = mm(o[:, 256 + h * HD:256 + h * HD + HD], th, grp(gRU, t, 256)[:, hs])
                    ins.then_inc(*filled(key))
                pe.wait_ge(*when("state_zero", (l, d)))
                for n, (t, c) in enumerate(steps(d)):
                    cs = slice(c * CHUNK, c * CHUNK + CHUNK)
                    key = ("vn", l, d, n)
                    if (l, d, n) == (0, 1, 4):
                        ada_turn(1, 1)
                    pe.wait_ge(*drained(("wu", l, d, t)))
                    if n:
                        pe.wait_ge(*drained(("su", l, d, n - 1)))
                    o = product(key, R6)
                    for i in range(2):
                        ins = mm(o[cs, i * P:(i + 1) * P], grp(gWU, t)[:, i * P + c * CHUNK:i * P + (c + 1) * CHUNK],
                                 state[:, i, :])
                    ins.then_inc(*filled(key))
                    between(l, d, n, 0)
                    go = ("go", l, d, t)
                    shown = l == 0 or t >= 2
                    if n % 2 == 0 and shown:
                        for i in range(2):
                            open_bank(pe, (*go, i), 6 + i)
                    for i in range(2 if shown else 0):
                        mm(psum[6 + i][:, cs], state[:, i, :],
                           grp(gKQ, t)[:, (2 + i) * P + c * CHUNK:(2 + i) * P + (c + 1) * CHUNK], True, False)
                    pe.wait_ge(*when("kd", (l, d, t)))
                    pe.wait_ge(*drained(("vn", l, d, n)))
                    key = ("su", l, d, n)
                    o = product(key, R6)
                    for h in range(4):
                        i, p = divmod(h, 2)
                        hs = slice(h * HD, h * HD + HD)
                        ins = mm(o[p * HD:p * HD + HD, i * HD:(i + 1) * HD], grp(gKD, t, 256)[cs, hs], vnew[cs, hs])
                    ins.then_inc(*filled(key))
                    for h in range(4 if shown else 0):
                        i, p = divmod(h, 2)
                        ins = mm(psum[6 + i][p * HD:p * HD + HD, cs], vnew[:, h * HD:h * HD + HD],
                                 grp(gAtt, t)[:, h * P + c * CHUNK:h * P + (c + 1) * CHUNK], False, True)
                        if n % 2 == 1 and p == 1:
                            ins.then_inc(*filled((*go, i)))
                    between(l, d, n, 1)

            def delta_finish(l):
                for i in range(2):
                    pe.wait_ge(*when("head_square", ("g", l, i)))
                    mm(product(("gvar", l, i), range(6))[:, needed(l):TOK], const("head_mean"), tmpB[:, needed(l):TOK])\
                        .then_inc(*filled(("gvar", l, i)))
                    if l == 0:
                        out_project_early(i)

            EARLY = 2

            def out_project_early(m):
                if m == 0:
                    for i in range(2):
                        pe.wait_ge(*when("ret_out", (0, i)))
                    for i in range(4):
                        pe.wait_ge(*drained(("so", 0, i)))
                    pe.wait_ge(*weights(("wo", 0, 0)))
                o = open_bank(pe, ("wo", 0, m), 6 + m)
                for k in (0, 1, 4, 5, 6, 7):
                    mm(o[:, :], kslot(where["wo", 0, 0])[:, k, m * P:(m + 1) * P], oT[:, k, :], k == 0, False)

            def out_project(l, lo):
                pe.wait_ge(*when("mixed", l))
                for n in range(2):
                    pe.wait_ge(*weights(("wo", l, n)))
                    for c in range(4):
                        m = 4 * n + c
                        if l == 0 and m < EARLY:
                            for k in (2, 3):
                                ins = mm(psum[L.at["bank", ("wo", 0, m)]][:, :], kslot(where["wo", 0, 0])[:, k, m * P:(m + 1) * P], oT[:, k, :], False, k == 3)
                            ins.then_inc(*filled(("wo", 0, m)))
                            continue
                        by_channel(("wo", l, 4 * n + c), kslot(where["wo", l, n]), c, oT, lo,
                                   ks=(2, 3) if l else range(DT))
                    fill_frees(("wo", l, n), ("wo", l, 4 * n + 3))
                norm(2 * l + 1, lo)

            def ffn():
                for half, (f0, f1) in enumerate(FF_PARTS):
                    for f in range(f0, f1):
                        w = kslot(where["up", f - f % 2])
                        pe.wait_ge(*weights(("up", f - f % 2)))
                        by_channel(("fa", f), w, f % 2, hT, n=None if f else 1)
                        by_channel(("fb", f), w, 2 + f % 2, hT)
                        if f % 2:
                            fill_frees(("up", f - 1), ("fb", f))
                    for d in range(DT):
                        open_bank(pe, ("fy", half, d), d)
                    for f in range(f0, f1, 4):
                        m = min(4, f1 - f)
                        pe.wait_ge(*weights(("down", f)))
                        for q in range(m):
                            pe.wait_ge(*drained(("fb", f + q)))
                        last = f + m == f1
                        w = slot(where["down", f])[:, 0:m * D].rearrange("p (q n) -> p q n", q=m)
                        for d in range(DT):
                            for q in range(m):
                                ins = mm(psum[d][:, :], w[:, q, d * P:(d + 1) * P], hidT(f + q - f0),
                                         f == f0 and q == 0, last and q == m - 1)
                            if last:
                                ins.then_inc(*filled(("fy", half, d)))
                        if last:
                            fill_frees(("down", f), ("fy", half, DT - 1))
                        else:
                            ins.then_inc(*mark("down_slot_used", f))
                            L.note("released", ("down", f), ("down_slot_used", f))

            def phase_leave(last):
                pe.wait_ge(*full_here(last))
                pe.sem_inc(phase_done, 1)

            def phase_enter(k):
                pe.wait_ge(phase_done, 4 * k)

            def full_here(key):
                return L.sem(f"bank_full{L.at['bank', key]}"), L.at[f"bank_full{L.at['bank', key]}", key]

            pe.wait_ge(*when("cond", 0))
            ada_bank[0] = 5
            ada(DT)
            pe.wait_ge(*when("x_in", 3))
            for k in range(DT):
                o = product(("x", k))
                for t in range(TT):
                    ins = turn(o[:, t * P:(t + 1) * P], xin[:, t * D + k * P:t * D + (k + 1) * P])
                ins.then_inc(*filled(("x", k)))
            ada(2 * DT)
            norm(0)
            ada(DT - 2)
            ada_turn(0, 0)
            pe.wait_ge(*when("table_in", "all"))
            for l in range(2):
                ada_bank[0] = None
                project(l)
                if l == 0:
                    ada_bank[0] = 5
                window(l)
                retention(l)
                phase_leave(("rvar", l, 1))
                delta_prepare(l)
                if l == 0:
                    ada(5)
                phase_enter(2 * l + 1)
                if l == 0:
                    ada_turn(0, 2)
                delta(l, 0)
                if l == 0:
                    ada_turn(1, 0)
                delta(l, 1)
                delta_finish(l)
                if l == 0:
                    ada_turn(1, 2)
                    assert ada_at[0] == 24 * DT
                phase_leave(("gvar", l, 1))
                phase_enter(2 * l + 2)
                ada_bank[0] = None
                if l == 1:
                    pe.sem_inc(moe_gate_done, EC)
                    pe.sem_inc(moe_up_done, EC)
                    pe.sem_inc(moe_down_done, EC - 2)
                out_project(l, needed(l))
                if l == 0:
                    ffn()
                    norm(2)
            pe.wait_ge(*full_here(("wo", 1, 7)))
            pe.sem_inc(moe_down_done, 2)
            pe.wait_ge(*when("mod", (3, DT - 1)))
            pe.wait_ge(*when("router_in", 0))
            key = "logits"
            o = product(key)
            for t in range(2):
                for k in range(DT):
                    ins = mm(o[:, t * 8:t * 8 + 8], hT[:, k, CTX + t * P:CTX + (t + 1) * P], router[:, k, :],
                             k == 0, k == DT - 1)
            ins.then_inc(*filled(key))
            for t in range(2):
                for q in range(2):
                    key = ("row", t, q)
                    o = product(key)
                    for j in range(4):
                        ins = turn(o[:, j * P:(j + 1) * P], hT[:, 4 * q + j, CTX + t * P:CTX + (t + 1) * P])
                    ins.then_inc(*filled(key))
            pe.wait_ge(*when("chosen", 0))
            key = "places"
            o = product(key)
            mm(o[:, 0:8], const("before"), sel[:, 0, :])
            mm(o[:, 8:16], const("ones"), sel[:, 0, :], True, False)
            mm(o[:, 8:16], const("before"), sel[:, 1, :], False, True)
            mm(o[:, 16:24], const("ones"), sel[:, 0, :], True, False)
            mm(o[:, 16:24], const("ones"), sel[:, 1, :], False, True).then_inc(*filled(key))
            for b in range(8):
                pe.wait_ge(L.sem(f"bank_read{b}"), uses[b])
            for t in range(2):
                for q in range(2):
                    pe.wait_ge(*drained(("row", t, q)))

            def gather():
                for q in range(2):
                    for j in range(4):
                        for t in range(2):
                            ins = mm(psum[GATHER_BANK[q]][:, j * P:(j + 1) * P],
                                     hrow[:, t, (4 * q + j) * P:(4 * q + j + 1) * P],
                                     pick[:, t * P:(t + 1) * P], t == 0, t == 1)
                    ins.then_inc(moe_gathered, 1)

            def scatter(u):
                pe.wait_ge(moe_y_ready, u + 1)
                pe.wait_ge(moe_spread_ready, u + 1)
                for j in range(4):
                    if j == 0:
                        pe.wait_ge(moe_hidT_ready, u * EC + 1)
                    if j >= 2:
                        pe.wait_ge(moe_added, u * 4 + j)
                    for n in range(2):
                        k = 2 * j + n
                        ins = mm(psum[4 + j % 2][:, n * 256:(n + 1) * 256], yrow[:, k * P:(k + 1) * P], spread[:, :])
                    ins.then_inc(moe_scattered, 1)

            def item(u):
                pe.wait_ge(moe_rows_ready, u * 2 + 2)

                def up(c, kind, b, read_sem, done):
                    s = MOE_SLOT[kind, c]
                    pe.wait_ge(moe_slot_full[s], u * 48 + (MOE_USE[kind, c] + 1) * 16)
                    pe.wait_ge(read_sem, u * EC + max(c, 1))
                    for k in range(DT):
                        ins = mm(psum[b][:, :], hg[:, k, 0:P], kslot(s)[:, k, :], k == 0, k == DT - 1)
                    ins.then_inc(done, 1)

                def gate_up(c):
                    up(c, "w1", c % 2, moe_silu_ready, moe_gate_done)

                def lin_up(c):
                    up(c, "w3", 2 + c % 2, moe_hid_ready, moe_up_done)

                def turn_hidden(c):
                    pe.wait_ge(moe_hid_ready, u * EC + (c + 2))
                    pe.wait_ge(moe_hidT_ready, u * EC + (c + 1))
                    if c == 0:
                        pe.wait_ge(moe_added, u * 4 + 4)
                    for q in range(4):
                        ins = turn(psum[4][:, q * P:(q + 1) * P], hid[:, (c % 2) * 512 + q * P:(c % 2) * 512 + (q + 1) * P])
                    ins.then_inc(moe_turned, 1)

                def down(c):
                    s = MOE_SLOT["w2", c]
                    pe.wait_ge(moe_slot_full[s], u * 48 + (MOE_USE["w2", c] + 1) * 16)
                    pe.wait_ge(moe_hidT_ready, u * EC + (c + 2))
                    if c == 0:
                        pe.wait_ge(moe_y_ready, u + 1)
                    w = slot(s).rearrange("p (q n) -> p q n", q=4)
                    for q in range(4):
                        for n in range(2):
                            ins = mm(psum[6 + n][:, :], mhT[:, (c % 2) * 512 + q * P:(c % 2) * 512 + (q + 1) * P],
                                     w[:, q, n * 512:(n + 1) * 512], c == 0 and q == 0, c == EC - 1 and q == 3)
                    ins.then_inc(moe_down_done, 1)

                gate_up(0)
                lin_up(0)
                scatter(u)
                for t in range(2):
                    ins = turn(psum[3][:, t * P:(t + 1) * P], wpick[:, t * P:(t + 1) * P])
                ins.then_inc(moe_spread, 1)
                for c in range(EC - 1):
                    gate_up(c + 1)
                    turn_hidden(c)
                    if c == 0:
                        pe.wait_ge(moe_spread_ready, u + 2)
                    lin_up(c + 1)
                    if c == EC - 2:
                        pe.wait_ge(moe_sel_ready, u + 2)
                        pe.wait_ge(moe_added, u * 4 + 5)
                        pe.wait_ge(moe_silu_ready, u * EC + EC)
                        gather()
                        turn_hidden(c + 1)
                    down(c)
                down(EC - 1)

            pe.sem_inc(moe_turned, 1)
            pe.wait_ge(moe_sel_ready, 1)
            gather()
            with pe.Fori(0, EXPERTS) as e:
                item(e)
            pe.wait_ge(ints_ready, 1)
            n_over = pe.value_load(ints[0:1, 0:1], min_val=0, max_val=3)
            with pe.Fori(0, ITEMS - EXPERTS) as o:
                with pe.If(o < n_over):
                    item(o + EXPERTS)

            scatter(n_over + EXPERTS)

            norm(4, CTX)
            pe.wait_ge(*when("mod", (4, DT - 1)))
            for t in range(2):
                for q in range(2):
                    key = ("out", t, q)
                    o = product(key)
                    for j in range(4):
                        ins = turn(o[:, j * P:(j + 1) * P], hT[:, 4 * q + j, CTX + t * P:CTX + (t + 1) * P])
                    ins.then_inc(*filled(key))

        @block.scalar
        def _(act):
            step, settle = stepper(act, "act_step")

            def fn(o, i, f, **kw):
                return nc.scalar.activation(o, i, f, **kw)

            act.dma_start(table[:, 0:NEARLY], ctab[:, 0:NEARLY]).then_inc(*mark("early_in", 0, 16))
            for l in range(2):
                def vec(r, n, src, last=False):
                    act.dma_start(vrows[r:r + n, l * P:(l + 1) * P], src)\
                        .then_inc(*mark(f"vec_in{l}", l if last else (l, r), 16))

                def by_row(ap):
                    return ap.rearrange("(r p) -> r p", p=P)
                vec(V_ADAB, 48, by_row(A["ada_b"][l]))
                vec(V_N1, 8, by_row(A["norm1_g"][l]))
                vec(V_N2, 8, by_row(A["norm2_g"][l]))
                vec(V_CONV, 30, A["gdn_conv_w"][l].rearrange("a (c p) -> (a c) p", p=P))
                vec(V_RETG, 2, by_row(A["ret_gn_g"][l]))
                vec(V_FIN, 8, by_row(A["final_g"]))
                for p in range(2):
                    act.dma_start(vrows[V_GDNG:V_GDNG + 1, l * P + p * HD:l * P + (p + 1) * HD],
                                  A["gdn_norm_g"][l:l + 1, :]).then_inc(*mark(f"vec_in{l}", (l, "g", p), 16))
                vec(V_C, 8, by_row(A["c"][0]))
                vec(V_CC, 8, by_row(A["c_ctx"]), True)
                if l == 0:
                    act.wait_ge(*drained(("vec", 0)))
                    act.wait_ge(*when("cond_zero", 0))
                    fn(condv[:, :, 6:8], VEC[0][:, V_C:V_C + 16].rearrange("p (v k) -> p k v", v=2), ACT.Silu)\
                        .then_inc(*mark("cond", 0))
                for i, src in enumerate((A["ret_decay"][l].rearrange("d h -> (d h)"),
                                         A["gdn_a_log"][l].rearrange("d h -> (d h)"),
                                         A["gdn_dt_bias"][l].rearrange("d h -> (d h)"), A["swa_sink"][l])):
                    act.dma_start(rows[:, 32 * l + 8 * i:32 * l + 8 * i + 8], src.partition_broadcast(P))\
                        .then_inc(*mark("rows_in", (l, i), 16))
            act.dma_start(router[:, :, :], A["router_w"][0].rearrange("(k p) e -> p k e", p=P))\
                .then_inc(*mark("router_in", 0, 16))
            for k in range(1, DT, 2):
                act.wait_ge(*full(("x", k)))
                fn(xT[:, k, :], bank(("x", k))[:, :], ACT.Copy).then_inc(*read(("x", k)))

            def ada_rows(l, g):
                act.wait_ge(*full(("ada", l, g)))
                if (l, g) != (0, 0):
                    act.wait_ge(*full(("adaT", l if g else 0, (g - 1) % 3)))
                fn(arow[0:8, :], bank(("ada", l, g))[0:8, :], ACT.Copy).then_inc(*read(("ada", l, g)))

            def norm(n, lo=0):
                l, w = divmod(n, 2)
                for k in range(DT):
                    if n == 4:
                        act.wait_ge(*when("final_residual", k))
                    else:
                        act.wait_ge(*drained(("x", k) if n == 0 else ("fy", 1, k) if n == 2 else ("wo", l, k)))
                    fn(squares(n)[:, k, lo:TOK], xT[:, k, lo:TOK], ACT.Square).then_inc(*mark("square", (n, k)))
                act.wait_ge(*full(("ss", n)))
                fn(root[:, lo // P:TT], bank(("ss", n))[:, lo // P:TT], ACT.Sqrt, bias=eps, scale=1.0 / D)\
                    .then_inc(*read(("ss", n)))
                if n == 4:
                    return
                if n == 0:
                    ada_rows(0, 0)
                act.wait_ge(*when("scales", (l, w)))
                mod = modv[l][:, 24 * w:24 * w + 16, :]
                for k in range(DT):
                    act.wait_ge(*when("normed", (n, k)))
                    if lo == 0:
                        step(fn(hT[:, k, 0:CTX], hT[:, k, 0:CTX], ACT.Identity,
                                bias=mod[:, k, 1:2], scale=mod[:, DT + k, 1:2]))
                    fn(hT[:, k, CTX:TOK], hT[:, k, CTX:TOK], ACT.Identity, bias=mod[:, k, 0:1],
                       scale=mod[:, DT + k, 0:1]).then_inc(*mark("mod", (n, k)))

            def project(l):
                lo = needed(l)
                act.wait_ge(*when("pads", l))
                for c in range(6):
                    key = ("gc", l, c)
                    act.wait_ge(*full(key))
                    s0 = 1 if l and c < 2 else 0
                    fn(cin[:, c, s0:2, 2:258], bank(key)[:, s0 * CTX:TOK].rearrange("p (s n) -> p s n", n=CTX),
                       ACT.Copy).then_inc(*read(key))
                for i in range(2):
                    key = ("z", l, i)
                    act.wait_ge(*full(key))
                    fn(zgate[:, i, lo:TOK], bank(key)[:, lo:TOK], ACT.Silu).then_inc(*read(key))
                for c in range(6):
                    act.wait_ge(*when("conv", (l, c)))
                    fn(acc2[:, c, :], acc2[:, c, :], ACT.Silu).then_inc(*mark("conv_silu", (l, c)))
                for i in range(2):
                    key = ("rg", l, i)
                    act.wait_ge(*full(key))
                    fn(rgate[:, i, lo:TOK], bank(key)[:, lo:TOK], ACT.Silu).then_inc(*read(key))
                act.wait_ge(*when("rows_in", (1, 3)))
                act.wait_ge(*when("gate_args", l))
                r = 32 * l
                step(fn(lgt, rows[:, r:r + 8], ACT.Exp))
                step(fn(ealog, rows[:, r + 8:r + 16], ACT.Exp))
                step(fn(spe, spz, ACT.Abs))
                settle()
                step(fn(spe, spe, ACT.Exp, scale=-1.0))
                for d in range(2):
                    step(fn(beta[:, 16 * d:16 * d + 16].rearrange("p (t h) -> p t h", t=TT),
                            ab.rearrange("p (t c) -> p t c", t=TT)[:, :, 8 + 4 * d:12 + 4 * d], ACT.Exp, scale=-1.0))
                settle()
                fn(spl, spe, ACT.Ln, bias=table[:, CONST["ones"][0]:CONST["ones"][0] + 1])\
                    .then_inc(*mark("gate_exps", l))

            def window(l):
                units = [(h, t) for h in range(8) for t in range(0 if l == 0 else 2, TT)]

                def turned(i):
                    h, t = units[i]
                    key = ("pt", l, h, t)
                    nk = CTX if t < 2 else TOK
                    act.wait_ge(*full(key))
                    fn(pT[:, (i % 2) * 512:(i % 2) * 512 + nk], bank(key)[:, 0:nk], ACT.Copy).then_inc(*read(key))

                def out_tile(m):
                    lo = needed(l)
                    key = ("so", l, m)
                    act.wait_ge(*full(key))
                    fn(oT[:, 4 + m, lo:TOK], bank(key)[:, lo:TOK], ACT.Copy).then_inc(*read(key))

                nu = len(units)
                per = nu // 4
                for i in range(nu + 5):
                    if i < nu:
                        h, t = units[i]
                        key = ("sc", l, h, t)
                        nk = CTX if t < 2 else TOK
                        act.wait_ge(*when("scored", (l, i)))
                        if i >= 4:
                            act.wait_ge(*full(("pt", l) + units[i - 4]))
                        fn(prob(i, nk), bank(key)[:, 0:nk], ACT.Exp, scale=SCALE, bias=nmx[:, i % 4:i % 4 + 1],
                           accum_out=rsm[:, i % 4:i % 4 + 1]).then_inc(*read(key))
                        fn(es[:, i % 4:i % 4 + 1], rows[:, 32 * l + 24 + h:32 * l + 25 + h], ACT.Exp,
                           bias=nmx[:, i % 4:i % 4 + 1]).then_inc(*mark("exped", (l, i)))
                    if 0 <= i - 3 < nu:
                        turned(i - 3)
                    if i >= 5 and (i - 5) % per == per - 1:
                        out_tile((i - 5) // per)

            def retention(l):
                lo = needed(l)
                if l == 0:
                    act.wait_ge(*when("table_in", "all"))
                    ada_rows(0, 1)
                for h in range(4):
                    act.wait_ge(*when("decay_args", (l, h)))
                    m = dec(h)
                    step(fn(m[:, 512:1024], m[:, 512:1024], ACT.Exp))
                    step(fn(m[:, 0:512], const("diff"), ACT.Exp, scale=lgt[:, h:h + 1], bias=l256[:, h:h + 1]))
                    fn(tmpB[:, :], const("diff"), ACT.Exp, scale=ln1[:, h:h + 1], bias=l256[:, 4 + h:5 + h])\
                        .then_inc(*mark("decays_exp", (l, h)))
                    if h == 0:
                        act.wait_ge(*when("gate_sums", l))
                        step(fn(gex, gex, ACT.Exp))
                        fn(kdf, kdf, ACT.Exp).then_inc(*mark("gate_sums_exp", l))
                for i in range(2):
                    key = ("ro", l, i)
                    act.wait_ge(*full(key))
                    fn(oraw2[i][:, lo:TOK], bank(key)[:, lo:TOK], ACT.Copy).then_inc(*read(key))
                for i in range(2):
                    act.wait_ge(*drained(("rmean", l, i)))
                    fn(osq2[i][:, lo:TOK], oraw2[i][:, lo:TOK], ACT.Square).then_inc(*mark("head_square", ("r", l, i)))
                for i in range(2):
                    act.wait_ge(*full(("rvar", l, i)))
                    fn(odev2[i][:, lo:TOK], bank(("rvar", l, i))[:, lo:TOK], ACT.Sqrt, bias=eps)\
                        .then_inc(*read(("rvar", l, i)))

            def delta_prepare(l):
                for t in range(TT):
                    key = ("ct", l, t, 0)
                    act.wait_ge(*full(key))
                    if t >= 2:
                        act.wait_ge(*when("squares_summed", (l, t - 2)))
                    fn((tmpA, tmpB)[t % 2][:, :], bank(key)[:, :], ACT.Square).then_inc(*mark("qk_square", (l, t)))
                    fn(tok[:, t, 0:512], bank(key)[:, :], ACT.Copy).then_inc(*read(key))
                act.wait_ge(*when("squares_summed", (l, 3)))
                fn(ssq, ssq, ACT.Sqrt, bias=eps).then_inc(*mark("qk_root", l))
                for t in range(TT):
                    key = ("qkt", l, t)
                    act.wait_ge(*full(key))
                    fn(qkT[:, :, t * P:(t + 1) * P], bank(key)[:, :].rearrange("p (c n) -> p c n", c=4), ACT.Copy)\
                        .then_inc(*read(key))

            def delta(l, d):
                def copy_out(key, dst):
                    act.wait_ge(*full(key))
                    fn(dst, bank(key)[:, :], ACT.Copy).then_inc(*read(key))

                for t in range(TT):
                    copy_out(("kq", l, d, t), grp(gKQ, t))
                for t in range(TT):
                    act.wait_ge(*when("decay_masked", (l, d, t)))
                    fn(grp(gP1, t), grp(gP1, t), ACT.Exp).then_inc(*mark("decay_ready", (l, d, t)))
                for t in range(TT):
                    copy_out(("T0", l, d, t), grp(gT, t))
                for v in range(1, 6):
                    for t in range(TT):
                        copy_out(("P1", l, d, v, t), grp(gP1, t))
                for t in range(TT):
                    copy_out(("wu", l, d, t), grp(gWU, t))

            def delta_finish(l):
                lo = needed(l)
                for i in range(2):
                    act.wait_ge(*when("delta_out", l))
                    if i:
                        act.wait_ge(*full(("gvar", l, 0)))
                    fn(tmpB[:, lo:TOK], oT[:, 2 + i, lo:TOK], ACT.Square).then_inc(*mark("head_square", ("g", l, i)))
                    act.wait_ge(*full(("gvar", l, i)))
                    if i:
                        act.wait_ge(*when("delta_normed", (l, 0)))
                    fn(tmpA[:, lo:TOK], bank(("gvar", l, i))[:, lo:TOK], ACT.Sqrt, bias=eps).then_inc(*read(("gvar", l, i)))

            def ffn():
                for f in range(22):
                    act.wait_ge(*full(("fa", f)))
                    if f >= 2:
                        act.wait_ge(*drained(("fb", f - 2)))
                    fn((tmpA, tmpB)[f % 2][:, :], bank(("fa", f))[:, :], ACT.Silu).then_inc(*read(("fa", f)))

            def phase_leave():
                step(fn(one[:, 0:1], eps, ACT.Copy))
                settle()
                act.sem_inc(phase_done, 1)

            def phase_enter(k):
                act.wait_ge(phase_done, 4 * k)

            for l in range(2):
                norm(2 * l)
                project(l)
                window(l)
                retention(l)
                phase_leave()
                delta_prepare(l)
                phase_enter(2 * l + 1)
                if l == 0:
                    ada_rows(0, 2)
                delta(l, 0)
                if l == 0:
                    ada_rows(1, 0)
                delta(l, 1)
                if l == 0:
                    ada_rows(1, 1)
                delta_finish(l)
                if l == 0:
                    ada_rows(1, 2)
                phase_leave()
                phase_enter(2 * l + 2)
                norm(2 * l + 1, needed(l))
                if l == 0:
                    ffn()
            act.wait_ge(*when("route_max", 0))
            for t in range(2):
                step(fn(wexp[:, t, :], lgts[:, t, :], ACT.Exp, bias=nm1[:, t:t + 1]))
            settle()
            fn(one[:, 0:1], eps, ACT.Copy).then_inc(*mark("route_exp", 0))
            for t in range(2):
                for q in range(2):
                    key = ("row", t, q)
                    act.wait_ge(*full(key))
                    fn(hrow[:, t, q * 512:(q + 1) * 512], bank(key)[:, :], ACT.Copy).then_inc(*read(key))

            def rows_out(q):
                fn(hg[:, 4 * q:4 * q + 4, :], psum[GATHER_BANK[q]][:, :].rearrange("p (k n) -> p k n", k=4),
                   ACT.Copy).then_inc(moe_rows_ready, 1)

            def item(u):

                def turned(c):
                    act.wait_ge(moe_turned, u * EC + (c + 2))
                    act.wait_ge(moe_down_done, u * EC + (EC if c < 2 else EC + c - 1))
                    fn(mhT[:, (c % 2) * 512:(c % 2) * 512 + 512], psum[4][:, :], ACT.Copy).then_inc(moe_hidT_ready, 1)

                for c in range(EC):
                    act.wait_ge(moe_gate_done, u * EC + (EC + c + 1))
                    act.wait_ge(moe_hid_ready, u * EC + max(c, 1))
                    fn((tmpA, tmpB)[c % 2][:, :], psum[c % 2][:, :], ACT.Silu).then_inc(moe_silu_ready, 1)
                    if c == 0:
                        act.wait_ge(moe_spread, u + 1)
                        fn(spread, psum[3][:, 0:256], ACT.Copy).then_inc(moe_spread_ready, 1)
                    else:
                        turned(c - 1)
                for q in range(2):
                    act.wait_ge(moe_gathered, u * 2 + (q + 3))
                    rows_out(q)
                turned(EC - 1)

            act.sem_inc(moe_silu_ready, 1)
            act.sem_inc(moe_hidT_ready, 1)
            for q in range(2):
                act.wait_ge(moe_gathered, q + 1)
                rows_out(q)
            with act.Fori(0, EXPERTS) as e:
                item(e)
            act.wait_ge(ints_ready, 1)
            n_over = act.value_load(ints[0:1, 0:1], min_val=0, max_val=3)
            with act.Fori(0, ITEMS - EXPERTS) as o:
                with act.If(o < n_over):
                    item(o + EXPERTS)
            norm(4, CTX)
            for t in range(2):
                for q in range(2):
                    key = ("out", t, q)
                    act.wait_ge(*full(key))
                    fn(osb[:, t * D + q * 512:t * D + (q + 1) * 512], bank(key)[:, :], ACT.Copy)\
                        .then_inc(*read(key))
            for t in range(2):
                act.wait_ge(*drained(("out", t, 1)))
                act.sem_inc(*mark("out_row", t))

        @block.vector
        def _(dve):
            v = nc.vector
            step, settle = stepper(dve, "dve_step")

            def halves(lo):
                return ([(slice(0, CTX), 1)] if lo == 0 else []) + [(slice(CTX, TOK), 0)]

            v.memset(cond[:, :], 0.0).then_inc(*mark("cond_zero", 0))

            def vectors(l):
                dve.wait_ge(*full(("vec", l)))
                v.tensor_copy(VEC[l][:, 0:NVEC], bank(("vec", l))[:, 0:NVEC]).then_inc(*read(("vec", l)))
            vectors(0)
            for k in range(0, DT, 2):
                dve.wait_ge(*full(("x", k)))
                v.tensor_copy(xT[:, k, :], bank(("x", k))[:, :]).then_inc(*read(("x", k)))

            def ada(l, g):
                key = ("adaT", l, g)
                dve.wait_ge(*full(key))
                dve.wait_ge(*drained(("vec", l)))
                ms = slice(16 * g, 16 * g + 16)
                v.tensor_tensor(modv[l][:, ms, :].rearrange("p (j c) v -> p j c v", j=4),
                                bank(key)[:, 0:32].rearrange("p (c j v) -> p j c v", c=4, j=4),
                                VEC[l][:, ms].rearrange("p (j c) -> p j c", j=4).unsqueeze(3)
                                .broadcast_to([P, 4, 4, 2]), ALU.add).then_inc(*read(key))
                dve.wait_ge(*drained(key))
                if g != 1:
                    w = g // 2
                    m = modv[l][:, 24 * w + 8:24 * w + 16, :]
                    gain = VEC[l][:, V_N2 if w else V_N1:][:, 0:8].unsqueeze(2).broadcast_to([P, 8, 2])
                    v.scalar_tensor_tensor(out=m, in0=m, scalar=1.0, in1=gain, op0=ALU.add, op1=ALU.mult)\
                        .then_inc(*mark("scales", (l, w)))

            def add_squares(n, k, lo=0):
                dve.wait_ge(*when("square", (n, k)))
                if k > 1:
                    dve.wait_ge(*when("squares_added", (n, k - 1)))
                a = squares(n)[:, 0, lo:TOK]
                v.tensor_tensor(a, a, squares(n)[:, k, lo:TOK], ALU.add).then_inc(*mark("squares_added", (n, k)))

            def norm(n, lo=0):
                if n == 0:
                    for k in range(1, DT - 1):
                        add_squares(n, k)
                add_squares(n, DT - 1, lo)
                dve.wait_ge(*drained(("ss", n)))
                v.reciprocal(rstd[:, lo // P:TT], root[:, lo // P:TT]).then_inc(*mark("inverse_root", n))
                key = ("rstd", n)
                dve.wait_ge(*full(key))
                r = bank(key)[:, lo:TOK]
                for k in range(DT):
                    last = k == DT - 1
                    if n < 4:
                        ins = v.tensor_tensor(hT[:, k, lo:TOK], xT[:, k, lo:TOK], r, ALU.mult)
                        ins.then_inc(*mark("normed", (n, k)))
                    else:
                        ins = v.scalar_tensor_tensor(
                            out=hT[:, k, lo:TOK], in0=xT[:, k, lo:TOK], scalar=VEC[0][:, V_FIN + k:V_FIN + k + 1],
                            in1=r, op0=ALU.mult, op1=ALU.mult)
                        ins.then_inc(*mark("mod", (n, k)))
                dve.wait_ge(*when("mod" if n == 4 else "normed", (n, DT - 1)))
                dve.sem_inc(*read(key))
                if n == 0:
                    ada(0, 0)

            def rope(key, dst, name, mkey, lo=0):
                dve.wait_ge(*full(key))
                b = bank(key)
                if lo == 0:
                    step(v.tensor_copy(dst[:, 0:CTX], b[:, 0:CTX]))
                step(v.tensor_tensor(tmpA[:, 0:LAT], b[:, CTX:TOK], const("cos"), ALU.mult))
                for q in range(4):
                    o = slice(32 * q, 32 * q + 32)
                    i = slice(32 * (q ^ 1), 32 * (q ^ 1) + 32)
                    ins = v.tensor_tensor(tmpB[o, 0:LAT], b[i, CTX:TOK], const("sin")[o, :], ALU.mult)
                    if q < 3:
                        step(ins)
                ins.then_inc(*read(key))
                dve.wait_ge(*drained(key))
                v.tensor_tensor(dst[:, CTX:TOK], tmpA[:, 0:LAT], tmpB[:, 0:LAT], ALU.add).then_inc(*mark(name, mkey))
                dve.wait_ge(*when(name, mkey))

            def project(l):
                rope(("sk", l), krot, "sk_rot", l)
                for g in range(2):
                    for p in range(2):
                        ins = v.tensor_copy(skd[p * HD:(p + 1) * HD, g, :], krot[g * HD:(g + 1) * HD, :])
                        if (g, p) != (1, 1):
                            step(ins)
                ins.then_inc(*mark("sk_ready", l))
                for t in range(TT):
                    key = ("vab", l, t)
                    dve.wait_ge(*full(key))
                    step(v.tensor_copy(sv[:, t, :], bank(key)[:, 0:P]))
                    v.tensor_copy(ab[:, 16 * t:16 * t + 16], bank(key)[:, P:P + 16]).then_inc(*read(key))
                dve.wait_ge(*when("rows_in", (1, 3)))
                dve.wait_ge(*drained(("vab", l, 3)))
                for d in range(2):
                    ins = (v.tensor_tensor(
                        spz[:, 16 * d:16 * d + 16].rearrange("p (t h) -> p t h", t=TT),
                        ab.rearrange("p (t c) -> p t c", t=TT)[:, :, 4 * d:4 * d + 4],
                        rows[:, 32 * l + 16 + 4 * d:32 * l + 20 + 4 * d].unsqueeze(1).broadcast_to([P, TT, 4]), ALU.add))
                    ins.then_inc(*mark("gate_args", l if d else (l, 0)))
                for c in range(4):
                    rope(("sq", l, c), sq[:, c, :], "sq_ready", (l, c), needed(l))
                for c in range(4):
                    rope(("rqk", l, c), rqk[:, c, :], "rqk_ready", (l, c), needed(l) if c < 2 else 0)
                for t in range(TT):
                    key = ("rv", l, t)
                    dve.wait_ge(*full(key))
                    v.tensor_copy(rv[:, t, :], bank(key)[:, 0:256]).then_inc(*read(key))
                dve.wait_ge(*when("gate_exps", l))
                step(v.scalar_tensor_tensor(out=gl, in0=spz, scalar=0.0, in1=spl, op0=ALU.max, op1=ALU.add))
                step(v.tensor_scalar(beta, beta, 1.0, None, ALU.add))
                step(v.tensor_scalar(lgt, lgt, -1.0, None, ALU.mult))
                settle()
                step(v.reciprocal(beta, beta))
                step(v.tensor_tensor(lsum, lgt[:, 0:4], lgt[:, 4:8], ALU.add))
                step(v.tensor_scalar(l256, lgt, 256.0, None, ALU.mult))
                step(v.tensor_scalar(ln1, lgt[:, 4:8], -1.0, None, ALU.mult))
                for d in range(2):
                    g = gl[:, 16 * d:16 * d + 16].rearrange("p (t h) -> p t h", t=TT)
                    ins = v.scalar_tensor_tensor(
                        out=g, in0=g, scalar=-1.0, in1=ealog[:, 4 * d:4 * d + 4].unsqueeze(1).broadcast_to([P, TT, 4]),
                        op0=ALU.mult, op1=ALU.mult)
                    ins.then_inc(*mark("log_decay", l if d else (l, 0)))
                settle()

            def window(l):
                units = [(h, t) for h in range(8) for t in range(0 if l == 0 else 2, TT)]

                def score(i):
                    h, t = units[i]
                    key = ("sc", l, h, t)
                    nk = CTX if t < 2 else TOK
                    c = slice(i % 4, i % 4 + 1)
                    b = bank(key)
                    dve.wait_ge(*full(key))
                    if t >= 2:
                        step(v.tensor_tensor(b[:, CTX:TOK], b[:, CTX:TOK],
                                             const("band")[:, (t - 2) * 256:(t - 1) * 256], ALU.add))
                        settle()
                    step(v.reduce_max(mx[:, c], b[:, 0:nk], AX_X))
                    settle()
                    v.tensor_scalar(nmx[:, c], mx[:, c], sink8[:, h:h + 1], -SCALE, ALU.max, ALU.mult)\
                        .then_inc(*mark("scored", (l, i)))

                def normalize(i):
                    c = slice(i % 4, i % 4 + 1)
                    dve.wait_ge(*when("exped", (l, i)))
                    if i >= 4:
                        dve.wait_ge(*when("probs", (l,) + units[i - 4]))
                    step(v.tensor_tensor(den[:, c], rsm[:, c], es[:, c], ALU.add))
                    settle()
                    v.reciprocal(den[:, c], den[:, c]).then_inc(*mark("divisor", (l, i)))

                step(v.tensor_scalar(sink8, rows[:, 32 * l + 24:32 * l + 32], 1.0 / SCALE, None, ALU.mult))
                settle()
                for i in range(len(units) + 1):
                    if i < len(units):
                        score(i)
                    if i:
                        normalize(i - 1)

            def retention(l):
                def args(h):
                    m = dec(h)
                    step(v.tensor_scalar(tmpA[:, :], const("diff"), lsum[:, h:h + 1], 0.0, ALU.mult, ALU.min))
                    settle()
                    v.scalar_tensor_tensor(out=m[:, 512:1024], in0=const("diff"), scalar=ln1[:, h:h + 1],
                                           in1=tmpA[:, :], op0=ALU.mult, op1=ALU.add)\
                        .then_inc(*mark("decay_args", (l, h)))
                args(0)
                key = ("gsum", l)
                dve.wait_ge(*full(key))
                v.tensor_copy(gex, bank(key)[:, 0:128]).then_inc(*read(key))
                dve.wait_ge(*drained(key))
                step(v.tensor_copy(gcs, gex[:, 0:32]))
                v.tensor_tensor(kdf, gex[:, 32:64], gex[:, 0:32], ALU.subtract).then_inc(*mark("gate_sums", l))
                for h in range(4):
                    m = dec(h)
                    dve.wait_ge(*when("decays_exp", (l, h)))
                    step(v.tensor_tensor(m[:, 512:1024], m[:, 512:1024], const("diag2"), ALU.mult))
                    step(v.tensor_tensor(m[:, 0:512], m[:, 0:512], tmpB[:, :], ALU.add))
                    settle()
                    if h < 3:
                        args(h + 1)
                    if h == 2:
                        dve.wait_ge(*when("ret_values", (l, 0)))
                    if h == 3:
                        dve.wait_ge(*full(("ro", l, 0)))
                    for part in range(2 if l else 3):
                        key = ("rs", l, h, part)
                        dve.wait_ge(*full(key))
                        v.scalar_tensor_tensor(out=smk(h, part), in0=bank(key)[:, :], scalar=SCALE,
                                               in1=m[:, 0:512] if part == 0 else m[:, 512:1024],
                                               op0=ALU.mult, op1=ALU.mult).then_inc(*read(key))
                    dve.wait_ge(*drained(("rs", l, h, 1 if l else 2)))
                    if (l, h) == (0, 0):
                        ada(0, 1)
                    if h == 0:
                        dve.wait_ge(*when("gate_sums_exp", l))
                        step(v.tensor_tensor(bgf, beta, gex[:, 0:32], ALU.mult))
                        for p in range(2):
                            for c in range(2):
                                hp = slice(p * HD, (p + 1) * HD)
                                step(v.tensor_copy(
                                    sdec.rearrange("p (g c i) -> p g c i", c=2, i=2)[hp, :, c, :],
                                    gex[:, 64 + 32 * c:96 + 32 * c].rearrange("p (g i q) -> p g i q", i=2, q=2)[hp, :, :, p]))
                        settle()
                        v.tensor_copy(mx[:, 1:2], gcs[:, 0:1]).then_inc(*mark("decays", l))
                cols = slice(needed(l), TOK)
                for i in range(2):
                    dve.wait_ge(*drained(("ro", l, i)))
                    dve.wait_ge(*full(("rmean", l, i)))
                    v.tensor_tensor(oraw2[i][:, cols], oraw2[i][:, cols], bank(("rmean", l, i))[:, cols],
                                    ALU.subtract).then_inc(*read(("rmean", l, i)))
                for i in range(2):
                    dve.wait_ge(*drained(("rvar", l, i)))
                    step(v.reciprocal(odev2[i][:, cols], odev2[i][:, cols]))
                    settle()
                    step(v.scalar_tensor_tensor(
                        out=oraw2[i][:, cols], in0=oraw2[i][:, cols], scalar=VEC[l][:, V_RETG + i:V_RETG + i + 1],
                        in1=odev2[i][:, cols], op0=ALU.mult, op1=ALU.mult))
                    settle()
                    dve.wait_ge(*drained(("rg", l, i)))
                    v.tensor_tensor(oT[:, i, cols], oraw2[i][:, cols], rgate[:, i, cols], ALU.mult)\
                        .then_inc(*mark("ret_out", (l, i)))

            def delta_prepare(l):
                for t in range(TT):
                    key = ("ct", l, t, 1)
                    dve.wait_ge(*full(key))
                    v.tensor_copy(tok[:, t, 512:768], bank(key)[:, 0:256]).then_inc(*read(key))
                    dve.wait_ge(*when("qk_square", (l, t)))
                    v.reduce_sum(ssq[:, 8 * t:8 * t + 8],
                                 (tmpA, tmpB)[t % 2][:, :].rearrange("p (h n) -> p h n", n=HD), AX_X)\
                        .then_inc(*mark("squares_summed", (l, t)))
                dve.wait_ge(*when("qk_root", l))
                step(v.reciprocal(ssq, ssq))
                settle()
                qs = ssq.rearrange("p (t h) -> p t h", t=TT)[:, :, 0:4]
                step(v.tensor_scalar(qs, qs, SCALE, None, ALU.mult))
                settle()
                for t in range(TT):
                    dve.wait_ge(*drained(("ct", l, t, 0)))
                    x = tok[:, t, 0:512].rearrange("p (h n) -> p h n", n=HD)
                    v.tensor_tensor(x, x, ssq[:, 8 * t:8 * t + 8].unsqueeze(2).broadcast_to([P, 8, HD]), ALU.mult)\
                        .then_inc(*mark("qk_unit", (l, t)))
            def delta(l, d):
                for t in range(TT):
                    key = ("dec", l, d, t)
                    at = 16 * d + 4 * t
                    dve.wait_ge(*full(key))
                    v.tensor_tensor(grp(gP1, t).rearrange("p (h n) -> p h n", h=4),
                                    bank(key)[:, :].rearrange("p (h n) -> p h n", h=4),
                                    gcs[:, at:at + 4].unsqueeze(2).broadcast_to([P, 4, P]), ALU.subtract)\
                        .then_inc(*read(key))
                for t in range(TT):
                    dve.wait_ge(*when("decay_ready", (l, d, t)))
                    for p in range(2):
                        key = ("kkqk", l, d, t, p)
                        dve.wait_ge(*full(key))
                        for j, dst in enumerate((gAT,) if l and t < 2 else (gAT, gAtt)):
                            def heads(x):
                                return grp(x, t).rearrange("p (i q n) -> p i q n", i=2, q=2)[:, :, p, :]
                            ins = v.tensor_tensor(heads(dst), bank(key)[:, j * 256:(j + 1) * 256].rearrange(
                                "p (i n) -> p i n", i=2), heads(gP1), ALU.mult)
                            if j == 0 and not (l and t < 2):
                                step(ins)
                        ins.then_inc(*read(key))
                for t in range(TT):
                    dve.wait_ge(*when("NT", (l, d, 0, t)))
                    v.tensor_tensor(grp(gTT, t).rearrange("p (h n) -> p h n", h=4),
                                    ident.unsqueeze(1).broadcast_to([P, 4, P]),
                                    grp(gNT, t).rearrange("p (h n) -> p h n", h=4), ALU.subtract)\
                        .then_inc(*mark("TT_first", (l, d, t)))
                for lv in range(1, 6):
                    for t in range(TT):
                        for name, dst in (("TP", gT), ("TTP", gTT)):
                            if name == "TP" and lv == 5:
                                continue
                            key = (name, l, d, lv, t)
                            dve.wait_ge(*full(key))
                            if lv == 1:
                                dve.wait_ge(*(drained(("T0", l, d, t)) if name == "TP" else when("TT_first", (l, d, t))))
                            else:
                                dve.wait_ge(*drained((name, l, d, lv - 1, t)))
                            v.tensor_tensor(grp(dst, t), grp(dst, t), bank(key)[:, :], ALU.subtract)\
                                .then_inc(*read(key))
                if d:
                    dve.wait_ge(*drained(("su", l, 0, 7)))
                step(v.memset(vnew, 0.0))
                v.memset(state[:, :, :], 0.0).then_inc(*mark("state_zero", (l, d)))
                for n, (t, c) in enumerate(steps(d)):
                    cs = slice(c * CHUNK, (c + 1) * CHUNK)
                    dve.wait_ge(*full(("vn", l, d, n)))
                    v.tensor_tensor(vnew[cs, :], grp(gWU, t)[cs, 256:512], bank(("vn", l, d, n))[cs, 0:256],
                                    ALU.subtract).then_inc(*read(("vn", l, d, n)))
                    key = ("su", l, d, n)
                    dve.wait_ge(*full(key))
                    dve.wait_ge(*(drained(("su", l, d, n - 1)) if n else when("state_zero", (l, d))))
                    for i in range(2):
                        at = ((d * 4 + t) * 2 + c) * 2 + i
                        for p in range(2):
                            hp = slice(p * HD, (p + 1) * HD)
                            x = state[hp, i, p * HD:(p + 1) * HD]
                            ins = v.scalar_tensor_tensor(out=x, in0=x, scalar=sdec[hp, at:at + 1],
                                                         in1=bank(key)[hp, i * HD:(i + 1) * HD],
                                                         op0=ALU.mult, op1=ALU.add)
                            if (i, p) != (1, 1):
                                step(ins)
                    ins.then_inc(*read(key))
                    if (l, d, n) == (0, 1, 4):
                        ada(1, 1)
                    if n % 2 and (l == 0 or t >= 2):
                        for i in range(2):
                            key = ("go", l, d, t, i)
                            dve.wait_ge(*full(key))
                            o = oT[:, 2 + i, t * P:(t + 1) * P]
                            b = bank(key)[:, 0:P]
                            if d == 0:
                                v.tensor_copy(o, b).then_inc(*read(key))
                            else:
                                dve.wait_ge(*drained(("go", l, 0, t, i)))
                                v.tensor_tensor(o, o, b, ALU.add).then_inc(*read(key))
                    if l and n % 2:
                        residual(l, ("woe", l, 4 * d + n // 2), 4 * d + n // 2, 16, CTX)
                settle()

            def delta_finish(l):
                lo = needed(l)
                for t in range(2 if l else 0, TT):
                    for i in range(2):
                        dve.wait_ge(*drained(("go", l, 1, t, i)))
                v.tensor_copy(mx[:, 2:3], gcs[:, 0:1]).then_inc(*mark("delta_out", l))
                for i in range(2):
                    o = oT[:, 2 + i, lo:TOK]
                    dve.wait_ge(*drained(("gvar", l, i)))
                    step(v.reciprocal(tmpA[:, lo:TOK], tmpA[:, lo:TOK]))
                    settle()
                    v.scalar_tensor_tensor(out=o, in0=o, scalar=VEC[l][:, V_GDNG:V_GDNG + 1], in1=tmpA[:, lo:TOK],
                                           op0=ALU.mult, op1=ALU.mult).then_inc(*mark("delta_normed", (l, i)))
                    dve.wait_ge(*when("delta_normed", (l, i)))
                    dve.wait_ge(*drained(("z", l, i)))
                    v.tensor_tensor(o, o, zgate[:, i, lo:TOK], ALU.mult).then_inc(*mark("mixed", l if i else (l, 0)))

            def residual(l, key, k, gate, lo):
                dve.wait_ge(*full(key))
                for cols, s in halves(lo):
                    ins = v.scalar_tensor_tensor(out=xT[:, k, cols], in0=bank(key)[:, cols],
                                                 scalar=modv[l][:, gate + k, s:s + 1], in1=xT[:, k, cols],
                                                 op0=ALU.mult, op1=ALU.add)
                    if s:
                        step(ins)
                ins.then_inc(*read(key))

            def ffn():
                for half, (f0, f1) in enumerate(FF_PARTS):
                    for f in range(f0, f1):
                        dve.wait_ge(*full(("fb", f)))
                        dve.wait_ge(*drained(("fa", f)))
                        v.tensor_tensor(hidT(f - f0), (tmpA, tmpB)[f % 2][:, :], bank(("fb", f))[:, :], ALU.mult)\
                            .then_inc(*read(("fb", f)))
                    for k in range(DT):
                        if half:
                            dve.wait_ge(*drained(("fy", 0, k)))
                        residual(0, ("fy", half, k), k, 40, 0)
                        if half and k >= 2:
                            add_squares(2, k - 1)

            def phase_leave():
                step(v.tensor_copy(mx[:, 0:1], gcs[:, 0:1]))
                settle()
                dve.sem_inc(phase_done, 1)

            def phase_enter(k):
                dve.wait_ge(phase_done, 4 * k)

            for l in range(2):
                norm(2 * l)
                if l == 0:
                    dve.wait_ge(*when("table_in", "all"))
                    vectors(1)
                project(l)
                window(l)
                retention(l)
                phase_leave()
                delta_prepare(l)
                phase_enter(2 * l + 1)
                if l == 0:
                    ada(0, 2)
                delta(l, 0)
                if l == 0:
                    ada(1, 0)
                delta(l, 1)
                delta_finish(l)
                if l == 0:
                    ada(1, 2)
                phase_leave()
                phase_enter(2 * l + 2)
                for k in range(DT):
                    if l:
                        dve.wait_ge(*drained(("woe", l, k)))
                    residual(l, ("wo", l, k), k, 16, needed(l))
                    if k >= 2:
                        add_squares(2 * l + 1, k - 1, needed(l))
                norm(2 * l + 1, needed(l))
                if l == 0:
                    ffn()

            key = "logits"
            dve.wait_ge(*full(key))
            v.tensor_copy(lgts, bank(key)[:, 0:16].rearrange("p (t e) -> p t e", t=2)).then_inc(*read(key))
            dve.wait_ge(*drained(key))
            ex = const("expert")
            step(v.tensor_tensor(less, ex.unsqueeze(1).broadcast_to([P, 8, 8]),
                                 ex.unsqueeze(2).broadcast_to([P, 8, 8]), ALU.is_lt))
            step(v.reduce_max(nm1, lgts, AX_X))
            settle()
            v.tensor_scalar(nm1, nm1, -1.0, None, ALU.mult).then_inc(*mark("route_max", 0))
            for t in range(2):
                a = lgts[:, t, :].unsqueeze(1).broadcast_to([P, 8, 8])
                b = lgts[:, t, :].unsqueeze(2).broadcast_to([P, 8, 8])
                step(v.tensor_tensor(cmp1, a, b, ALU.is_gt))
                step(v.tensor_tensor(cmp2, a, b, ALU.is_equal))
                settle()
                step(v.tensor_tensor(cmp2, cmp2, less, ALU.mult))
                settle()
                step(v.tensor_tensor(cmp1, cmp1, cmp2, ALU.add))
                settle()
                step(v.reduce_sum(rank, cmp1, AX_X))
                settle()
                ins = v.tensor_scalar(sel[:, t, :], rank, 2.0, None, ALU.is_lt)
                ins.then_inc(*mark("chosen", 0 if t else ("first", 0)))
            dve.wait_ge(*when("chosen", 0))
            dve.wait_ge(*when("route_exp", 0))
            step(v.tensor_tensor(wexp, wexp, sel, ALU.mult))
            settle()
            step(v.reduce_sum(wsum, wexp, AX_X))
            settle()
            step(v.reciprocal(wsum, wsum))
            settle()
            step(v.tensor_tensor(wexp, wexp, wsum.unsqueeze(2).broadcast_to([P, 2, 8]), ALU.mult))
            key = "places"
            dve.wait_ge(*full(key))
            v.tensor_copy(place, bank(key)[:, 0:24]).then_inc(*read(key))
            dve.wait_ge(*drained(key))
            settle()
            pos = place[:, 0:16].rearrange("p (t e) -> p t e", t=2)
            step(v.memset(items[:, :, :, :], 0.0))
            step(v.memset(yacc[:, :, :], 0.0))
            settle()
            for i, src in enumerate((pos, sel, wexp)):
                step(v.tensor_copy(items[:, i, 0:8, :], src.rearrange("p t e -> p e t")))
            settle()

            for i, dst in ((1, pick), (2, wpick)):
                for t in range(2):
                    v.tensor_scalar(dst[:, t * P:(t + 1) * P], const("iota"), itemf[:, t:t + 1],
                                    itemf[:, 24 * i + t:24 * i + t + 1], ALU.is_equal, ALU.mult)\
                        .then_inc(moe_picks, 1)
            dve.wait_ge(moe_picks, 4)
            dve.sem_inc(moe_sel_ready, 1)
            step(v.memset(yrow, 0.0))
            step(v.memset(spread, 0.0))
            settle()
            for counted in (moe_hid_ready, moe_y_ready, moe_added, moe_spread_ready):
                dve.sem_inc(counted, 1)

            step(v.tensor_scalar(over, place[:, 16:24], float(P), None, ALU.is_gt))
            settle()
            step(v.tensor_tensor(cmp1, less, over.unsqueeze(1).broadcast_to([P, 8, 8]), ALU.mult))
            step(v.reduce_sum(intf[:, 0:1], over, AX_X))
            settle()
            step(v.reduce_sum(rank, cmp1, AX_X))
            settle()
            for o in range(3):
                step(v.scalar_tensor_tensor(out=cmp2[:, 0, :], in0=rank, scalar=float(o), in1=over,
                                            op0=ALU.is_equal, op1=ALU.mult))
                settle()
                step(v.tensor_tensor(cmp2[:, 1, :], cmp2[:, 0, :], ex, ALU.mult))
                for i, src in enumerate((pos, sel, wexp)):
                    step(v.tensor_tensor(cmp1[:, 2 * i:2 * i + 2, :], src,
                                         cmp2[:, 0, :].unsqueeze(1).broadcast_to([P, 2, 8]), ALU.mult))
                settle()
                step(v.reduce_sum(intf[:, 1 + o:2 + o], cmp2[:, 1, :], AX_X))
                for i in range(3):
                    step(v.reduce_sum(items[:, i, 8 + o, :], cmp1[:, 2 * i:2 * i + 2, :], AX_X))
                settle()
                step(v.tensor_scalar(items[:, 0, 8 + o, :], items[:, 0, 8 + o, :], float(P), None, ALU.subtract))
                settle()
            v.tensor_copy(ints[:, 0:4], intf).then_inc(ints_ready, 1)


            def add_rows(u):
                for j in range(4):
                    dve.wait_ge(moe_scattered, u * 4 + (j + 1))
                    if j == 0:
                        dve.wait_ge(moe_added, u * 4 + 1)
                    y = yacc[:, 2 * j:2 * j + 2, :]
                    v.tensor_tensor(y, y, psum[4 + j % 2][:, :].rearrange("p (k n) -> p k n", k=2), ALU.add)\
                        .then_inc(moe_added, 1)

            def item(u):
                for c in range(EC):
                    dve.wait_ge(moe_up_done, u * EC + (EC + c + 1))
                    dve.wait_ge(moe_silu_ready, u * EC + (c + 2))
                    dve.wait_ge(moe_turned, u * EC + max(c, 1))
                    v.tensor_tensor(hid[:, (c % 2) * 512:(c % 2) * 512 + 512], (tmpA, tmpB)[c % 2][:, :],
                                    psum[2 + c % 2][:, :], ALU.mult).then_inc(moe_hid_ready, 1)
                    if c == 0:
                        add_rows(u)
                    if c == 2:
                        dve.wait_ge(moe_spread, u + 1)
                        for i, dst in ((1, pick), (2, wpick)):
                            for t in range(2):
                                v.tensor_scalar(dst[:, t * P:(t + 1) * P], const("iota"),
                                                itemf[:, bass.ds(u * 2 + (t + 2), 1)],
                                                itemf[:, bass.ds(u * 2 + (t + 2 + 24 * i), 1)],
                                                ALU.is_equal, ALU.mult).then_inc(moe_picks, 1)
                        dve.wait_ge(moe_picks, u * 4 + 8)
                        dve.sem_inc(moe_sel_ready, 1)
                dve.wait_ge(moe_down_done, u * EC + 2 * EC)
                v.tensor_copy(yrow[:, 0:512], psum[6][:, :]).then_inc(moe_y_half, 1)
                dve.wait_ge(moe_y_half, u + 1)
                v.tensor_copy(yrow[:, 512:1024], psum[7][:, :]).then_inc(moe_y_ready, 1)

            with dve.Fori(0, EXPERTS) as e:
                item(e)
            n_over = dve.value_load(ints[0:1, 0:1], min_val=0, max_val=3)
            with dve.Fori(0, ITEMS - EXPERTS) as o:
                with dve.If(o < n_over):
                    item(o + EXPERTS)
            add_rows(n_over + EXPERTS)
            settle()
            step(v.memset(wsum, 0.0))
            settle()
            for k in range(DT):
                v.scalar_tensor_tensor(out=xT[:, k, CTX:TOK], in0=yacc[:, k, :], scalar=modv[1][:, 40 + k, 0:1],
                                       in1=xT[:, k, CTX:TOK], op0=ALU.mult, op1=ALU.add)\
                    .then_inc(*mark("final_residual", k))
                if k >= 2:
                    add_squares(4, k - 1, CTX)
            norm(4, CTX)

        @block.gpsimd
        def _(pool):
            g = nc.gpsimd
            step, settle = stepper(pool, "pool_step")

            def conv(l):
                pool.wait_ge(*(drained(("fy", 1, DT - 1)) if l else full(("ss", 0))))
                if l:
                    step(g.memset(cin[:, 0:2, 0, :], 0.0))
                    settle()
                step(g.memset(cin[:, :, :, 0:2], 0.0))
                g.memset(cin[:, :, :, 258:260], 0.0).then_inc(*mark("pads", l))
                pool.wait_ge(*drained(("vec", l)))
                pool.wait_ge(*when("pads", l))
                for c in range(6):
                    pool.wait_ge(*drained(("gc", l, c)))
                    for k in range(5):
                        w = VEC[l][:, V_CONV + 6 * k + c:V_CONV + 6 * k + c + 1]
                        x = cin[:, c, :, k:k + 256]
                        tap = taps[:, (k % 2) * 512:(k % 2) * 512 + 512].rearrange("p (s n) -> p s n", s=2)
                        if k == 0:
                            step(g.tensor_scalar(acc[:, c], x, w, None, ALU.mult))
                            continue
                        step(g.tensor_scalar(tap, x, w, None, ALU.mult))
                        settle()
                        ins = g.tensor_tensor(acc[:, c], acc[:, c], tap, ALU.add)
                        if k < 4:
                            step(ins)
                    ins.then_inc(*mark("conv", (l, c)))

            def window(l):
                for i, (h, t) in enumerate([(h, t) for h in range(8) for t in range(0 if l == 0 else 2, TT)]):
                    x = prob(i, CTX if t < 2 else TOK)
                    pool.wait_ge(*when("divisor", (l, i)))
                    g.tensor_scalar(x, x, den[:, i % 4:i % 4 + 1], None, ALU.mult).then_inc(*mark("probs", (l, h, t)))

            def phase_leave():
                step(g.memset(poolone[:, :], 0.0))
                settle()
                pool.sem_inc(phase_done, 1)

            def phase_enter(k):
                pool.wait_ge(phase_done, 4 * k)

            def scaled(dst, src, f, at):
                return g.tensor_tensor(dst.rearrange("p (h n) -> p h n", h=4), src.rearrange("p (h n) -> p h n", h=4),
                                       f[:, at:at + 4].unsqueeze(2).broadcast_to([P, 4, HD]), ALU.mult)

            def delta(l, d):
                if d == 0:
                    pool.wait_ge(*when("decays", l))
                    for t in range(TT):
                        pool.wait_ge(*when("qk_unit", (l, t)))
                        pool.wait_ge(*drained(("ct", l, t, 1)))
                for t in range(TT):
                    at = 16 * d + 4 * t
                    if t >= 2:
                        pool.wait_ge(*full(("kq", l, d, t - 2)))
                    elif d:
                        pool.wait_ge(*full(("kq", l, 0, t + 2)))
                    q, k = tok[:, t, 0:256], tok[:, t, 256:512]
                    step(scaled(kbuf(t)[:, 0:256], k, beta, at))
                    scaled(kbuf(t)[:, 256:512], q, gex, at).then_inc(*mark("kbqd", (l, d, t)))
                if d:
                    pool.wait_ge(*full(("su", l, 0, 7)))
                for t in range(TT):
                    pool.wait_ge(*drained(("dec", l, d, t)))
                    x = grp(gP1, t).rearrange("p (h n) -> p h n", h=4)
                    g.tensor_tensor(x, x, const(f"neg{d}").unsqueeze(1).broadcast_to([P, 4, P]), ALU.add)\
                        .then_inc(*mark("decay_masked", (l, d, t)))
                for t in range(TT):
                    scaled(grp(gKD, t, 256), tok[:, t, 256:512], kdf, 16 * d + 4 * t)\
                        .then_inc(*mark("kd", (l, d, t)))
                for lv in range(6):
                    for t in range(TT if lv == 3 else 0):
                        at = 16 * d + 4 * t
                        if d:
                            pool.wait_ge(*full(("wu", l, 0, t)))
                        step(scaled(grp(gRW, t, 256), tok[:, t, 256:512], bgf, at))
                        scaled(grp(gRU, t, 256), tok[:, t, 512:768], beta, at).then_inc(*mark("rhs", (l, d, t)))
                    for t in range(TT):
                        if lv == 0:
                            for p in range(2):
                                pool.wait_ge(*drained(("kkqk", l, d, t, p)))
                        elif lv == 1:
                            pool.wait_ge(*when("TT_first", (l, d, t)))
                        else:
                            pool.wait_ge(*full(("P1", l, d, lv - 1, t)))
                        g.tensor_tensor(grp(gNT, t).rearrange("p (h n) -> p h n", h=4),
                                        grp(gAT, t).rearrange("p (h n) -> p h n", h=4),
                                        const(f"level{d}", lv).unsqueeze(1).broadcast_to([P, 4, P]), ALU.mult)\
                            .then_inc(*mark("NT", (l, d, lv, t)))

            pool.wait_ge(*when("table_in", "all"))
            for l in range(2):
                conv(l)
                window(l)
                phase_leave()
                phase_enter(2 * l + 1)
                delta(l, 0)
                delta(l, 1)
                phase_leave()
                phase_enter(2 * l + 2)
        assert len(was_read) == sum(uses)
        return L


_INS = ['x', 'c', 'ctx', 'c_ctx', 'ada_w', 'ada_b', 'norm1_g', 'w_in', 'ret_decay', 'ret_gn_g', 'gdn_conv_w',
        'gdn_a_log', 'gdn_dt_bias', 'gdn_norm_g', 'swa_sink', 'w_out', 'norm2_g', 'ffn_w1', 'ffn_w3', 'ffn_w2',
        'router_w', 'moe_w1', 'moe_w3', 'moe_w2', 'final_g']


def kernel(**inputs):
    import numpy as _np
    import concourse.bacc as _bacc
    from concourse import mybir as _mybir
    from concourse.bass_utils import run_bass_kernel_spmd as _run

    arrays = {f"in_{n}_dram": _np.ascontiguousarray(inputs[n]) for n in _INS}
    arrays["const_table"] = const_table()
    known = None
    for _ in range(2):
        nc = _bacc.Bacc("TRN2", target_bir_lowering=False, num_devices=1)
        A = {n: nc.dram_tensor(f"in_{n}_dram", inputs[n].shape, _mybir.dt.float32, kind="ExternalInput").ap()
             for n in _INS}
        table = nc.dram_tensor("const_table", (P, NCONST), _mybir.dt.float32, kind="ExternalInput").ap()
        out = nc.dram_tensor("out_0_dram", (1, LAT, D), _mybir.dt.float32, kind="ExternalOutput").ap()
        known = build(nc, A, out, table, known)
    r = _run(nc, [arrays], core_ids=[0])
    return r.results[0]["out_0_dram"]
```
